# Optimizing a Trainium2 kernel written in Bass

```python
import math
import jax, jax.numpy as jnp
from jax import lax
import numpy as np

D_MODEL = 1024
BATCH = 1
SEQ = 512
DEPTH = 1

CONV_WIDTH = D_MODEL // 2
CONV_KERNEL = 31
N_HEADS = 8
HEAD_DIM = 64
ATT_WIDTH = N_HEADS * HEAD_DIM
N_BRANCH = 2
D_FF = -(-8 * D_MODEL // (3 * 256)) * 256
IN_COLS = 2 * CONV_WIDTH + 3 * ATT_WIDTH + N_BRANCH * D_MODEL
Q_BLOCK = 128
EPS = 1e-6


def rmsnorm(x, g):
    xf = x.astype(jnp.float32)
    y = xf * lax.rsqrt(jnp.mean(xf * xf, axis=-1, keepdims=True) + EPS)
    return (y * g.astype(jnp.float32)).astype(x.dtype)

def layernorm(x, g, b):
    xf = x.astype(jnp.float32)
    mu = jnp.mean(xf, axis=-1, keepdims=True)
    xc = xf - mu
    y = xc * lax.rsqrt(jnp.mean(xc * xc, axis=-1, keepdims=True) + EPS)
    return (y * g.astype(jnp.float32) + b.astype(jnp.float32)).astype(x.dtype)

def causal_depthwise_conv(u, w, b):
    ch = u.shape[-1]
    y = lax.conv_general_dilated(
        u, w[:, None, :].astype(u.dtype), window_strides=(1,), padding=[(CONV_KERNEL - 1, 0)],
        dimension_numbers=("NWC", "WIO", "NWC"), feature_group_count=ch)
    return y + b

def stick_breaking_attention(q, k, v):
    s_len = q.shape[1]
    scale = 1.0 / math.sqrt(q.shape[-1])
    qf = q.astype(jnp.float32) * scale
    kf = k.astype(jnp.float32)
    vf = v.astype(jnp.float32)
    outs = []
    for start in range(0, s_len, Q_BLOCK):
        end = start + Q_BLOCK
        z = jnp.einsum("bqhd,bkhd->bhqk", qf[:, start:end], kf[:, :end])
        t_idx = start + jnp.arange(Q_BLOCK)[:, None]
        s_idx = jnp.arange(end)[None, :]
        causal = s_idx < t_idx
        log_keep = jnp.where(causal, jax.nn.log_sigmoid(-z), 0.0)
        log_after = lax.cumsum(log_keep, axis=3, reverse=True) - log_keep
        a = jnp.where(causal, jnp.exp(jax.nn.log_sigmoid(z) + log_after), 0.0)
        outs.append(jnp.einsum("bhqk,bkhd->bqhd", a, vf[:, :end]))
    return jnp.concatenate(outs, axis=1).astype(q.dtype)

def hybrid_mixer(h, w_in, conv_w, conv_b, conv_ln_g, conv_ln_b, w_conv_out, w_att_out, w_o):
    b, s, _ = h.shape
    proj = h @ w_in
    glu_in, qkv, gates = jnp.split(proj, [2 * CONV_WIDTH, 2 * CONV_WIDTH + 3 * ATT_WIDTH], axis=-1)
    u_val, u_gate = jnp.split(glu_in, 2, axis=-1)
    u = u_val * jax.nn.sigmoid(u_gate)
    u = causal_depthwise_conv(u, conv_w, conv_b)
    u = jax.nn.silu(layernorm(u, conv_ln_g, conv_ln_b))
    y_conv = u @ w_conv_out
    qkv = qkv.reshape(b, s, 3, N_HEADS, HEAD_DIM)
    o = stick_breaking_attention(qkv[:, :, 0], qkv[:, :, 1], qkv[:, :, 2])
    y_att = o.reshape(b, s, ATT_WIDTH) @ w_att_out
    g_conv, g_att = jnp.split(gates, 2, axis=-1)
    merged = jax.nn.sigmoid(g_conv) * y_conv + jax.nn.sigmoid(g_att) * y_att
    return merged @ w_o

def swiglu_ffn(h, w_ffn_in, w_ffn_out):
    gate, up = jnp.split(h @ w_ffn_in, 2, axis=-1)
    return (jax.nn.silu(gate) * up) @ w_ffn_out

def _normal(k, shape, scale):
    return jax.random.normal(k, shape, jnp.float32) * scale

def first_inputs(seed: int = 0) -> dict:
    key = jax.random.key(seed)
    ks = jax.random.split(key, 20)
    D = D_MODEL
    return {
        "x": _normal(ks[0], (BATCH, SEQ, D), 1.0),
        "c": _normal(ks[1], (BATCH, D), 1.0),
        "ada_w": _normal(ks[2], (DEPTH, D, 6 * D), D ** -0.5),
        "ada_b": _normal(ks[3], (DEPTH, 6 * D), 0.02),
        "pre_mix_g": 1.0 + _normal(ks[4], (DEPTH, D), 0.02),
        "post_mix_g": 1.0 + _normal(ks[5], (DEPTH, D), 0.02),
        "pre_ffn_g": 1.0 + _normal(ks[6], (DEPTH, D), 0.02),
        "post_ffn_g": 1.0 + _normal(ks[7], (DEPTH, D), 0.02),
        "w_in": _normal(ks[8], (DEPTH, D, IN_COLS), D ** -0.5),
        "conv_w": _normal(ks[9], (DEPTH, CONV_KERNEL, CONV_WIDTH), CONV_KERNEL ** -0.5),
        "conv_b": _normal(ks[10], (DEPTH, CONV_WIDTH), 0.02),
        "conv_ln_g": 1.0 + _normal(ks[11], (DEPTH, CONV_WIDTH), 0.02),
        "conv_ln_b": _normal(ks[12], (DEPTH, CONV_WIDTH), 0.02),
        "w_conv_out": _normal(ks[13], (DEPTH, CONV_WIDTH, D), CONV_WIDTH ** -0.5),
        "w_att_out": _normal(ks[14], (DEPTH, ATT_WIDTH, D), ATT_WIDTH ** -0.5),
        "w_o": _normal(ks[15], (DEPTH, D, D), D ** -0.5),
        "w_ffn_in": _normal(ks[16], (DEPTH, D, 2 * D_FF), D ** -0.5),
        "w_ffn_out": _normal(ks[17], (DEPTH, D_FF, D), D_FF ** -0.5),
    }

def first_block(x, c, ada_w, ada_b, pre_mix_g, post_mix_g, pre_ffn_g, post_ffn_g, w_in, conv_w, conv_b,
              conv_ln_g, conv_ln_b, w_conv_out, w_att_out, w_o, w_ffn_in, w_ffn_out):
    c_act = jax.nn.silu(c)
    for l in range(DEPTH):
        mod = c_act @ ada_w[l] + ada_b[l]
        sh1, sc1, ga1, sh2, sc2, ga2 = [m[:, None, :] for m in jnp.split(mod, 6, axis=-1)]
        h = rmsnorm(x, pre_mix_g[l]) * (1.0 + sc1) + sh1
        y = hybrid_mixer(h, w_in[l], conv_w[l], conv_b[l], conv_ln_g[l], conv_ln_b[l],
                         w_conv_out[l], w_att_out[l], w_o[l])
        x = x + ga1 * rmsnorm(y, post_mix_g[l])
        h = rmsnorm(x, pre_ffn_g[l]) * (1.0 + sc2) + sh2
        y = swiglu_ffn(h, w_ffn_in[l], w_ffn_out[l])
        x = x + ga2 * rmsnorm(y, post_ffn_g[l])
    return x


RET_HEADS = 8
RET_HEAD_DIM = 64
RET_WIDTH = RET_HEADS * RET_HEAD_DIM
RET_CHUNK = 128
MLA_HEADS = 8
MLA_NOPE_DIM = 64
MLA_ROPE_DIM = 32
MLA_V_DIM = 64
MLA_Q_RANK = 256
MLA_KV_RANK = 128
MLA_WIDTH = MLA_HEADS * MLA_V_DIM
MIX_WIDTH = RET_WIDTH + MLA_WIDTH
IN_WIDTH = 4 * RET_WIDTH + MLA_Q_RANK + MLA_KV_RANK + MLA_ROPE_DIM
D_FF_2 = 2816
CONV_WIDTH_2 = 3
ROPE_BASE = 10000.0


def rms_norm(x, w):
    xf = x.astype(jnp.float32)
    y = xf * lax.rsqrt(jnp.mean(xf * xf, axis=-1, keepdims=True) + EPS)
    return (y * w.astype(jnp.float32)).astype(x.dtype)

def rope(x, positions):
    d = x.shape[-1]
    inv_freq = ROPE_BASE ** (-jnp.arange(0, d, 2, dtype=jnp.float32) / d)
    ang = positions.astype(jnp.float32)[..., None] * inv_freq
    if x.ndim == 4:
        ang = ang[:, :, None, :]
    cos, sin = jnp.cos(ang), jnp.sin(ang)
    xf = x.astype(jnp.float32)
    x1, x2 = xf[..., : d // 2], xf[..., d // 2:]
    return jnp.concatenate([x1 * cos - x2 * sin, x1 * sin + x2 * cos], axis=-1).astype(x.dtype)

def retention(q, k, v):
    B, S, H, dk = q.shape
    dv = v.shape[-1]
    C = RET_CHUNK
    N = S // C
    log_gamma = jnp.log1p(-jnp.power(2.0, -5.0 - jnp.arange(H, dtype=jnp.float32)))
    qc = q.astype(jnp.float32).reshape(B, N, C, H, dk)
    kc = k.astype(jnp.float32).reshape(B, N, C, H, dk)
    vc = v.astype(jnp.float32).reshape(B, N, C, H, dv)
    idx = jnp.arange(C, dtype=jnp.float32)
    diff = idx[:, None] - idx[None, :]
    decay_mask = jnp.where(diff >= 0, jnp.exp(log_gamma[:, None, None] * jnp.maximum(diff, 0.0)), 0.0)
    scores = jnp.einsum('bnihd,bnjhd->bnhij', qc, kc) * decay_mask
    o_inner = jnp.einsum('bnhij,bnjhe->bnihe', scores, vc)
    zeta = jnp.exp(log_gamma[:, None] * (C - 1.0 - idx))
    chunk_states = jnp.einsum('bnjhd,hj,bnjhe->nbhde', kc, zeta, vc)
    chunk_decay = jnp.exp(log_gamma * C)[None, :, None, None]

    def step(R, s_n):
        return chunk_decay * R + s_n, R

    _, r_prev = lax.scan(step, jnp.zeros((B, H, dk, dv), jnp.float32), chunk_states)
    r_prev = jnp.moveaxis(r_prev, 0, 1)
    xi = jnp.exp(log_gamma[:, None] * (idx + 1.0))
    o_cross = jnp.einsum('bnihd,bnhde,hi->bnihe', qc, r_prev, xi)
    return (o_inner + o_cross).reshape(B, S, H, dv)

def retention_group(q, k, v, g, positions, gn_w):
    B, S, _ = q.shape
    q = rope(q.reshape(B, S, RET_HEADS, RET_HEAD_DIM), positions)
    k = rope(k.reshape(B, S, RET_HEADS, RET_HEAD_DIM), positions) * (RET_HEAD_DIM ** -0.5)
    v = v.reshape(B, S, RET_HEADS, RET_HEAD_DIM)
    o = retention(q, k, v)
    mu = jnp.mean(o, axis=-1, keepdims=True)
    var = jnp.mean(jnp.square(o - mu), axis=-1, keepdims=True)
    o = ((o - mu) * lax.rsqrt(var + EPS)).reshape(B, S, RET_WIDTH) * gn_w.astype(jnp.float32)
    return (jax.nn.silu(g.astype(jnp.float32)) * o).astype(g.dtype)

def mla_group(c_q, c_kv, k_pe, positions, q_norm_w, w_uq, kv_norm_w, w_ukv):
    B, S, _ = c_q.shape
    H = MLA_HEADS
    q = jnp.einsum('bsr,rf->bsf', rms_norm(c_q, q_norm_w), w_uq).reshape(B, S, H, MLA_NOPE_DIM + MLA_ROPE_DIM)
    q_nope = q[..., :MLA_NOPE_DIM]
    q_pe = rope(q[..., MLA_NOPE_DIM:], positions)
    kv = jnp.einsum('bsr,rf->bsf', rms_norm(c_kv, kv_norm_w), w_ukv).reshape(B, S, H, MLA_NOPE_DIM + MLA_V_DIM)
    k_nope = kv[..., :MLA_NOPE_DIM]
    v = kv[..., MLA_NOPE_DIM:]
    k_pe = rope(k_pe, positions)
    scale = (MLA_NOPE_DIM + MLA_ROPE_DIM) ** -0.5
    N = S // Q_BLOCK
    qn_b = jnp.moveaxis(q_nope.reshape(B, N, Q_BLOCK, H, MLA_NOPE_DIM), 1, 0)
    qp_b = jnp.moveaxis(q_pe.reshape(B, N, Q_BLOCK, H, MLA_ROPE_DIM), 1, 0)
    key_pos = jnp.arange(S)
    neg = jnp.finfo(jnp.float32).min

    def block(args):
        qn, qp, blk = args
        s = (jnp.einsum('bqhd,bkhd->bhqk', qn, k_nope)
             + jnp.einsum('bqhr,bkr->bhqk', qp, k_pe)).astype(jnp.float32) * scale
        q_pos = blk * Q_BLOCK + jnp.arange(Q_BLOCK)
        s = jnp.where(key_pos[None, :] <= q_pos[:, None], s, neg)
        p = jax.nn.softmax(s, axis=-1).astype(v.dtype)
        return jnp.einsum('bhqk,bkhd->bqhd', p, v)

    o = lax.map(block, (qn_b, qp_b, jnp.arange(N)))
    return jnp.moveaxis(o, 0, 1).reshape(B, S, MLA_WIDTH)

def conv_ffn(h, w_up, conv_w, conv_b, w_down):
    S = h.shape[1]
    u = jnp.einsum('bsd,df->bsf', h, w_up)
    up = jnp.pad(u, ((0, 0), (CONV_WIDTH_2 - 1, 0), (0, 0)))
    u = conv_b + sum(conv_w[j] * up[:, j:j + S] for j in range(CONV_WIDTH_2))
    gate, val = u[..., :D_FF_2], u[..., D_FF_2:]
    return jnp.einsum('bsf,fd->bsd', jax.nn.silu(gate) * val, w_down)

def second_inputs(seed: int = 0) -> dict:
    key = jax.random.key(seed)
    ks = jax.random.split(key, 20)
    f32 = jnp.float32

    def nrm(k, shape, fan_in):
        return jax.random.normal(k, shape, f32) * (fan_in ** -0.5)

    def gain(k, shape):
        return 1.0 + 0.02 * jax.random.normal(k, shape, f32)

    x = jax.random.normal(ks[0], (BATCH, SEQ, D_MODEL), f32)
    offset = jax.random.randint(ks[1], (BATCH, 1), 0, 4096, dtype=jnp.int32)
    positions = (offset + jnp.arange(SEQ, dtype=jnp.int32)[None, :]).astype(jnp.int32)
    return {
        "x": x,
        "positions": positions,
        "attn_norm_w": gain(ks[2], (DEPTH, D_MODEL)),
        "w_in": nrm(ks[3], (DEPTH, D_MODEL, IN_WIDTH), D_MODEL),
        "ret_gn_w": gain(ks[4], (DEPTH, RET_WIDTH)),
        "mla_q_norm_w": gain(ks[5], (DEPTH, MLA_Q_RANK)),
        "w_uq": nrm(ks[6], (DEPTH, MLA_Q_RANK, MLA_HEADS * (MLA_NOPE_DIM + MLA_ROPE_DIM)), MLA_Q_RANK),
        "mla_kv_norm_w": gain(ks[7], (DEPTH, MLA_KV_RANK)),
        "w_ukv": nrm(ks[8], (DEPTH, MLA_KV_RANK, MLA_HEADS * (MLA_NOPE_DIM + MLA_V_DIM)), MLA_KV_RANK),
        "w_out": nrm(ks[9], (DEPTH, MIX_WIDTH, D_MODEL), MIX_WIDTH),
        "ffn_norm_w": gain(ks[10], (DEPTH, D_MODEL)),
        "w_up": nrm(ks[11], (DEPTH, D_MODEL, 2 * D_FF_2), D_MODEL),
        "conv_w": nrm(ks[12], (DEPTH, CONV_WIDTH_2, 2 * D_FF_2), CONV_WIDTH_2),
        "conv_b": 0.01 * jax.random.normal(ks[13], (DEPTH, 2 * D_FF_2), f32),
        "w_down": nrm(ks[14], (DEPTH, D_FF_2, D_MODEL), D_FF_2),
        "final_norm_w": gain(ks[15], (D_MODEL,)),
    }

def second_block(x, positions, attn_norm_w, w_in, ret_gn_w, mla_q_norm_w, w_uq, mla_kv_norm_w, w_ukv,
              w_out, ffn_norm_w, w_up, conv_w, conv_b, w_down, final_norm_w):
    splits = np.cumsum([RET_WIDTH, RET_WIDTH, RET_WIDTH, RET_WIDTH, MLA_Q_RANK, MLA_KV_RANK]).tolist()
    for l in range(DEPTH):
        h = rms_norm(x, attn_norm_w[l])
        proj = jnp.einsum('bsd,df->bsf', h, w_in[l])
        r_q, r_k, r_v, r_g, c_q, c_kv, k_pe = jnp.split(proj, splits, axis=-1)
        y_ret = retention_group(r_q, r_k, r_v, r_g, positions, ret_gn_w[l])
        y_mla = mla_group(c_q, c_kv, k_pe, positions, mla_q_norm_w[l], w_uq[l],
                          mla_kv_norm_w[l], w_ukv[l])
        mixed = jnp.concatenate([y_ret, y_mla.astype(y_ret.dtype)], axis=-1)
        x = x + jnp.einsum('bsm,md->bsd', mixed, w_out[l])
        x = x + conv_ffn(rms_norm(x, ffn_norm_w[l]), w_up[l], conv_w[l], conv_b[l], w_down[l])
    return rms_norm(x, final_norm_w)


def setup_inputs(seed=0):
    out = dict(first_inputs(seed))
    for name, value in second_inputs(seed + 1).items():
        if name != "x":
            out[name + "_2"] = value
    return out


def reference(
    x, c, ada_w, ada_b, pre_mix_g, post_mix_g, pre_ffn_g, post_ffn_g, w_in, conv_w, conv_b,
    conv_ln_g, conv_ln_b, w_conv_out, w_att_out, w_o, w_ffn_in, w_ffn_out, positions_2,
    attn_norm_w_2, w_in_2, ret_gn_w_2, mla_q_norm_w_2, w_uq_2, mla_kv_norm_w_2, w_ukv_2,
    w_out_2, ffn_norm_w_2, w_up_2, conv_w_2, conv_b_2, w_down_2, final_norm_w_2,
):
    x = first_block(
        x, c, ada_w, ada_b, pre_mix_g, post_mix_g, pre_ffn_g, post_ffn_g, w_in, conv_w, conv_b,
        conv_ln_g, conv_ln_b, w_conv_out, w_att_out, w_o, w_ffn_in, w_ffn_out,
    )
    return second_block(
        x, positions_2, attn_norm_w_2, w_in_2, ret_gn_w_2, mla_q_norm_w_2, w_uq_2,
        mla_kv_norm_w_2, w_ukv_2, w_out_2, ffn_norm_w_2, w_up_2, conv_w_2, conv_b_2, w_down_2,
        final_norm_w_2,
    )


_drawn_inputs = setup_inputs


def setup_inputs(seed=0):
    import zlib

    import numpy as np

    out = dict(_drawn_inputs(seed))
    spreads = {}
    factors = {'pre_mix_g': 3.869,
     'post_mix_g': 3.693,
     'pre_ffn_g': 3.872,
     'post_ffn_g': 5.016,
     'conv_b': 4.258,
     'conv_ln_g': 6.907,
     'conv_ln_b': 7.653,
     'attn_norm_w_2': 3.933,
     'ret_gn_w_2': 8.0,
     'mla_q_norm_w_2': 8.0,
     'mla_kv_norm_w_2': 8.0,
     'ffn_norm_w_2': 13.995,
     'conv_b_2': 27.351,
     'final_norm_w_2': 8.355}
    for name, (base, spread) in spreads.items():
        noise = np.random.default_rng([zlib.crc32(name.encode()), seed]).standard_normal(out[name].shape)
        drawn = base * np.exp(spread * noise) if base else spread * noise
        out[name] = __import__('jax').numpy.asarray(drawn.astype(out[name].dtype))
    for name, factor in factors.items():
        out[name] = (out[name] * factor).astype(out[name].dtype)
    return out
```

```python
from contextlib import ExitStack

import numpy as np
import concourse.bass as bass
from concourse import mybir

F32 = mybir.dt.float32
F32R = mybir.dt.float32r
I32 = mybir.dt.int32
ACT = mybir.ActivationFunctionType
ALU = mybir.AluOpType
AX = mybir.AxisListType

P = 128
S = 512
D = 1024
DC = D // P
FF = 2816
FC = FF // P
HEADS = 8
PAIRS = HEADS // 2
HD = 64
QB = S // P
EPS = 1e-6
MLA_SCALE = (64 + 32) ** -0.5
NEG = -1e30
TAPS = 32
PAD = TAPS - 1

STAGES = [
    ("glu", 4, 8), ("qk", 4, 8), ("val", 2, 8), ("gate", 8, 8),
    ("att_out", 4, 4), ("conv_out", 4, 4), ("mix_out", 4, 8),
    ("ffn_in0", 8, 8), ("ffn_out0", 4, 8), ("ffn_in1", 8, 8), ("ffn_out1", 4, 8), ("ffn_in2", 6, 8), ("ffn_out2", 4, 6),
    ("latent", 2, 8), ("ret_qk", 4, 8), ("ret_val", 2, 8), ("ret_gate", 2, 8),
    ("up_v", 2, 1), ("up_k", 2, 1), ("up_q", 4, 2), ("mix_out2", 4, 8),
    ("up0", 8, 8), ("down0", 4, 8), ("up1", 8, 8), ("down1", 4, 8), ("up2", 6, 8), ("down2", 4, 6),
]
FFN_PARTS = [8, 8, 6]
PART_AT = [0, 8, 16]
ADA_FIRST = 16
ADA_REST = 6 * DC - ADA_FIRST

VECTORS = [("c", DC), ("ada_b", 6 * DC), ("pre_mix_g", DC), ("post_mix_g", DC), ("pre_ffn_g", DC), ("post_ffn_g", DC),
           ("conv_w", 4 * TAPS), ("conv_b", 4), ("conv_ln_g", 4), ("conv_ln_b", 4),
           ("attn_norm_w_2", DC), ("ret_gn_w_2", PAIRS), ("mla_q_norm_w_2", 2), ("mla_kv_norm_w_2", 1),
           ("ffn_norm_w_2", DC), ("conv_w_2", 3 * 2 * FC), ("conv_b_2", 2 * FC), ("final_norm_w_2", DC)]
VEC, N_VEC = {}, 0
for _name, _n in VECTORS:
    VEC[_name] = N_VEC
    N_VEC += _n

MATS = ["ident", "tri", "ones_neg", "mask_kq", "mask_qk", "ones", "block_mean"]
SMALL = {"eps": 0, "freq_ret": 1, "sign_ret": 2, "freq_mla": 3, "sign_mla": 4, "log_gamma": 5}
N_SMALL = 16

BLOCK_AT = [0, 512, 1024, 896]
BLOCK_W = [S - kb * P for kb in range(QB)]
ZW = 1280
ROW_AT = [896, 1024, 512, 0]
ROW_W = [(t + 1) * P for t in range(QB)]
HALVES = [(0, 512), (512, ZW)]

NORMS = {}
_q = 0
for _e, (_name, _n) in enumerate([("pre_mix", 8), ("conv_ln", 4), ("post_mix", 8), ("pre_ffn", 8), ("post_ffn", 8),
                                  ("attn2", 8), ("c_q", 2), ("c_kv", 1), ("ffn2", 8), ("final", 8)]):
    NORMS[_name] = (_e, _q, _n)
    _q += _n
MADE = {"pre_mix": 0, "conv": 8, "pre_ffn": 12, "attn2": 20, "lat": 28, "gn": 31, "ffn2": 35}

MAGIC = 1.5 * 2.0 ** 23
TWO_PI = [6.28125, float(np.float32(0.0019350051879882812)), 2 * np.pi - 6.28125 - float(np.float32(0.0019350051879882812))]
PI = float(np.nextafter(np.float32(np.pi), np.float32(0)))


class Stage:

    def __init__(self, name, groups, chunks, first):
        self.name, self.n, self.kc, self.g0, self.next = name, groups, chunks, first, None


def plan():
    out, g = {}, 0
    for name, n, kc in STAGES:
        out[name] = Stage(name, n, kc, g)
        g += n
    order = list(out.values())
    for a, b in zip(order, order[1:]):
        a.next = b
    return out


def positive(v):
    return not isinstance(v, int) or v > 0


def build(nc, dram, out):
    st = plan()
    off = [16512]

    def fixed(name, shape, dt=F32):
        size = int(np.prod(shape[1:])) * 4
        t = nc.alloc_sbuf_tensor_at(name, shape, dt, offset=off[0])
        off[0] += (size + 31) // 32 * 32
        return t

    x = fixed("x", [P, DC, S])
    h_hi, h_lo = (fixed(f"h_{p}", [P, DC, S], F32R) for p in ("hi", "lo"))
    raw = [fixed(f"raw{s}", [P, 8, 256]) for s in range(2)]
    w_hi = [fixed(f"w_hi{s}", [P, 8, 256], F32R) for s in range(2)]
    w_lo = [fixed(f"w_lo{s}", [P, 8, 256], F32R) for s in range(2)]
    vec, small = fixed("vec", [P, N_VEC]), fixed("small", [P, N_SMALL])
    mod, gain, c_act = fixed("mod", [P, 6 * DC]), fixed("gain", [P, 4, DC]), fixed("c_act", [P, DC])
    spare = fixed("spare", [P, 1])
    row_stat = fixed("row_stat", [P, 2, 16])
    rounded = fixed("rounded", [P, 5, P], F32R)
    ident, ones, block_mean = fixed("ident", [P, P]), fixed("ones", [P, P]), fixed("block_mean", [P, P])
    ident_r, tri_r, ones_neg_r, mask_kq_r, mask_qk_r = (rounded[:, k, :] for k in range(5))
    BASE = off[0]
    ROOM = 229344 - BASE

    def at(name, kb, shape, dt=F32):
        size = int(np.prod(shape[1:])) * 4
        assert kb * 1024 + size <= ROOM, (name, kb, size, ROOM)
        return nc.alloc_sbuf_tensor_at(name, shape, dt, offset=BASE + int(kb * 1024))

    ada_first = at("ada_first", 0, [P, ADA_FIRST, 8, P])
    ada_acc0 = at("ada_acc0", 64, [P, 4, 4, P])
    const_raw = at("const_raw", 96.5, [P, 5, P])
    qkT = at("qkT", 0, [P, 2 * PAIRS, S])
    v_rows = at("v_rows", 16, [P, QB, S])
    zbuf = at("zbuf", 24, [P, ZW])
    ada_acc = [at(f"ada_acc_{s}", 29 + s / 2, [P, P]) for s in range(2)]
    conv_tmp = at("conv_tmp", 30, [P, S])
    gates = at("gates", 32, [P, 2 * DC, S])
    u = at("u", 64, [P, 4, PAD + S])
    conv3 = at("conv3", 72.5, [P, S])
    stage_hi = at("stage_hi", 74.5, [P, 3, S], F32R)
    stage_lo = at("stage_lo", 80.5, [P, 3, S], F32R)
    t_hi, t_lo = at("t_hi", 86.5, [P, ZW], F32R), at("t_lo", 91.5, [P, ZW], F32R)
    ada_raw = [at(f"ada_raw{s}", 96.5 + 4 * s, [P, 8, P]) for s in range(2)]
    glu_sig = [at(f"glu_sig{s}", 92.5 + 2 * s, [P, S]) for s in range(2)]
    sq = [at(f"sq{s}", 74.5 + 2 * s, [P, S]) for s in range(2)]
    sq_sum = at("sq_sum", 78.5, [P, S])
    rs = at("rs", 80.5, [P, S])
    t_n = [at(f"t_n{s}", 82.5 + 2 * s, [P, S]) for s in range(2)]
    h_f = [at(f"h_f{s}", 86.5 + 2 * s, [P, S]) for s in range(2)]
    mean, ln_ms = at("mean", 90.5, [P, S]), at("ln_ms", 92.5, [P, S])
    mid_hi, mid_lo = at("mid_hi", 0, [P, DC, S], F32R), at("mid_lo", 16, [P, DC, S], F32R)
    y = at("y", 32, [P, DC, S])
    act_a = [at(f"act_a{s}", 48 + 2 * s, [P, S]) for s in range(2)]
    act_b = [at(f"act_b{s}", 52 + 2 * s, [P, S]) for s in range(2)]
    act_p = [at(f"act_p{s}", 56 + 2 * s, [P, S]) for s in range(2)]
    cos_ret, sin_ret, cos_mla, sin_mla = (at(n, 61 + 2 * k, [P, S]) for k, n in
                                          enumerate(["cos_ret", "sin_ret", "cos_mla", "sin_mla"]))
    pos_i = at("pos_i", 94.5, [P, S], I32)
    pos_f, angle, turns = (at(n, 96.5 + 2 * k, [P, S]) for k, n in enumerate(["pos_f", "angle", "turns"]))
    rqk = at("rqk", 0, [P, 2 * PAIRS, S])
    rv_rows = at("rv_rows", 16, [P, QB, S])
    rgate = at("rgate", 24, [P, PAIRS, S])
    lat = at("lat", 32, [P, 3, S])
    lat_hi, lat_lo = at("lat_hi", 40, [P, 3, S], F32R), at("lat_lo", 46, [P, 3, S], F32R)
    swapped = [at(f"swapped{s}", 52 + 2 * s, [P, S]) for s in range(2)]
    lag = at("lag", 57, [P, S])
    decay = [at(f"decay{s}", 61 + 2 * s, [P, S]) for s in range(2)]
    rope_t = [at(f"rope_t{s}", 96.5 + 2 * s, [P, S]) for s in range(2)]
    kpe = at("kpe", 102.5, [P, S])
    rp = [at("rp0", 69, [P, ZW]), at("rp1", 32, [P, ZW])]
    r_hi = [t_hi, at("r_hi1", 96.5, [P, ZW], F32R)]
    r_lo = [t_lo, at("r_lo1", 52, [P, ZW], F32R)]
    mk, mv_rows, mq = at("mk", 16, [P, HEADS, S]), at("mv_rows", 32, [P, QB, S]), at("mq", 0, [P, HEADS, S])
    m_hi, m_lo = at("m_hi", 40, [P, 5, S], F32R), at("m_lo", 50, [P, 5, S], F32R)
    mp = [at("mp0", 74.5, [P, ZW]), at("mp1", 79.5, [P, ZW])]
    mt_lo = [t_lo, at("mt_lo1", 60, [P, ZW], F32R)]

    names = """in_const in_mats in_vec in_x in_lag in_pos ada_f0 ada_f1 ada_f2 ada_f3 ada_a0 ada_a1 raw_full0 raw_full1
        rounded c_act ada0_step ada0_sum mod0_cols mod0_done gain_step gain_done
        w_hi_done w_lo_done tile_done group_free
        sq_done sum_done stat_done ms_done rs_done tn_done hf_done made_hi made_lo upd_step x_done
        ada_step ada_sum mod_cols mod_done
        sig_done tap
        stg_hi stg_lo z_done zm_done e_done l_done sp_done sph_done spl_done cum_done a_done ah_done al_done o_done o_evac
        gate_sig osp_hi osp_lo mean_ps mean_done xc_done
        merge_m mid_silu mid_f mid_hi_done mid_lo_done
        ident_done conv2 silu_arg
        ang_step ang_arg trig sw_done rope_m rope_s rp_done lat_done kpe_done
        rz_done dec_done rp_f rp_hi rp_lo ro_done ro_evac
        gn_mean gn_xc gn_sq gn_var gn_y
        mq_done qrope_done mstg_hi mstg_lo kst_hi kst_lo mz_done mx_done nmx_done mp_done rcp_done pn_done mt_done mth mtl
        mo_done mo_evac mos_hi mos_lo fin_done out_done""".split()

    with ExitStack() as ctx:
        sem = {n: ctx.enter_context(nc.semaphore(n)) for n in names}
        psum = ctx.enter_context(nc.psum_tensor("psum", [P, 8 * S], F32))
        bank = [psum[:, b * S:(b + 1) * S] for b in range(8)]
        z2 = [psum[:, 4 * S:7 * S], psum[:, 0:3 * S]]
        o2 = [bank[7], bank[3]]
        z, o_ps = z2[0], o2[0]
        mod_ps = z[:, ZW:ZW + 6 * DC]
        raw_full = [sem["raw_full0"], sem["raw_full1"]]
        ada_full = [sem["ada_a0"], sem["ada_a1"]]
        block = ctx.enter_context(nc.Block())

        def col(name, k=0, n=1):
            return vec[:, bass.ds(VEC[name] + k, n)]

        def scol(name, k=0):
            return small[:, bass.ds(SMALL[name] + k, 1)]

        def rstds(name):
            return NORMS[name][0] + (PAIRS if name in ("ffn2", "final") else 0)

        def chunk(t, k, rows=slice(0, P)):
            return t[rows, bass.ds(k, 1), :].rearrange("p a n -> p (a n)")

        def pair_v(t):
            return t.rearrange("p (b n) -> p b n", b=QB)

        @block.sync
        def _(sp):
            sp.dma_start(small[:, :], dram["small"]).then_inc(sem["in_const"], 16)
            sp.dma_start(vec[:, :], dram["vec"]).then_inc(sem["in_vec"], 16)
            sp.dma_start(x[:, :, :], dram["x"]).then_inc(sem["in_x"], 16)
            sp.dma_start(const_raw[:, :, :], dram["mats"][:, 0:5, :]).then_inc(sem["in_mats"], 16)
            for t, k in ((ident, 0), (ones, 5), (block_mean, 6)):
                sp.dma_start(t[:, :], dram["mats"][:, k, :]).then_inc(sem["in_mats"], 16)
            for b in range(4):
                sp.dma_start(ada_first[:, 4 * b:4 * b + 4], dram["ada"][4 * b:4 * b + 4].rearrange("g p k n -> p g k n")
                             ).then_inc(sem[f"ada_f{b}"], 16)

            def load(stage, k, slot):
                g = stage.g0 + k
                if positive(g - 1):
                    sp.wait_ge(sem["w_lo_done"], g - 1)
                sp.dma_start(raw[slot][:, 0:stage.kc, :].rearrange("p k n -> p (k n)"),
                             dram["w_" + stage.name][bass.ds(k, 1)].rearrange("g p n -> p (g n)")).then_inc(raw_full[slot], 16)

            def load_ada(a, slot):
                if positive(a - 1):
                    sp.wait_ge(sem["ada_sum"], a - 1)
                if isinstance(a, int) and a == 0:
                    sp.wait_ge(sem["rounded"], 1)
                sp.dma_start(ada_raw[slot][:, :, :].rearrange("p k n -> p (k n)"),
                             dram["ada"][bass.ds(ADA_FIRST + a, 1)].rearrange("g p k n -> p (g k n)")).then_inc(ada_full[slot], 16)

            def stage_loads(stage, ada=None, per=0):
                def body(i):
                    for s in range(2):
                        load(stage, 2 * i + s, s)
                        for r in range(per):
                            load_ada(ada + (2 * i + s) * per + r, r if per > 1 else s)
                first = 1 if stage.g0 == 0 or ada == 0 else 0
                if first:
                    body(0)
                with sp.Fori(first, stage.n // 2) as i:
                    body(i)

            stage_loads(st["glu"])
            stage_loads(st["qk"], 0, 2)
            stage_loads(st["val"], 8, 2)
            stage_loads(st["gate"], 12, 2)
            stage_loads(st["att_out"], 28, 1)
            stage_loads(st["conv_out"])
            stage_loads(st["mix_out"])
            stage_loads(st["ffn_in0"])
            sp.wait_ge(sem["made_lo"], MADE["attn2"])
            sp.dma_start(pos_i[:, :], dram["positions"].to_broadcast([P, S])).then_inc(sem["in_pos"], 16)
            for name in ["ffn_out0", "ffn_in1", "ffn_out1", "ffn_in2", "ffn_out2"]:
                stage_loads(st[name])
            sp.wait_ge(sem["mid_lo_done"], 8 + FC)
            sp.dma_start(lag[:, :], dram["lag"]).then_inc(sem["in_lag"], 16)
            for name in ["latent", "ret_qk", "ret_val", "ret_gate", "up_v", "up_k", "up_q", "mix_out2",
                         "up0", "down0", "up1", "down1", "up2", "down2"]:
                stage_loads(st[name])
            for k in range(DC):
                sp.wait_ge(sem["fin_done"], k + 1)
                sp.dma_start(out[:, k], y[:, k]).then_inc(sem["out_done"], 16)
            sp.wait_ge(sem["out_done"], 16 * DC)

        @block.tensor
        def _(pe):
            mm = nc.tensor.matmul

            def stat_sum(name):
                e, q0, n = NORMS[name]
                pe.wait_ge(sem["sum_done"], q0 + n)
                if e:
                    pe.wait_ge(sem["ms_done"], rstds(name))
                mm(o_ps, ones[:, :], sq_sum[:, :], start=True, stop=True).then_inc(sem["stat_done"], 1)

            def tile(stage, slot, t, x_hi, x_lo, k0=0, rows=False, ready=None):
                ps, kc = bank[2 * slot + t], stage.kc
                for r in range(2 if rows else 1):
                    for n, (w, xv) in enumerate(((w_hi, x_hi), (w_lo, x_hi), (w_hi, x_lo))):
                        for k in range(kc):
                            if ready and n == 0 and slot == 0 and t == 0 and r == 0 and k >= ready[2]:
                                pe.wait_ge(sem[ready[0]], ready[1] + k - ready[2] + 1)
                            first, final = n == 0 and k == 0, n == 2 and k == kc - 1
                            if rows:
                                b = 2 * t + r
                                last = mm(ps[:, r * 256:(r + 1) * 256], xv[:, k0 + k, b * P:(b + 1) * P], w[slot][:, k, :],
                                          start=first, stop=final)
                            else:
                                last = mm(ps, w[slot][:, k, t * P:(t + 1) * P], xv[:, k0 + k, :], start=first, stop=final)
                last.then_inc(sem["tile_done"], 1)

            def weights(g):
                pe.wait_ge(sem["w_lo_done"], g + 1)
                if positive(g - 1):
                    pe.wait_ge(sem["group_free"], g - 1)

            def mod_column(a, slot):
                pe.wait_ge(sem["ada_sum"], a + 1)
                mm(psum[:, bass.ds(4 * S + ZW + ADA_FIRST + a, 1)], ada_acc[slot][:, :], ones[:, 0:1], start=True, stop=True
                   ).then_inc(sem["mod_cols"], 1)

            def gemm(stage, x_hi, x_lo, k0=0, rows=False, ready=None, ada=0, per=0):
                def body(i):
                    for s in range(2):
                        for r in range(per):
                            mod_column(ada + (2 * i + s) * per + r, r if per > 1 else s)
                        weights(stage.g0 + 2 * i + s)
                        for t in range(2):
                            tile(stage, s, t, x_hi, x_lo, k0, rows, ready)
                first = 1 if stage.g0 == 0 else 0
                if first:
                    body(0)
                with pe.Fori(first, stage.n // 2) as i:
                    body(i)

            def scores(zz, q_rows, k_rows, q_at, k_at, hi, lo, start_mask):
                for kb in range(QB):
                    a, w = BLOCK_AT[kb], BLOCK_W[kb]
                    for n, (kk, qq) in enumerate(((hi, hi), (hi, lo), (lo, hi))):
                        last = mm(zz[:, a:a + w], kk[k_rows, k_at, kb * P:(kb + 1) * P], qq[q_rows, q_at, kb * P:S],
                                  start=(n == 0 and kb < 3), stop=(n == 2), skip_group_check=True)
                    if start_mask:
                        last = mm(zz[:, a:a + P], ident_r, mask_kq_r, start=False, stop=True, skip_group_check=True)
                return last

            def values(o, vs_hi, vs_lo, v_at, p_hi, p_lo):
                for kb in range(QB):
                    a, w = BLOCK_AT[kb], BLOCK_W[kb]
                    for n, (vv, aa) in enumerate(((vs_hi, p_hi), (vs_hi, p_lo), (vs_lo, p_hi))):
                        last = mm(o[:, kb * P:S], vv[:, v_at, kb * P:(kb + 1) * P], aa[:, a:a + w],
                                  start=(n == 0 and kb == 0), stop=(n == 2 and kb == QB - 1), skip_group_check=True)
                return last

            pe.wait_ge(sem["in_mats"], 64)
            stat_sum("pre_mix")
            for b in range(4):
                pe.wait_ge(sem["ada0_sum"], b + 1)
                for k in range(4):
                    last = mm(mod_ps[:, 4 * b + k:4 * b + k + 1], ada_acc0[:, b, k, :], ones[:, 0:1], start=True, stop=True)
                last.then_inc(sem["mod0_cols"], 1)
            pe.wait_ge(sem["mod0_done"], 1)
            gemm(st["glu"], h_hi, h_lo, ready=("made_lo", MADE["pre_mix"], 0))
            gemm(st["qk"], h_hi, h_lo, ada=0, per=2)
            gemm(st["val"], h_hi, h_lo, rows=True, ada=8, per=2)

            def head(i, s):
                rows, n = slice(HD * s, HD * s + HD), 2 * i + s
                for r in range(2):
                    mod_column(12 + n * 2 + r, r)
                if s == 0:
                    pe.wait_ge(sem["stg_lo"], 3 * i + 2)
                scores(z, rows, rows, 0, 1, stage_hi, stage_lo, True).then_inc(sem["z_done"], 1)
                weights(st["gate"].g0 + n)
                tile(st["gate"], s, 0, h_hi, h_lo)
                pe.wait_ge(sem["spl_done"], 2 * n + 2)
                for kb in range(QB):
                    a, w = BLOCK_AT[kb], BLOCK_W[kb]
                    for part in (t_hi, t_lo):
                        last = mm(z[:, a:a + w], tri_r, part[:, a:a + w], start=False, stop=True, skip_group_check=True)
                        for later in range(kb + 1, QB):
                            a2, w2 = BLOCK_AT[later], BLOCK_W[later]
                            last = mm(z[:, a + w - w2:a + w], ones_neg_r, part[:, a2:a2 + w2], start=False, stop=True,
                                      skip_group_check=True)
                last.then_inc(sem["cum_done"], 1)
                tile(st["gate"], s, 1, h_hi, h_lo)
                pe.wait_ge(sem["al_done"], n + 1)
                if s == 0:
                    pe.wait_ge(sem["stg_lo"], 3 * i + 3)
                else:
                    pe.wait_ge(sem["o_evac"], n)
                values(o_ps, stage_hi, stage_lo, 2, t_hi, t_lo).then_inc(sem["o_done"], 1)

            with pe.Fori(0, PAIRS) as i:
                for s in range(2):
                    head(i, s)
            gemm(st["att_out"], h_hi, h_lo, k0=4, ready=("osp_lo", 0, 0), ada=28, per=1)
            pe.wait_ge(sem["tap"], 4 * (TAPS + 1))
            pe.wait_ge(sem["o_evac"], HEADS)
            for k in range(4):
                last = mm(o_ps, ones[:, :], u[:, k, PAD:PAD + S] if k < 3 else conv3[:, :], start=(k == 0), stop=(k == 3))
            last.then_inc(sem["mean_ps"], 1)
            stat_sum("conv_ln")
            gemm(st["conv_out"], h_hi, h_lo, ready=("made_lo", MADE["conv"], 0))
            gemm(st["mix_out"], mid_hi, mid_lo, ready=("mid_lo_done", 0, 0))
            stat_sum("post_mix")
            stat_sum("pre_ffn")
            for r, n in enumerate(FFN_PARTS):
                gemm(st[f"ffn_in{r}"], h_hi, h_lo, ready=("made_lo", MADE["pre_ffn"], 0) if r == 0 else None)
                gemm(st[f"ffn_out{r}"], mid_hi, mid_lo, ready=("mid_lo_done", 8 + PART_AT[r], 0))
            stat_sum("post_ffn")
            stat_sum("attn2")
            gemm(st["latent"], h_hi, h_lo, ready=("made_lo", MADE["attn2"], 0))
            gemm(st["ret_qk"], h_hi, h_lo)
            stat_sum("c_q")
            stat_sum("c_kv")
            gemm(st["ret_val"], h_hi, h_lo, rows=True)
            gemm(st["ret_gate"], h_hi, h_lo)

            pe.wait_ge(sem["group_free"], st["up_v"].g0)
            with pe.Fori(0, PAIRS) as i:
                pe.wait_ge(sem["stg_lo"], 3 * PAIRS + 3 * i + 3)
                for s in range(2):
                    rows = slice(HD * s, HD * s + HD)
                    scores(z2[s], rows, rows, 0, 1, stage_hi, stage_lo, False).then_inc(sem["rz_done"], 1)
                for s in range(2):
                    pe.wait_ge(sem["rp_lo"], 2 * i + s + 1)
                    values(o2[s], stage_hi, stage_lo, 2, r_hi[s], r_lo[s]).then_inc(sem["ro_done"], 1)
            pe.wait_ge(sem["ro_evac"], HEADS)
            gemm(st["up_v"], lat_hi, lat_lo, k0=2, rows=True, ready=("made_lo", MADE["lat"] + 2, 0))
            for k in range(PAIRS):
                if k:
                    pe.wait_ge(sem["ms_done"], 8 + k)
                mm(o_ps, block_mean[:, :], rqk[:, k, :], start=True, stop=True).then_inc(sem["gn_mean"], 1)
                pe.wait_ge(sem["gn_sq"], k + 1)
                mm(o_ps, block_mean[:, :], sq[k % 2][:, :], start=True, stop=True).then_inc(sem["gn_var"], 1)
            gemm(st["up_k"], lat_hi, lat_lo, k0=2)
            gemm(st["up_q"], lat_hi, lat_lo, ready=("made_lo", MADE["lat"], 0))

            pe.wait_ge(sem["group_free"], st["mix_out2"].g0)
            pe.wait_ge(sem["kst_lo"], 2)
            with pe.Fori(0, PAIRS) as i:
                pe.wait_ge(sem["mstg_lo"], 5 * i + 5)
                for s in range(2):
                    for t in range(QB):
                        a, w = ROW_AT[t], ROW_W[t]
                        for n, (qq, kk) in enumerate(((m_hi, m_hi), (m_hi, m_lo), (m_lo, m_hi))):
                            mm(z2[s][:, a:a + w], qq[0:96, s, t * P:(t + 1) * P], kk[0:96, 2 + s, 0:w],
                               start=(n == 0), stop=(n == 2), skip_group_check=True)
                        last = mm(z2[s][:, a + w - P:a + w], ident_r, mask_qk_r, start=False, stop=True, skip_group_check=True)
                    last.then_inc(sem["mz_done"], 1)
                for s in range(2):
                    pe.wait_ge(sem["pn_done"], 2 * i + s + 1)
                    for kb in range(QB):
                        for t in range(kb, QB):
                            a = BLOCK_AT[kb] + (t - kb) * P
                            last = nc.tensor.transpose(z2[s][:, a:a + P], mp[s][:, ROW_AT[t] + kb * P:ROW_AT[t] + (kb + 1) * P],
                                                       ident[:, :])
                    last.then_inc(sem["mt_done"], 1)
                for s in range(2):
                    pe.wait_ge(sem["mtl"], 2 * i + s + 1)
                    values(o2[s], m_hi, m_lo, 4, r_hi[s], mt_lo[s]).then_inc(sem["mo_done"], 1)
            pe.wait_ge(sem["mo_evac"], HEADS)
            pe.wait_ge(sem["made_lo"], MADE["gn"] + PAIRS)
            gemm(st["mix_out2"], h_hi, h_lo, ready=("mos_lo", 0, PAIRS))
            stat_sum("ffn2")
            for r, n in enumerate(FFN_PARTS):
                gemm(st[f"up{r}"], h_hi, h_lo, ready=("made_lo", MADE["ffn2"], 0) if r == 0 else None)
                gemm(st[f"down{r}"], mid_hi, mid_lo, ready=("mid_lo_done", 8 + FC + PART_AT[r], 0))
            stat_sum("final")

        @block.scalar
        def _(act):
            A = nc.scalar.activation
            hf = [0]
            norms = [0]

            def apart():
                A(spare[:, :], small[:, 0:1], ACT.Copy)

            def split_hi(stage, k, slot, half):
                g = stage.g0 + k
                act.wait_ge(raw_full[slot], 16 * (stage.g0 // 2 + half + 1))
                if positive(g - 1):
                    act.wait_ge(sem["tile_done"], 2 * g - 2)
                A(w_hi[slot][:, 0:stage.kc, :], raw[slot][:, 0:stage.kc, :], ACT.Copy).then_inc(sem["w_hi_done"], 1)

            def run(stage, evac):
                def step(i, s, final=False):
                    def ahead():
                        if not (final and s):
                            split_hi(stage, 2 * i + s + 1, 1 - s, i + s)
                        elif stage.next:
                            split_hi(stage.next, 0, 0, 0)
                    evac(i, s, 2 * i + s, ahead)
                n = stage.n // 2
                if n == 2:
                    step(0, 0)
                    step(0, 1)
                elif n > 2:
                    with act.Fori(0, n - 1) as i:
                        step(i, 0)
                        step(i, 1)
                step(n - 1, 0, True)
                step(n - 1, 1, True)

            def arrived(stage, k, t):
                act.wait_ge(sem["tile_done"], 2 * (stage.g0 + k) + t + 1)

            def free(stage, k, ins_of):
                if positive(stage.g0 + k):
                    act.wait_ge(sem["group_free"], stage.g0 + k)
                ins_of().then_inc(sem["group_free"], 1)

            def squares(name, of, wait):
                e, q0, n = NORMS[name]
                for c in range(n):
                    if q0 + c >= 2:
                        act.wait_ge(sem["sum_done"], q0 + c - 1)
                    wait(c)
                    A(sq[(q0 + c) % 2][:, :], of(c), ACT.Square).then_inc(sem["sq_done"], 1)

            def rstd(width, wait):
                nc.scalar.preload_act_table_set("natural_log_exp_and_others")
                wait()
                A(ln_ms[:, :], o_ps, ACT.Ln, scale=1.0 / width, bias=scol("eps")).then_inc(sem["ms_done"], 1)
                norms[0] += 1
                act.wait_ge(sem["ms_done"], norms[0])
                A(rs[:, :], ln_ms[:, :], ACT.Exp, scale=-0.5).then_inc(sem["rs_done"], 1)

            def norm_rstd(name, width):
                rstd(width, lambda: act.wait_ge(sem["stat_done"], NORMS[name][0] + 1))

            def made(m, dst, shift=None, func=None):
                src = t_n[m % 2]
                act.wait_ge(sem["tn_done"], m + 1)
                if shift is not None:
                    if m >= 2:
                        act.wait_ge(sem["made_lo"], m - 1)
                    A(h_f[m % 2][:, :], src[:, :], func, bias=shift).then_inc(sem["hf_done"], 1)
                    hf[0] += 1
                    act.wait_ge(sem["hf_done"], hf[0])
                    src = h_f[m % 2]
                A(dst, src[:, :], ACT.Copy).then_inc(sem["made_hi"], 1)

            act.wait_ge(sem["in_vec"], 16)
            A(c_act[:, :], col("c", 0, DC), ACT.Silu).then_inc(sem["c_act"], 1)
            act.wait_ge(sem["in_x"], 16)
            squares("pre_mix", lambda c: x[:, c, :], lambda c: None)
            act.wait_ge(sem["in_mats"], 64)
            A(rounded[:, :, :], const_raw[:, :, :], ACT.Copy).then_inc(sem["rounded"], 1)
            act.wait_ge(sem["in_const"], 16)
            norm_rstd("pre_mix", D)
            act.wait_ge(sem["mod0_done"], 1)
            for c in range(DC):
                if c == 2:
                    split_hi(st["glu"], 0, 0, 0)
                made(MADE["pre_mix"] + c, h_hi[:, c, :], mod[:, c:c + 1], ACT.Identity)

            def glu(i, s, k, ahead):
                ahead()
                arrived(st["glu"], k, 1)
                if positive(k - 1):
                    act.wait_ge(sem["group_free"], k - 1)
                A(glu_sig[s][:, :], bank[2 * s + 1], ACT.Sigmoid).then_inc(sem["sig_done"], 1)

            def qk(i, s, k, ahead):
                ahead()
                arrived(st["qk"], k, 0)
                A(qkT[:, 2 * k, :], bank[2 * s], ACT.Copy)
                arrived(st["qk"], k, 1)
                free(st["qk"], k, lambda: A(qkT[:, 2 * k + 1, :], bank[2 * s + 1], ACT.Copy))

            def rows_of(stage, dst):
                def evac(i, s, k, ahead):
                    ahead()
                    cols = slice(256 * k, 256 * k + 256)
                    arrived(stage, k, 0)
                    A(dst[:, 0:2, cols], bank[2 * s].rearrange("p (b n) -> p b n", b=2), ACT.Copy)
                    arrived(stage, k, 1)
                    free(stage, k, lambda: A(dst[:, 2:4, cols], bank[2 * s + 1].rearrange("p (b n) -> p b n", b=2), ACT.Copy))
                return evac

            run(st["glu"], glu)
            run(st["qk"], qk)
            run(st["val"], rows_of(st["val"], v_rows))

            def stage_pair(i, q, k, v):
                A(stage_hi[:, 0, :], chunk(q, i), ACT.Copy, scale=HD ** -0.5
                  ).then_inc(sem["stg_hi"], 1)
                A(stage_hi[:, 1, :], chunk(k, PAIRS + i), ACT.Copy).then_inc(sem["stg_hi"], 1)
                A(pair_v(stage_hi[:, 2, :]), v[:, :, bass.ds(P * i, P)], ACT.Copy).then_inc(sem["stg_hi"], 1)

            def head(i, s, n, ahead):
                rows, g = slice(HD * s, HD * s + HD), st["gate"].g0 + n
                if s == 0:
                    stage_pair(i, qkT, qkT, v_rows)
                for j, (a, b) in enumerate(HALVES):
                    act.wait_ge(sem["zm_done"], 2 * n + j + 1)
                    A(zbuf[:, a:b], zbuf[:, a:b], ACT.Exp).then_inc(sem["e_done"], 1)
                for j, (a, b) in enumerate(HALVES):
                    act.wait_ge(sem["e_done"], 2 * n + j + 1)
                    A(zbuf[:, a:b], zbuf[:, a:b], ACT.Ln, bias=1.0).then_inc(sem["l_done"], 1)
                for j, (a, b) in enumerate(HALVES):
                    act.wait_ge(sem["sp_done"], 2 * n + j + 1)
                    A(t_hi[:, a:b], zbuf[:, a:b], ACT.Copy).then_inc(sem["sph_done"], 1)
                arrived(st["gate"], n, 0)
                A(chunk(gates, 2 * n), bank[2 * s], ACT.Copy)
                ahead()
                act.wait_ge(sem["cum_done"], n + 1)
                A(zbuf[:, :], z[:, 0:ZW], ACT.Exp).then_inc(sem["a_done"], 1)
                act.wait_ge(sem["a_done"], n + 1)
                A(t_hi[:, :], zbuf[:, :], ACT.Copy).then_inc(sem["ah_done"], 1)
                arrived(st["gate"], n, 1)
                free(st["gate"], n, lambda: A(chunk(gates, 2 * n + 1), bank[2 * s + 1], ACT.Copy))
                act.wait_ge(sem["o_done"], n + 1)
                apart()
                A(chunk(qkT, i, rows), o_ps[rows, :], ACT.Copy).then_inc(sem["o_evac"], 1)

            nc.scalar.preload_act_table_set("natural_log_exp_and_others")
            act.wait_ge(sem["group_free"], st["gate"].g0)
            run(st["gate"], head)
            act.wait_ge(sem["o_evac"], HEADS)
            for c in range(4):
                A(h_hi[:, 4 + c, :], qkT[:, c, :], ACT.Copy).then_inc(sem["osp_hi"], 1)
            act.wait_ge(sem["group_free"], st["att_out"].g0)
            A(gates[:, DC:, :], gates[:, DC:, :], ACT.Sigmoid).then_inc(sem["gate_sig"], 1)
            A(gates[:, 0:DC, :], gates[:, 0:DC, :], ACT.Sigmoid).then_inc(sem["gate_sig"], 1)
            run(st["att_out"], lambda i, s, k, ahead: ahead())
            act.wait_ge(sem["mean_ps"], 1)
            A(mean[:, :], o_ps, ACT.Copy, scale=1.0 / (4 * P)).then_inc(sem["mean_done"], 1)
            squares("conv_ln", lambda c: u[:, c, PAD:PAD + S] if c < 3 else conv3[:, :],
                    lambda c: act.wait_ge(sem["xc_done"], c + 1))
            norm_rstd("conv_ln", 4 * P)
            for c in range(4):
                made(MADE["conv"] + c, h_hi[:, c, :], col("conv_ln_b", c), ACT.Silu)

            def merged(i, s, k, ahead):
                ahead()
                for t in range(2):
                    n = 2 * k + t
                    act.wait_ge(sem["mid_f"], n + 1)
                    A(mid_hi[:, n, :], gates[:, n, :], ACT.Copy).then_inc(sem["mid_hi_done"], 1)

            def to_y(stage):
                def evac(i, s, k, ahead):
                    ahead()
                    arrived(stage, k, 0)
                    A(y[:, 2 * k, :], bank[2 * s], ACT.Copy)
                    arrived(stage, k, 1)
                    free(stage, k, lambda: A(y[:, 2 * k + 1, :], bank[2 * s + 1], ACT.Copy))
                return evac

            run(st["conv_out"], merged)
            run(st["mix_out"], to_y(st["mix_out"]))
            act.wait_ge(sem["group_free"], st["ffn_in0"].g0)
            squares("post_mix", lambda c: y[:, c, :], lambda c: None)
            norm_rstd("post_mix", D)
            squares("pre_ffn", lambda c: x[:, c, :], lambda c: act.wait_ge(sem["x_done"], c + 1))
            norm_rstd("pre_ffn", D)
            act.wait_ge(sem["mod_done"], 1)
            for c in range(DC):
                made(MADE["pre_ffn"] + c, h_hi[:, c, :], mod[:, 3 * DC + c:3 * DC + c + 1], ACT.Identity)

            def gated(stage):
                def evac(i, s, k, ahead):
                    ahead()
                    arrived(stage, k, 0)
                    act.wait_ge(sem["group_free"], stage.g0 + k - 1)
                    A(act_a[s][:, :], bank[2 * s], ACT.Silu).then_inc(sem["mid_silu"], 1)
                    act.wait_ge(sem["group_free"], stage.g0 + k + 1)
                    A(chunk(mid_hi, k), act_p[s][:, :], ACT.Copy
                      ).then_inc(sem["mid_hi_done"], 1)
                return evac

            for r in range(3):
                run(st[f"ffn_in{r}"], gated(st[f"ffn_in{r}"]))
                if r == 0:
                    for k, table in enumerate((sin_ret, cos_ret, sin_mla, cos_mla)):
                        act.wait_ge(sem["ang_arg"], k + 1)
                        A(table[:, :], table[:, :], ACT.Sin).then_inc(sem["trig"], 1)
                run(st[f"ffn_out{r}"], to_y(st["ffn_out0"]) if r == 0 else (lambda i, s, k, ahead: ahead()))
            squares("post_ffn", lambda c: y[:, c, :], lambda c: act.wait_ge(sem["group_free"], st["ffn_out2"].g0 + c // 2 + 1))
            norm_rstd("post_ffn", D)
            squares("attn2", lambda c: x[:, c, :], lambda c: act.wait_ge(sem["x_done"], 8 + c + 1))
            norm_rstd("attn2", D)
            for c in range(DC):
                made(MADE["attn2"] + c, h_hi[:, c, :])

            def latent(i, s, k, ahead):
                ahead()
                arrived(st["latent"], k, 0)
                A(lat[:, 2 * k, :], bank[2 * s], ACT.Copy).then_inc(sem["lat_done"], 1)
                if k == 0:
                    arrived(st["latent"], k, 1)
                    free(st["latent"], k, lambda: A(lat[:, 1, :], bank[2 * s + 1], ACT.Copy))

            def rotary(i, s, k, ahead):
                ahead()
                for t in range(2):
                    arrived(st["ret_qk"], k, t)
                    if k:
                        act.wait_ge(sem["rp_done"], 2 * (k - 1) + t + 1)
                    for b in range(4):
                        last = A(swapped[t][32 * b:32 * b + 32, :], bank[2 * s + t][32 * (b ^ 1):32 * (b ^ 1) + 32, :], ACT.Copy)
                    last.then_inc(sem["sw_done"], 1)

            def ret_gate(i, s, k, ahead):
                ahead()
                arrived(st["ret_gate"], k, 0)
                A(rgate[:, 2 * k, :], bank[2 * s], ACT.Silu)
                arrived(st["ret_gate"], k, 1)
                free(st["ret_gate"], k, lambda: A(rgate[:, 2 * k + 1, :], bank[2 * s + 1], ACT.Silu))

            run(st["latent"], latent)
            act.wait_ge(sem["lat_done"], 2)
            act.wait_ge(sem["group_free"], st["latent"].g0 + 1)
            squares("c_q", lambda c: lat[:, c, :], lambda c: None)
            squares("c_kv", lambda c: lat[:, 2, :], lambda c: None)
            run(st["ret_qk"], rotary)
            norm_rstd("c_q", 2 * P)
            for c in range(2):
                made(MADE["lat"] + c, lat_hi[:, c, :])
            norm_rstd("c_kv", P)
            made(MADE["lat"] + 2, lat_hi[:, 2, :])
            run(st["ret_val"], rows_of(st["ret_val"], rv_rows))
            run(st["ret_gate"], ret_gate)

            nc.scalar.preload_act_table_set("natural_log_exp_and_others")
            act.wait_ge(sem["rp_done"], 2 * PAIRS)
            act.wait_ge(sem["group_free"], st["up_v"].g0)
            act.wait_ge(sem["in_lag"], 16)
            with act.Fori(0, PAIRS) as i:
                stage_pair(i, rqk, rqk, rv_rows)
                for s in range(2):
                    A(decay[s][:, :], lag[:, :], ACT.Exp, scale=scol("log_gamma", 2 * i + s)).then_inc(sem["dec_done"], 1)
                for s in range(2):
                    act.wait_ge(sem["rp_f"], 2 * i + s + 1)
                    A(r_hi[s][:, :], rp[s][:, :], ACT.Copy).then_inc(sem["rp_hi"], 1)
                act.wait_ge(sem["ro_done"], 2 * i + 2)
                apart()
                for s in range(2):
                    rows = slice(HD * s, HD * s + HD)
                    A(chunk(rqk, i, rows), o2[s][rows, :], ACT.Copy).then_inc(sem["ro_evac"], 1)
            run(st["up_v"], rows_of(st["up_v"], mv_rows))
            for k in range(PAIRS):
                m = MADE["gn"] + k
                act.wait_ge(sem["gn_xc"], k + 1)
                A(sq[k % 2][:, :], rqk[:, k, :], ACT.Square).then_inc(sem["gn_sq"], 1)
                if k:
                    act.wait_ge(sem["tn_done"], m)
                rstd(1.0, lambda: act.wait_ge(sem["gn_var"], k + 1))
                act.wait_ge(sem["gn_y"], k + 1)
                A(h_hi[:, k, :], h_f[m % 2][:, :], ACT.Copy).then_inc(sem["made_hi"], 1)

            def keys(i, s, k, ahead):
                ahead()
                for t in range(2):
                    arrived(st["up_k"], k, t)
                    A(mk[0:HD, 2 * (2 * k + t), :], bank[2 * s + t][0:HD, :], ACT.Copy)
                    last = lambda: A(mk[0:HD, 2 * (2 * k + t) + 1, :], bank[2 * s + t][HD:P, :], ACT.Copy)
                    if t == 0:
                        last()
                    else:
                        free(st["up_k"], k, last)

            def queries(i, s, k, ahead):
                ahead()
                for t in range(2):
                    arrived(st["up_q"], k, t)
                    A(mq[0:HD, 2 * k + t, :], bank[2 * s + t][0:HD, :], ACT.Copy).then_inc(sem["mq_done"], 1)

            run(st["up_k"], keys)
            run(st["up_q"], queries)
            act.wait_ge(sem["kpe_done"], 1)
            act.wait_ge(sem["group_free"], st["mix_out2"].g0)
            for s in range(2):
                A(m_hi[64:96, 2 + s, :], kpe[64:96, :], ACT.Copy).then_inc(sem["kst_hi"], 1)
            act.wait_ge(sem["qrope_done"], HEADS)
            nc.scalar.preload_act_table_set("natural_log_exp_and_others")
            with act.Fori(0, PAIRS) as i:
                for s in range(2):
                    A(m_hi[0:96, s, :], chunk(mq, 2 * i + s, slice(0, 96)), ACT.Copy
                      ).then_inc(sem["mstg_hi"], 1)
                for s in range(2):
                    A(m_hi[0:HD, 2 + s, :], chunk(mk, 2 * i + s, slice(0, HD)), ACT.Copy
                      ).then_inc(sem["mstg_hi"], 1)
                A(pair_v(m_hi[:, 4, :]), mv_rows[:, :, bass.ds(P * i, P)], ACT.Copy).then_inc(sem["mstg_hi"], 1)
                for s in range(2):
                    act.wait_ge(sem["nmx_done"], 2 * i + s + 1)
                    for t in range(QB):
                        a, w = ROW_AT[t], ROW_W[t]
                        last = A(mp[s][:, a:a + w], z2[s][:, a:a + w], ACT.Exp, scale=MLA_SCALE, bias=row_stat[:, s, 4 + t:5 + t],
                                 accum_out=row_stat[:, s, 8 + t:9 + t])
                    last.then_inc(sem["mp_done"], 1)
                for s in range(2):
                    act.wait_ge(sem["mt_done"], 2 * i + s + 1)
                    A(r_hi[s][:, :], z2[s][:, 0:ZW], ACT.Copy).then_inc(sem["mth"], 1)
                act.wait_ge(sem["mo_done"], 2 * i + 2)
                apart()
                for s in range(2):
                    rows = slice(HD * s, HD * s + HD)
                    A(chunk(mq, 2 * i, rows), o2[s][rows, :], ACT.Copy).then_inc(sem["mo_evac"], 1)
            act.wait_ge(sem["mo_evac"], HEADS)
            for c in range(4):
                A(h_hi[:, 4 + c, :], mq[:, 2 * c, :], ACT.Copy).then_inc(sem["mos_hi"], 1)
            run(st["mix_out2"], lambda i, s, k, ahead: ahead())
            squares("ffn2", lambda c: x[:, c, :], lambda c: act.wait_ge(sem["group_free"], st["mix_out2"].g0 + c // 2 + 1))
            norm_rstd("ffn2", D)
            for c in range(DC):
                made(MADE["ffn2"] + c, h_hi[:, c, :])

            def conv_gated(stage, part):
                def evac(i, s, k, ahead):
                    c0 = PART_AT[part] + k
                    chan = c0
                    ahead()
                    act.wait_ge(sem["mid_f"], DC + c0 - 1)
                    for t, buf in ((0, act_a[s]), (1, act_b[s])):
                        arrived(stage, k, t)
                        A(buf[:, :], bank[2 * s + t], ACT.Identity, scale=col("conv_w_2", 2 * 2 * FC + t * FC + chan),
                          bias=col("conv_b_2", t * FC + chan)).then_inc(sem["ident_done"], 1)
                    act.wait_ge(sem["silu_arg"], c0 + 1)
                    A(act_a[s][:, :], act_a[s][:, :], ACT.Silu).then_inc(sem["mid_silu"], 1)
                    act.wait_ge(sem["mid_f"], DC + c0 + 1)
                    A(chunk(mid_hi, k), act_p[s][:, :], ACT.Copy
                      ).then_inc(sem["mid_hi_done"], 1)
                return evac

            for r in range(3):
                run(st[f"up{r}"], conv_gated(st[f"up{r}"], r))
                run(st[f"down{r}"], lambda i, s, k, ahead: ahead())
            squares("final", lambda c: x[:, c, :], lambda c: act.wait_ge(sem["group_free"], st["down2"].g0 + c // 2 + 1))
            norm_rstd("final", D)

        @block.vector
        def _(dve):
            tt, ts, stt = nc.vector.tensor_tensor, nc.vector.tensor_scalar, nc.vector.scalar_tensor_tensor
            taps = [0]

            def less(out_lo, full, high):
                return tt(out_lo, full, high.bitcast(F32), ALU.subtract)

            def split_lo(stage, k, slot):
                dve.wait_ge(sem["w_hi_done"], stage.g0 + k + 1)
                less(w_lo[slot][:, 0:stage.kc, :], raw[slot][:, 0:stage.kc, :], w_hi[slot][:, 0:stage.kc, :]
                     ).then_inc(sem["w_lo_done"], 1)

            def run(stage, evac):
                def step(i, s, final=False):
                    def ahead():
                        if not (final and s):
                            split_lo(stage, 2 * i + s + 1, 1 - s)
                        elif stage.next:
                            split_lo(stage.next, 0, 0)
                    evac(i, s, 2 * i + s, ahead)
                n = stage.n // 2
                if n == 2:
                    step(0, 0)
                    step(0, 1)
                elif n > 2:
                    with dve.Fori(0, n - 1) as i:
                        step(i, 0)
                        step(i, 1)
                step(n - 1, 0, True)
                step(n - 1, 1, True)

            def arrived(stage, k, t):
                dve.wait_ge(sem["tile_done"], 2 * (stage.g0 + k) + t + 1)

            def free(stage, k, ins_of):
                if positive(stage.g0 + k):
                    dve.wait_ge(sem["group_free"], stage.g0 + k)
                ins_of().then_inc(sem["group_free"], 1)

            def freed(stage, k):
                dve.wait_ge(sem["group_free"], stage.g0 + k + 1)

            def normalised(m, src, g):
                stt(t_n[m % 2][:, :], src, g, rs[:, :], ALU.mult, ALU.mult).then_inc(sem["tn_done"], 1)

            def made(m0, n, src, g, dst_hi, dst_lo, shifted, between=None):
                for c in range(n + 1):
                    if c < n:
                        if c >= 2:
                            dve.wait_ge(sem["made_lo"], m0 + c - 1)
                        normalised(m0 + c, src(c), g(c))
                    if c:
                        m = m0 + c - 1
                        dve.wait_ge(sem["made_hi"], m + 1)
                        less(dst_lo[:, c - 1, :], (h_f if shifted else t_n)[m % 2][:, :], dst_hi[:, c - 1, :]
                             ).then_inc(sem["made_lo"], 1)
                    if c == 2 and between:
                        between()

            dve.wait_ge(sem["c_act"], 1)
            for b in range(4):
                dve.wait_ge(sem[f"ada_f{b}"], 16)
                for k in range(8):
                    part, acc = ada_first[:, 4 * b:4 * b + 4, k, :], ada_acc0[:, b]
                    if k == 0:
                        last = ts(acc, part, c_act[:, 0:1], None, ALU.mult)
                    else:
                        dve.wait_ge(sem["ada0_step"], 7 * b + k)
                        last = stt(acc, part, c_act[:, k:k + 1], acc, ALU.mult, ALU.add)
                    last.then_inc(sem["ada0_step" if k < 7 else "ada0_sum"], 1)
            dve.wait_ge(sem["mod0_cols"], 4)
            tt(mod[:, 0:ADA_FIRST], mod_ps[:, 0:ADA_FIRST], col("ada_b", 0, ADA_FIRST), ALU.add).then_inc(sem["mod0_done"], 1)
            nc.vector.memset(u[:, :, 0:PAD], 0.0).then_inc(sem["gain_step"], 1)
            dve.wait_ge(sem["mod0_done"], 1)
            stt(gain[:, 0, :], mod[:, DC:2 * DC], 1.0, col("pre_mix_g", 0, DC), ALU.add, ALU.mult).then_inc(sem["gain_done"], 1)
            dve.wait_ge(sem["gain_done"], 1)
            dve.wait_ge(sem["rs_done"], 1)
            made(MADE["pre_mix"], DC, lambda c: x[:, c, :], lambda c: gain[:, 0, c:c + 1], h_hi, h_lo, True,
                 between=lambda: split_lo(st["glu"], 0, 0))

            def glu(i, s, k, ahead):
                ahead()
                dve.wait_ge(sem["sig_done"], k + 1)
                arrived(st["glu"], k, 0)
                free(st["glu"], k, lambda: tt(u[:, k, PAD:PAD + S], glu_sig[s][:, :], bank[2 * s], ALU.mult))

            def conv_start(c, acc):
                if taps[0]:
                    dve.wait_ge(sem["tap"], taps[0])
                ts(acc[:, :], u[:, c, 0:S], col("conv_w", c * TAPS), col("conv_b", c), ALU.mult, ALU.add).then_inc(sem["tap"], 1)
                taps[0] += 1

            def conv_tap(c, j, acc, dst, before):
                dve.wait_ge(sem["tap"], before)
                stt(dst, u[:, c, bass.ds(j, S)], col("conv_w", c * TAPS + j), acc[:, :], ALU.mult, ALU.add).then_inc(sem["tap"], 1)

            def conv_half(c, half):
                if half == 0:
                    conv_start(c, conv_tmp)
                for j in range(half * TAPS // 2, (half + 1) * TAPS // 2):
                    conv_tap(c, j, conv_tmp, u[:, c, PAD:PAD + S] if j == TAPS - 1 else conv_tmp[:, :], taps[0])
                    taps[0] += 1

            def conv_beside(c0):
                def evac(i, s, k, ahead):
                    ahead()
                    conv_half(c0 + i, s)
                return evac

            run(st["glu"], glu)
            dve.wait_ge(sem["gain_step"], 1)
            dve.wait_ge(sem["group_free"], st["qk"].g0)
            run(st["qk"], conv_beside(0))
            run(st["val"], conv_beside(2))

            def stage_pair(i, base, q, k, v):
                dve.wait_ge(sem["stg_hi"], base + 3 * i + 1)
                stt(stage_lo[:, 0, :], chunk(q, i), HD ** -0.5, stage_hi[:, 0, :].bitcast(F32), ALU.mult, ALU.subtract
                    ).then_inc(sem["stg_lo"], 1)
                dve.wait_ge(sem["stg_hi"], base + 3 * i + 2)
                less(stage_lo[:, 1, :], chunk(k, PAIRS + i), stage_hi[:, 1, :]).then_inc(sem["stg_lo"], 1)
                dve.wait_ge(sem["stg_hi"], base + 3 * i + 3)
                less(pair_v(stage_lo[:, 2, :]), v[:, :, bass.ds(P * i, P)], pair_v(stage_hi[:, 2, :])).then_inc(sem["stg_lo"], 1)

            conv_start(3, conv3)

            def head(i, s, n, ahead):
                def some_taps(r0):
                    for r in range(r0, r0 + 2):
                        conv_tap(3, 4 * n + r, conv3, conv3[:, :], taps[0] + 4 * n + r)
                if s == 0:
                    stage_pair(i, 0, qkT, qkT, v_rows)
                dve.wait_ge(sem["z_done"], n + 1)
                for a, b in HALVES:
                    ts(zbuf[:, a:b], z[:, a:b], 40.0, None, ALU.min).then_inc(sem["zm_done"], 1)
                some_taps(0)
                for j, (a, b) in enumerate(HALVES):
                    dve.wait_ge(sem["l_done"], 2 * n + j + 1)
                    tt(zbuf[:, a:b], z[:, a:b], zbuf[:, a:b], ALU.max).then_inc(sem["sp_done"], 1)
                for j, (a, b) in enumerate(HALVES):
                    dve.wait_ge(sem["sph_done"], 2 * n + j + 1)
                    less(t_lo[:, a:b], zbuf[:, a:b], t_hi[:, a:b]).then_inc(sem["spl_done"], 1)
                some_taps(2)
                ahead()
                dve.wait_ge(sem["ah_done"], n + 1)
                less(t_lo[:, :], zbuf[:, :], t_hi[:, :]).then_inc(sem["al_done"], 1)

            run(st["gate"], head)
            for c in range(PAIRS):
                dve.wait_ge(sem["osp_hi"], c + 1)
                less(h_lo[:, 4 + c, :], qkT[:, c, :], h_hi[:, 4 + c, :]).then_inc(sem["osp_lo"], 1)

            def gate_att(i, s, k, ahead):
                ahead()
                dve.wait_ge(sem["gate_sig"], 1)
                arrived(st["att_out"], k, 0)
                tt(gates[:, DC + 2 * k, :], gates[:, DC + 2 * k, :], bank[2 * s], ALU.mult)
                arrived(st["att_out"], k, 1)
                free(st["att_out"], k, lambda: tt(gates[:, DC + 2 * k + 1, :], gates[:, DC + 2 * k + 1, :], bank[2 * s + 1], ALU.mult))

            run(st["att_out"], gate_att)
            def convolved(c):
                return u[:, c, PAD:PAD + S] if c < 3 else conv3[:, :]

            dve.wait_ge(sem["mean_done"], 1)
            for c in range(4):
                tt(convolved(c), convolved(c), mean[:, :], ALU.subtract).then_inc(sem["xc_done"], 1)
            dve.wait_ge(sem["mod_cols"], ADA_REST)
            tt(mod[:, 2 * DC:], mod_ps[:, 2 * DC:], col("ada_b", 2 * DC, 4 * DC), ALU.add).then_inc(sem["mod_done"], 1)
            dve.wait_ge(sem["mod_done"], 1)
            tt(gain[:, 1, :], mod[:, 2 * DC:3 * DC], col("post_mix_g", 0, DC), ALU.mult).then_inc(sem["gain_done"], 1)
            stt(gain[:, 2, :], mod[:, 4 * DC:5 * DC], 1.0, col("pre_ffn_g", 0, DC), ALU.add, ALU.mult).then_inc(sem["gain_done"], 1)
            tt(gain[:, 3, :], mod[:, 5 * DC:6 * DC], col("post_ffn_g", 0, DC), ALU.mult).then_inc(sem["gain_done"], 1)
            dve.wait_ge(sem["xc_done"], 4)
            dve.wait_ge(sem["rs_done"], 2)
            made(MADE["conv"], 4, convolved, lambda c: col("conv_ln_g", c), h_hi, h_lo, True)

            def merged(i, s, k, ahead):
                ahead()
                dve.wait_ge(sem["gate_sig"], 2)
                for t in range(2):
                    n = 2 * k + t
                    arrived(st["conv_out"], k, t)
                    gate = lambda: tt(gates[:, n, :], gates[:, n, :], bank[2 * s + t], ALU.mult)
                    if t == 0:
                        gate().then_inc(sem["merge_m"], 1)
                        dve.wait_ge(sem["merge_m"], k + 1)
                    else:
                        free(st["conv_out"], k, gate)
                        freed(st["conv_out"], k)
                    tt(gates[:, n, :], gates[:, n, :], gates[:, DC + n, :], ALU.add).then_inc(sem["mid_f"], 1)
                for t in range(2):
                    n = 2 * k + t
                    dve.wait_ge(sem["mid_hi_done"], n + 1)
                    less(mid_lo[:, n, :], gates[:, n, :], mid_hi[:, n, :]).then_inc(sem["mid_lo_done"], 1)

            def add_normed(base, done, g):
                for c in range(DC + 1):
                    if c < DC:
                        if c >= 2:
                            dve.wait_ge(sem["x_done"], base + c - 1)
                        stt(t_n[c % 2][:, :], y[:, c, :], gain[:, g, c:c + 1], rs[:, :], ALU.mult, ALU.mult).then_inc(sem["upd_step"], 1)
                    if c:
                        dve.wait_ge(sem["upd_step"], base + c)
                        tt(x[:, c - 1, :], x[:, c - 1, :], t_n[(c - 1) % 2][:, :], ALU.add).then_inc(sem["x_done"], 1)

            run(st["conv_out"], merged)
            run(st["mix_out"], lambda i, s, k, ahead: ahead())
            dve.wait_ge(sem["gain_done"], 4)
            dve.wait_ge(sem["rs_done"], 3)
            add_normed(0, 0, 1)
            dve.wait_ge(sem["x_done"], DC)
            dve.wait_ge(sem["rs_done"], 4)
            made(MADE["pre_ffn"], DC, lambda c: x[:, c, :], lambda c: gain[:, 2, c:c + 1], h_hi, h_lo, True)

            def mid_low(m, k, s):
                dve.wait_ge(sem["mid_hi_done"], m + 1)
                less(chunk(mid_lo, k), act_p[s][:, :], chunk(mid_hi, k)).then_inc(sem["mid_lo_done"], 1)

            def gated(stage, part):
                def evac(i, s, k, ahead):
                    ahead()
                    dve.wait_ge(sem["mid_silu"], PART_AT[part] + k + 1)
                    arrived(stage, k, 1)
                    free(stage, k, lambda: tt(act_p[s][:, :], act_a[s][:, :], bank[2 * s + 1], ALU.mult))
                    mid_low(DC + PART_AT[part] + k, k, s)
                return evac

            def add_to(dst, stage):
                def evac(i, s, k, ahead):
                    ahead()
                    arrived(stage, k, 0)
                    tt(dst[:, 2 * k, :], dst[:, 2 * k, :], bank[2 * s], ALU.add)
                    arrived(stage, k, 1)
                    free(stage, k, lambda: tt(dst[:, 2 * k + 1, :], dst[:, 2 * k + 1, :], bank[2 * s + 1], ALU.add))
                return evac

            for r in range(3):
                run(st[f"ffn_in{r}"], gated(st[f"ffn_in{r}"], r))
                run(st[f"ffn_out{r}"], add_to(y, st[f"ffn_out{r}"]) if r else (lambda i, s, k, ahead: ahead()))
            dve.wait_ge(sem["rs_done"], 5)
            add_normed(DC, DC, 3)
            dve.wait_ge(sem["x_done"], 2 * DC)
            dve.wait_ge(sem["rs_done"], 6)
            made(MADE["attn2"], DC, lambda c: x[:, c, :], lambda c: col("attn_norm_w_2", c), h_hi, h_lo, False)

            def latent(i, s, k, ahead):
                ahead()
                if k:
                    arrived(st["latent"], 1, 1)
                    dve.wait_ge(sem["trig"], 4)
                    tt(rope_t[0][64:96, :], bank[2 * s + 1][64:96, :], cos_mla[64:96, :], ALU.mult).then_inc(sem["rope_m"], 1)
                    dve.wait_ge(sem["lat_done"], 2)
                    free(st["latent"], 1, lambda: tt(rope_t[1][64:96, :], bank[2 * s + 1][96:128, :], sin_mla[96:128, :], ALU.mult))
                    freed(st["latent"], 1)
                    dve.wait_ge(sem["rope_m"], 1)
                    tt(kpe[64:96, :], rope_t[0][64:96, :], rope_t[1][64:96, :], ALU.add).then_inc(sem["kpe_done"], 1)

            def rotary(i, s, k, ahead):
                ahead()
                for t in range(2):
                    n = 2 * k + t
                    if n >= 2:
                        dve.wait_ge(sem["rp_done"], n - 1)
                    elif n == 0:
                        dve.wait_ge(sem["kpe_done"], 1)
                    dve.wait_ge(sem["sw_done"], n + 1)
                    turn = lambda: tt(rope_t[t][:, :], bank[2 * s + t], cos_ret[:, :], ALU.mult)
                    if t == 0:
                        turn().then_inc(sem["rope_m"], 1)
                    else:
                        free(st["ret_qk"], k, turn)
                    tt(swapped[t][:, :], swapped[t][:, :], sin_ret[:, :], ALU.mult).then_inc(sem["rope_s"], 1)
                    if t == 0:
                        dve.wait_ge(sem["rope_m"], 1 + k + 1)
                    else:
                        freed(st["ret_qk"], k)
                    dve.wait_ge(sem["rope_s"], n + 1)
                    tt(rqk[:, n, :], rope_t[t][:, :], swapped[t][:, :], ALU.add).then_inc(sem["rp_done"], 1)

            only_ahead = lambda i, s, k, ahead: ahead()
            run(st["latent"], latent)
            run(st["ret_qk"], rotary)
            dve.wait_ge(sem["rs_done"], 7)
            made(MADE["lat"], 2, lambda c: lat[:, c, :], lambda c: col("mla_q_norm_w_2", c), lat_hi, lat_lo, False)
            dve.wait_ge(sem["rs_done"], 8)
            dve.wait_ge(sem["made_lo"], MADE["lat"] + 1)
            made(MADE["lat"] + 2, 1, lambda c: lat[:, 2, :], lambda c: col("mla_kv_norm_w_2"), lat_hi[:, 2:3], lat_lo[:, 2:3], False)
            run(st["ret_val"], only_ahead)
            run(st["ret_gate"], only_ahead)

            dve.wait_ge(sem["rp_done"], 2 * PAIRS)
            with dve.Fori(0, PAIRS) as i:
                stage_pair(i, 3 * PAIRS, rqk, rqk, rv_rows)
                for s in range(2):
                    n = 2 * i + s
                    dve.wait_ge(sem["dec_done"], n + 1)
                    dve.wait_ge(sem["rz_done"], n + 1)
                    for kb in range(QB):
                        a, w = BLOCK_AT[kb], BLOCK_W[kb]
                        last = tt(rp[s][:, a:a + w], z2[s][:, a:a + w], decay[s][:, 0:w], ALU.mult)
                    last.then_inc(sem["rp_f"], 1)
                for s in range(2):
                    dve.wait_ge(sem["rp_hi"], 2 * i + s + 1)
                    less(r_lo[s][:, :], rp[s][:, :], r_hi[s][:, :]).then_inc(sem["rp_lo"], 1)
            run(st["up_v"], only_ahead)
            dve.wait_ge(sem["ro_evac"], HEADS)
            for k in range(PAIRS):
                m = MADE["gn"] + k
                dve.wait_ge(sem["gn_mean"], k + 1)
                tt(rqk[:, k, :], rqk[:, k, :], o_ps, ALU.subtract).then_inc(sem["gn_xc"], 1)
                dve.wait_ge(sem["gn_xc"], k + 1)
                dve.wait_ge(sem["rs_done"], 8 + k + 1)
                normalised(m, rqk[:, k, :], col("ret_gn_w_2", k))
                dve.wait_ge(sem["tn_done"], m + 1)
                tt(h_f[m % 2][:, :], t_n[m % 2][:, :], rgate[:, k, :], ALU.mult).then_inc(sem["gn_y"], 1)
                dve.wait_ge(sem["made_hi"], m + 1)
                less(h_lo[:, k, :], h_f[m % 2][:, :], h_hi[:, k, :]).then_inc(sem["made_lo"], 1)

            def queries(i, s, k, ahead):
                ahead()
                for t in range(2):
                    h = 2 * k + t
                    dve.wait_ge(sem["mq_done"], h + 1)
                    if h:
                        dve.wait_ge(sem["qrope_done"], h)
                    tt(rope_t[0][64:96, :], bank[2 * s + t][64:96, :], cos_mla[64:96, :], ALU.mult).then_inc(sem["rope_m"], 1)
                    turn = lambda: tt(rope_t[1][64:96, :], bank[2 * s + t][96:128, :], sin_mla[96:128, :], ALU.mult)
                    if t == 0:
                        turn().then_inc(sem["rope_s"], 1)
                        dve.wait_ge(sem["rope_s"], 2 * PAIRS + k + 1)
                    else:
                        free(st["up_q"], k, turn)
                        freed(st["up_q"], k)
                    dve.wait_ge(sem["rope_m"], 1 + PAIRS + h + 1)
                    tt(mq[64:96, h, :], rope_t[0][64:96, :], rope_t[1][64:96, :], ALU.add).then_inc(sem["qrope_done"], 1)

            run(st["up_k"], only_ahead)
            run(st["up_q"], queries)
            for s in range(2):
                dve.wait_ge(sem["kst_hi"], s + 1)
                less(m_lo[64:96, 2 + s, :], kpe[64:96, :], m_hi[64:96, 2 + s, :]).then_inc(sem["kst_lo"], 1)
            dve.wait_ge(sem["qrope_done"], HEADS)
            with dve.Fori(0, PAIRS) as i:
                for s in range(2):
                    dve.wait_ge(sem["mstg_hi"], 5 * i + s + 1)
                    less(m_lo[0:96, s, :], chunk(mq, 2 * i + s, slice(0, 96)), m_hi[0:96, s, :]).then_inc(sem["mstg_lo"], 1)
                for s in range(2):
                    dve.wait_ge(sem["mstg_hi"], 5 * i + 2 + s + 1)
                    less(m_lo[0:HD, 2 + s, :], chunk(mk, 2 * i + s, slice(0, HD)), m_hi[0:HD, 2 + s, :]).then_inc(sem["mstg_lo"], 1)
                dve.wait_ge(sem["mstg_hi"], 5 * i + 5)
                less(pair_v(m_lo[:, 4, :]), mv_rows[:, :, bass.ds(P * i, P)], pair_v(m_hi[:, 4, :])).then_inc(sem["mstg_lo"], 1)
                for s in range(2):
                    n = 2 * i + s
                    dve.wait_ge(sem["mz_done"], n + 1)
                    for t in range(QB):
                        a, w = ROW_AT[t], ROW_W[t]
                        last = nc.vector.reduce_max(row_stat[:, s, t:t + 1], z2[s][:, a:a + w], AX.X)
                    last.then_inc(sem["mx_done"], 1)
                    dve.wait_ge(sem["mx_done"], n + 1)
                    ts(row_stat[:, s, 4:8], row_stat[:, s, 0:4], -MLA_SCALE, None, ALU.mult).then_inc(sem["nmx_done"], 1)
                for s in range(2):
                    n = 2 * i + s
                    dve.wait_ge(sem["mp_done"], n + 1)
                    nc.vector.reciprocal(row_stat[:, s, 12:16], row_stat[:, s, 8:12]).then_inc(sem["rcp_done"], 1)
                    dve.wait_ge(sem["rcp_done"], n + 1)
                    for t in range(QB):
                        a, w = ROW_AT[t], ROW_W[t]
                        last = ts(mp[s][:, a:a + w], mp[s][:, a:a + w], row_stat[:, s, 12 + t:13 + t], None, ALU.mult)
                    last.then_inc(sem["pn_done"], 1)
                for s in range(2):
                    dve.wait_ge(sem["mth"], 2 * i + s + 1)
                    less(mt_lo[s][:, :], z2[s][:, 0:ZW], r_hi[s][:, :]).then_inc(sem["mtl"], 1)
            for c in range(PAIRS):
                dve.wait_ge(sem["mos_hi"], c + 1)
                less(h_lo[:, 4 + c, :], mq[:, 2 * c, :], h_hi[:, 4 + c, :]).then_inc(sem["mos_lo"], 1)
            run(st["mix_out2"], add_to(x, st["mix_out2"]))
            freed(st["mix_out2"], 3)
            dve.wait_ge(sem["rs_done"], 13)
            made(MADE["ffn2"], DC, lambda c: x[:, c, :], lambda c: col("ffn_norm_w_2", c), h_hi, h_lo, False)

            def conv_gated(stage, part):
                def evac(i, s, k, ahead):
                    c0 = PART_AT[part] + k
                    ahead()
                    for t, buf in ((0, act_a[s]), (1, act_b[s])):
                        tap = lambda back: stt(buf[:, back:], bank[2 * s + t][:, 0:S - back],
                                               col("conv_w_2", ((2 - back) * 2 + t) * FC + c0), buf[:, back:], ALU.mult, ALU.add)
                        dve.wait_ge(sem["ident_done"], 2 * c0 + t + 1)
                        tap(1).then_inc(sem["conv2"], 1)
                        dve.wait_ge(sem["conv2"], 2 * c0 + t + 1)
                        if t == 0:
                            tap(2).then_inc(sem["silu_arg"], 1)
                        else:
                            free(stage, k, lambda: tap(2))
                    freed(stage, k)
                    dve.wait_ge(sem["mid_silu"], FC + c0 + 1)
                    tt(act_p[s][:, :], act_a[s][:, :], act_b[s][:, :], ALU.mult).then_inc(sem["mid_f"], 1)
                    mid_low(DC + FC + c0, k, s)
                return evac

            for r in range(3):
                run(st[f"up{r}"], conv_gated(st[f"up{r}"], r))
                run(st[f"down{r}"], add_to(x, st[f"down{r}"]))
            freed(st["down2"], 3)
            dve.wait_ge(sem["rs_done"], 14)
            for k in range(DC):
                stt(y[:, k, :], x[:, k, :], col("final_norm_w_2", k), rs[:, :], ALU.mult, ALU.mult).then_inc(sem["fin_done"], 1)

        @block.gpsimd
        def _(pool):
            tt, ts = nc.gpsimd.tensor_tensor, nc.gpsimd.tensor_scalar

            def sums(name):
                e, q0, n = NORMS[name]
                for q in range(q0, q0 + n):
                    pool.wait_ge(sem["sq_done"], q + 1)
                    if q == q0:
                        if e:
                            pool.wait_ge(sem["stat_done"], e)
                        last = nc.gpsimd.tensor_copy(sq_sum[:, :], sq[q % 2][:, :])
                    else:
                        pool.wait_ge(sem["sum_done"], q)
                        last = tt(sq_sum[:, :], sq_sum[:, :], sq[q % 2][:, :], ALU.add)
                    last.then_inc(sem["sum_done"], 1)

            def ada_tile(a, slot, half):
                r = ada_raw[slot]
                pool.wait_ge(ada_full[slot], 16 * (half + 1))
                tt(r[:, :, :], r[:, :, :], c_act[:, :].unsqueeze(2).to_broadcast([P, 8, P]), ALU.mult).then_inc(sem["ada_step"], 1)
                for k, n in enumerate((4, 2, 1)):
                    pool.wait_ge(sem["ada_step"], 3 * a + k + 1)
                    if n > 1:
                        tt(r[:, 0:n], r[:, 0:n], r[:, n:2 * n], ALU.add).then_inc(sem["ada_step"], 1)
                if positive(a - 1):
                    pool.wait_ge(sem["mod_cols"], a - 1)
                tt(ada_acc[slot][:, :], r[:, 0, :], r[:, 1, :], ALU.add).then_inc(sem["ada_sum"], 1)

            sums("pre_mix")
            pool.wait_ge(sem["c_act"], 1)
            ada_tile(0, 0, 0)
            ada_tile(1, 1, 0)
            with pool.Fori(1, ADA_REST // 2) as i:
                ada_tile(2 * i, 0, i)
                ada_tile(2 * i + 1, 1, i)
            for name in ["conv_ln", "post_mix", "pre_ffn"]:
                sums(name)

            steps = [0]

            def step(ins):
                ins.then_inc(sem["ang_step"], 1)
                steps[0] += 1
                pool.wait_ge(sem["ang_step"], steps[0])

            pool.wait_ge(sem["in_pos"], 16)
            step(nc.gpsimd.tensor_copy(pos_f[:, :], pos_i[:, :]))
            for kind, sin_t, cos_t in (("ret", sin_ret, cos_ret), ("mla", sin_mla, cos_mla)):
                step(ts(angle[:, :], pos_f[:, :], scol("freq_" + kind), None, ALU.mult))
                step(ts(turns[:, :], angle[:, :], 1 / (2 * np.pi), MAGIC, ALU.mult, ALU.add))
                step(ts(turns[:, :], turns[:, :], MAGIC, None, ALU.subtract))
                for part in TWO_PI:
                    step(ts(sin_t[:, :], turns[:, :], part, None, ALU.mult))
                    step(tt(angle[:, :], angle[:, :], sin_t[:, :], ALU.subtract))
                step(ts(angle[:, :], angle[:, :], PI, -PI, ALU.min, ALU.max))
                ts(sin_t[:, :], angle[:, :], scol("sign_" + kind), None, ALU.mult).then_inc(sem["ang_arg"], 1)
                step(ts(turns[:, :], angle[:, :], 0.0, None, ALU.max))
                step(ts(angle[:, :], angle[:, :], 0.0, None, ALU.min))
                step(tt(turns[:, :], turns[:, :], angle[:, :], ALU.subtract))
                ts(cos_t[:, :], turns[:, :], -1.0, float(np.float32(np.pi / 2)), ALU.mult, ALU.add).then_inc(sem["ang_arg"], 1)

            for name in ["post_ffn", "attn2", "c_q", "c_kv", "ffn2", "final"]:
                sums(name)


def packed(vectors):
    return np.ascontiguousarray(np.concatenate([v.reshape(-1, P).T for v in vectors], axis=1))


def shape_constants():
    p, f = np.arange(P)[:, None], np.arange(P)[None, :]
    mats = {"ident": p == f, "tri": -1.0 * (p >= f), "ones_neg": -np.ones((P, P)), "mask_kq": NEG * (p >= f),
            "mask_qk": NEG * (f > p), "ones": np.ones((P, P)), "block_mean": (p // HD == f // HD) / HD}
    j = np.arange(P)
    small = np.zeros((P, N_SMALL), np.float32)
    small[:, SMALL["eps"]] = EPS
    small[:, SMALL["freq_ret"]] = 10000.0 ** (-2.0 * (j % 32) / 64)
    small[:, SMALL["sign_ret"]] = np.where(j % 64 < 32, -1, 1)
    small[:, SMALL["freq_mla"]] = 10000.0 ** (-2.0 * (j % 16) / 32)
    small[:, SMALL["sign_mla"]] = np.where(j % 32 < 16, -1, 1)
    small[:, SMALL["log_gamma"]:SMALL["log_gamma"] + HEADS] = np.log1p(-2.0 ** (-5.0 - np.arange(HEADS)))
    lag = np.where(np.arange(S)[None, :] >= p, np.arange(S)[None, :] - p, 1e9)
    return np.stack([mats[n] for n in MATS], axis=1).astype(np.float32), small, lag.astype(np.float32)


def grouped(w, groups):
    rows, cols = w.shape
    return np.ascontiguousarray(w.reshape(rows // P, P, groups, 256).transpose(2, 1, 0, 3).reshape(groups, P, -1))


def stage_weights(a):
    def halves(w, width, first, n):
        return np.concatenate([w[:, half * width + P * c:half * width + P * c + P] for c in range(first, first + n) for half in range(2)], axis=1)

    w_in, w_in2 = a["w_in"][0], a["w_in_2"][0]
    w_uq = a["w_uq_2"][0].reshape(-1, HEADS, 96)
    w_ukv = a["w_ukv_2"][0].reshape(-1, HEADS, P)
    rope = w_in2[:, 2432:2464]
    out = {"glu": halves(w_in[:, 0:1024], 512, 0, 4), "qk": w_in[:, 1024:2048], "val": w_in[:, 2048:2560], "gate": w_in[:, 2560:],
           "att_out": a["w_att_out"][0], "conv_out": a["w_conv_out"][0], "mix_out": a["w_o"][0],
           "latent": np.concatenate([w_in2[:, 2048:2432], rope, rope, rope, rope[:, 16:], rope[:, :16]], axis=1),
           "ret_qk": w_in2[:, 0:1024], "ret_val": w_in2[:, 1024:1536], "ret_gate": w_in2[:, 1536:2048],
           "up_v": w_ukv[:, :, 64:].reshape(P, -1), "up_k": w_ukv[:, :, :64].reshape(P, -1),
           "up_q": np.concatenate([w_uq, w_uq[:, :, 80:96], w_uq[:, :, 64:80]], axis=2).reshape(256, -1), "mix_out2": a["w_out_2"][0]}
    for r, n in enumerate(FFN_PARTS):
        rows = slice(PART_AT[r] * P, (PART_AT[r] + n) * P)
        out[f"ffn_in{r}"] = halves(a["w_ffn_in"][0], FF, PART_AT[r], n)
        out[f"ffn_out{r}"] = a["w_ffn_out"][0][rows]
        out[f"up{r}"] = halves(a["w_up_2"][0], FF, PART_AT[r], n)
        out[f"down{r}"] = a["w_down_2"][0][rows]
    return {name: grouped(out[name], groups) for name, groups, _ in STAGES}


def kernel(**inputs):
    import concourse.bacc as bacc
    from concourse.bass_utils import run_bass_kernel_spmd

    a = {name: np.asarray(v) for name, v in inputs.items()}
    mats, small, lag = shape_constants()
    zero_tap = np.zeros((1, 4 * P), np.float32)
    vectors = dict(a, conv_w=np.concatenate([zero_tap, a["conv_w"][0]]).reshape(TAPS, 4, P).transpose(1, 0, 2))
    arrays = {"x": np.ascontiguousarray(a["x"][0].T.reshape(DC, P, S).transpose(1, 0, 2)),
              "ada": np.ascontiguousarray(a["ada_w"][0].reshape(DC, P, 6 * DC, P).transpose(2, 1, 0, 3)),
              "vec": packed([vectors[name] for name, _ in VECTORS]), "small": small, "mats": mats, "lag": lag,
              "positions": a["positions_2"].astype(np.int32, copy=False)}
    for name, w in stage_weights(a).items():
        arrays["w_" + name] = w
    nc = bacc.Bacc("TRN2", target_bir_lowering=False, num_devices=1)
    dram = {name: nc.dram_tensor(name, v.shape, mybir.dt.from_np(v.dtype), kind="ExternalInput").ap() for name, v in arrays.items()}
    out = nc.dram_tensor("out", (P, DC, S), F32, kind="ExternalOutput").ap()
    build(nc, dram, out)
    r = run_bass_kernel_spmd(nc, [arrays], core_ids=[0])
    got = np.asarray(r.results[0]["out"])
    return np.ascontiguousarray(got.transpose(1, 0, 2).reshape(1, D, S).transpose(0, 2, 1))
```

```python
from contextlib import ExitStack

import numpy as np
import concourse.bass as bass
from concourse import mybir

F32 = mybir.dt.float32
F32R = mybir.dt.float32r
I32 = mybir.dt.int32
ACT = mybir.ActivationFunctionType
ALU = mybir.AluOpType
AX = mybir.AxisListType

P = 128
S = 512
D = 1024
DC = D // P
FF = 2816
FC = FF // P
HEADS = 8
PAIRS = HEADS // 2
HD = 64
QB = S // P
EPS = 1e-6
MLA_SCALE = (64 + 32) ** -0.5
NEG = -1e30
TAPS = 32
PAD = TAPS - 1

STAGES = [
    ("glu", 4, 8), ("qk", 4, 8), ("val", 2, 8), ("gate", 8, 8),
    ("att_out", 4, 4), ("conv_out", 4, 4), ("mix_out", 4, 8),
    ("ffn_in0", 8, 8), ("ffn_out0", 4, 8), ("ffn_in1", 8, 8), ("ffn_out1", 4, 8), ("ffn_in2", 6, 8), ("ffn_out2", 4, 6),
    ("latent", 2, 8), ("ret_qk", 4, 8), ("ret_val", 2, 8), ("ret_gate", 2, 8),
    ("up_v", 2, 1), ("up_k", 2, 1), ("up_q", 4, 2), ("mix_out2", 4, 8),
    ("up0", 8, 8), ("down0", 4, 8), ("up1", 8, 8), ("down1", 4, 8), ("up2", 6, 8), ("down2", 4, 6),
]
FFN_PARTS = [8, 8, 6]
PART_AT = [0, 8, 16]
ADA_FIRST = 16
ADA_REST = 6 * DC - ADA_FIRST

VECTORS = [("c", DC), ("ada_b", 6 * DC), ("pre_mix_g", DC), ("post_mix_g", DC), ("pre_ffn_g", DC), ("post_ffn_g", DC),
           ("conv_w", 4 * TAPS), ("conv_b", 4), ("conv_ln_g", 4), ("conv_ln_b", 4),
           ("attn_norm_w_2", DC), ("ret_gn_w_2", PAIRS), ("mla_q_norm_w_2", 2), ("mla_kv_norm_w_2", 1),
           ("ffn_norm_w_2", DC), ("conv_w_2", 3 * 2 * FC), ("conv_b_2", 2 * FC), ("final_norm_w_2", DC)]
VEC, N_VEC = {}, 0
for _name, _n in VECTORS:
    VEC[_name] = N_VEC
    N_VEC += _n

MATS = ["ident", "tri", "ones_neg", "mask_kq", "mask_qk", "ones", "block_mean"]
SMALL = {"eps": 0, "freq_ret": 1, "sign_ret": 2, "freq_mla": 3, "sign_mla": 4, "log_gamma": 5}
N_SMALL = 16

BLOCK_AT = [0, 512, 1024, 896]
BLOCK_W = [S - kb * P for kb in range(QB)]
ZW = 1280
ROW_AT = [896, 1024, 512, 0]
ROW_W = [(t + 1) * P for t in range(QB)]
HALVES = [(0, 512), (512, ZW)]

NORMS = {}
_q = 0
for _e, (_name, _n) in enumerate([("pre_mix", 8), ("conv_ln", 4), ("post_mix", 8), ("pre_ffn", 8), ("post_ffn", 8),
                                  ("attn2", 8), ("c_q", 2), ("c_kv", 1), ("ffn2", 8), ("final", 8)]):
    NORMS[_name] = (_e, _q, _n)
    _q += _n
POOL_NORMS = ["pre_mix", "conv_ln", "post_mix", "post_ffn", "c_q", "c_kv", "ffn2", "final"]
MADE = {"pre_mix": 0, "conv": 8, "pre_ffn": 12, "attn2": 20, "lat": 28, "gn": 31, "ffn2": 35}

MAGIC = 1.5 * 2.0 ** 23
TWO_PI = [6.28125, float(np.float32(0.0019350051879882812)), 2 * np.pi - 6.28125 - float(np.float32(0.0019350051879882812))]
PI = float(np.nextafter(np.float32(np.pi), np.float32(0)))


class Stage:

    def __init__(self, name, groups, chunks, first):
        self.name, self.n, self.kc, self.g0, self.next = name, groups, chunks, first, None


def plan():
    out, g = {}, 0
    for name, n, kc in STAGES:
        out[name] = Stage(name, n, kc, g)
        g += n
    order = list(out.values())
    for a, b in zip(order, order[1:]):
        a.next = b
    return out


def positive(v):
    return not isinstance(v, int) or v > 0


def build(nc, dram, out):
    st = plan()
    off = [16512]

    def fixed(name, shape, dt=F32):
        size = int(np.prod(shape[1:])) * 4
        t = nc.alloc_sbuf_tensor_at(name, shape, dt, offset=off[0])
        off[0] += (size + 31) // 32 * 32
        return t

    x = fixed("x", [P, DC, S])
    h_hi, h_lo = (fixed(f"h_{p}", [P, DC, S], F32R) for p in ("hi", "lo"))
    raw = [fixed(f"raw{s}", [P, 8, 256]) for s in range(2)]
    w_hi = [fixed(f"w_hi{s}", [P, 8, 256], F32R) for s in range(2)]
    w_lo = [fixed(f"w_lo{s}", [P, 8, 256], F32R) for s in range(2)]
    vec, small = fixed("vec", [P, N_VEC]), fixed("small", [P, N_SMALL])
    mod, gain, c_act = fixed("mod", [P, 6 * DC]), fixed("gain", [P, 4, DC]), fixed("c_act", [P, DC])
    spare = fixed("spare", [P, 2])
    row_stat = fixed("row_stat", [P, 2, 16])
    rounded = fixed("rounded", [P, 5, P], F32R)
    ident, ones, block_mean = fixed("ident", [P, P]), fixed("ones", [P, P]), fixed("block_mean", [P, P])
    ident_r, tri_r, ones_neg_r, mask_kq_r, mask_qk_r = (rounded[:, k, :] for k in range(5))
    BASE = off[0]
    ROOM = 229344 - BASE

    def at(name, kb, shape, dt=F32):
        size = int(np.prod(shape[1:])) * 4
        assert kb * 1024 + size <= ROOM, (name, kb, size, ROOM)
        return nc.alloc_sbuf_tensor_at(name, shape, dt, offset=BASE + int(kb * 1024))

    ada_first = at("ada_first", 0, [P, ADA_FIRST, 8, P])
    ada_acc0 = at("ada_acc0", 64, [P, 4, 4, P])
    const_raw = at("const_raw", 96.5, [P, 5, P])
    qkT = at("qkT", 0, [P, 2 * PAIRS, S])
    v_rows = at("v_rows", 16, [P, QB, S])
    zbuf = at("zbuf", 24, [P, ZW])
    ada_acc = [at(f"ada_acc_{s}", 29 + s / 2, [P, P]) for s in range(2)]
    conv_tmp = at("conv_tmp", 30, [P, S])
    gates = at("gates", 32, [P, 2 * DC, S])
    u = at("u", 64, [P, 4, PAD + S])
    conv3 = at("conv3", 72.5, [P, S])
    stage_hi = at("stage_hi", 74.5, [P, 3, S], F32R)
    stage_lo = at("stage_lo", 80.5, [P, 3, S], F32R)
    t_hi, t_lo = at("t_hi", 86.5, [P, ZW], F32R), at("t_lo", 91.5, [P, ZW], F32R)
    ada_raw = [at(f"ada_raw{s}", 96.5 + 4 * s, [P, 8, P]) for s in range(2)]
    glu_sig = [at(f"glu_sig{s}", 92.5 + 2 * s, [P, S]) for s in range(2)]
    sq = [at(f"sq{s}", 74.5 + 2 * s, [P, S]) for s in range(2)]
    sq_sum = at("sq_sum", 78.5, [P, S])
    rs = at("rs", 80.5, [P, S])
    t_n = [at(f"t_n{s}", 82.5 + 2 * s, [P, S]) for s in range(2)]
    h_f = [at(f"h_f{s}", 86.5 + 2 * s, [P, S]) for s in range(2)]
    mean, ln_ms = at("mean", 90.5, [P, S]), at("ln_ms", 92.5, [P, S])
    mid_hi, mid_lo = at("mid_hi", 0, [P, DC, S], F32R), at("mid_lo", 16, [P, DC, S], F32R)
    y = at("y", 32, [P, DC, S])
    act_a = [at(f"act_a{s}", 48 + 2 * s, [P, S]) for s in range(2)]
    act_b = [at(f"act_b{s}", 52 + 2 * s, [P, S]) for s in range(2)]
    act_p = [at(f"act_p{s}", 56 + 2 * s, [P, S]) for s in range(2)]
    cos_ret, sin_ret, cos_mla, sin_mla = (at(n, 61 + 2 * k, [P, S]) for k, n in
                                          enumerate(["cos_ret", "sin_ret", "cos_mla", "sin_mla"]))
    pos_i = at("pos_i", 94.5, [P, S], I32)
    pos_f, angle, turns = (at(n, 96.5 + 2 * k, [P, S]) for k, n in enumerate(["pos_f", "angle", "turns"]))
    rqk = at("rqk", 0, [P, 2 * PAIRS, S])
    rv_rows = at("rv_rows", 16, [P, QB, S])
    rgate = at("rgate", 24, [P, PAIRS, S])
    lat = at("lat", 32, [P, 3, S])
    lat_hi, lat_lo = at("lat_hi", 40, [P, 3, S], F32R), at("lat_lo", 46, [P, 3, S], F32R)
    swapped = [at(f"swapped{s}", 52 + 2 * s, [P, S]) for s in range(2)]
    lag = at("lag", 57, [P, S])
    decay = [at(f"decay{s}", 61 + 2 * s, [P, S]) for s in range(2)]
    rope_t = [at(f"rope_t{s}", 96.5 + 2 * s, [P, S]) for s in range(2)]
    kpe = at("kpe", 102.5, [P, S])
    rp = [at("rp0", 69, [P, ZW]), at("rp1", 32, [P, ZW])]
    r_hi = [t_hi, at("r_hi1", 96.5, [P, ZW], F32R)]
    r_lo = [t_lo, at("r_lo1", 52, [P, ZW], F32R)]
    mk, mv_rows, mq = at("mk", 16, [P, HEADS, S]), at("mv_rows", 32, [P, QB, S]), at("mq", 0, [P, HEADS, S])
    m_hi, m_lo = at("m_hi", 40, [P, 5, S], F32R), at("m_lo", 50, [P, 5, S], F32R)
    mp = [at("mp0", 74.5, [P, ZW]), at("mp1", 79.5, [P, ZW])]
    mt_lo = [t_lo, at("mt_lo1", 60, [P, ZW], F32R)]

    names = """in_const in_mats in_vec in_x in_lag in_pos ada_f0 ada_f1 ada_f2 ada_f3 ada_a0 ada_a1 raw_full0 raw_full1
        rounded c_act ada0_step ada0_sum mod0_cols mod0_done gain_step gain_done
        w_hi_done w_lo_done tile_done group_free
        sq_done sum_done stat_done ms_done rs_done tn_done hf_done made_hi made_lo upd_step x_done
        ada_step ada_sum mod_cols mod_done
        sig_done tap
        qk_hi qk_lo v_hi v_lo z_done zm_done e_done l_done sp_done sph_done spl_done cum_done a_done ah_done al_done o_done o_evac
        gate_sig osp_hi osp_lo mean_ps mean_done xc_done
        merge_m mid_silu mid_f mid_hi_done mid_lo_done
        ident_done conv2 silu_arg
        ang_step ang_arg trig sw_done rope_m rope_s rp_done lat_done kpe_done
        rz_done dec_done rp_f rp_hi rp_lo ro_done ro_evac
        gn_mean gn_xc gn_sq gn_var gn_y
        mq_done qrope_done mqk_hi mqk_lo mv_hi mv_lo kst_hi kst_lo mz_done mx_done nmx_done mp_done rcp_done pn_done mt_done mth mtl
        mo_done mo_evac mos_hi mos_lo fin_done out_done""".split()

    with ExitStack() as ctx:
        sem = {n: ctx.enter_context(nc.semaphore(n)) for n in names}
        psum = ctx.enter_context(nc.psum_tensor("psum", [P, 8 * S], F32))
        bank = [psum[:, b * S:(b + 1) * S] for b in range(8)]
        z2 = [psum[:, 4 * S:7 * S], psum[:, 0:3 * S]]
        o2 = [bank[7], bank[3]]
        z, o_ps = z2[0], o2[0]
        mod_ps = z[:, ZW:ZW + 6 * DC]
        raw_full = [sem["raw_full0"], sem["raw_full1"]]
        ada_full = [sem["ada_a0"], sem["ada_a1"]]
        block = ctx.enter_context(nc.Block())

        def col(name, k=0, n=1):
            return vec[:, bass.ds(VEC[name] + k, n)]

        def scol(name, k=0):
            return small[:, bass.ds(SMALL[name] + k, 1)]

        def rstds(name):
            return NORMS[name][0] + (PAIRS if name in ("ffn2", "final") else 0)

        def chunk(t, k, rows=slice(0, P)):
            return t[rows, bass.ds(k, 1), :].rearrange("p a n -> p (a n)")

        def pair_v(t):
            return t.rearrange("p (b n) -> p b n", b=QB)

        @block.sync
        def _(sp):
            sp.dma_start(small[:, :], dram["small"]).then_inc(sem["in_const"], 16)
            sp.dma_start(vec[:, :], dram["vec"]).then_inc(sem["in_vec"], 16)
            sp.dma_start(x[:, :, :], dram["x"]).then_inc(sem["in_x"], 16)
            sp.dma_start(const_raw[:, :, :], dram["mats"][:, 0:5, :]).then_inc(sem["in_mats"], 16)
            for t, k in ((ident, 0), (ones, 5), (block_mean, 6)):
                sp.dma_start(t[:, :], dram["mats"][:, k, :]).then_inc(sem["in_mats"], 16)
            for b in range(4):
                sp.dma_start(ada_first[:, 4 * b:4 * b + 4], dram["ada"][4 * b:4 * b + 4].rearrange("g p k n -> p g k n")
                             ).then_inc(sem[f"ada_f{b}"], 16)

            def load(stage, k, slot):
                g = stage.g0 + k
                if positive(g - 1):
                    sp.wait_ge(sem["w_lo_done"], g - 1)
                sp.dma_start(raw[slot][:, 0:stage.kc, :].rearrange("p k n -> p (k n)"),
                             dram["w_" + stage.name][bass.ds(k, 1)].rearrange("g p n -> p (g n)")).then_inc(raw_full[slot], 16)

            def load_ada(a, slot):
                if positive(a - 1):
                    sp.wait_ge(sem["ada_sum"], a - 1)
                if isinstance(a, int) and a == 0:
                    sp.wait_ge(sem["rounded"], 1)
                sp.dma_start(ada_raw[slot][:, :, :].rearrange("p k n -> p (k n)"),
                             dram["ada"][bass.ds(ADA_FIRST + a, 1)].rearrange("g p k n -> p (g k n)")).then_inc(ada_full[slot], 16)

            def stage_loads(stage, ada=None, per=0):
                def body(i):
                    for s in range(2):
                        load(stage, 2 * i + s, s)
                        for r in range(per):
                            load_ada(ada + (2 * i + s) * per + r, r if per > 1 else s)
                first = 1 if stage.g0 == 0 or ada == 0 else 0
                if first:
                    body(0)
                with sp.Fori(first, stage.n // 2) as i:
                    body(i)

            stage_loads(st["glu"])
            stage_loads(st["qk"], 0, 2)
            stage_loads(st["val"], 8, 2)
            stage_loads(st["gate"], 12, 2)
            stage_loads(st["att_out"], 28, 1)
            stage_loads(st["conv_out"])
            stage_loads(st["mix_out"])
            stage_loads(st["ffn_in0"])
            sp.wait_ge(sem["made_lo"], MADE["attn2"])
            sp.dma_start(pos_i[:, :], dram["positions"].to_broadcast([P, S])).then_inc(sem["in_pos"], 16)
            for name in ["ffn_out0", "ffn_in1", "ffn_out1", "ffn_in2", "ffn_out2"]:
                stage_loads(st[name])
            sp.wait_ge(sem["mid_lo_done"], 8 + FC)
            sp.dma_start(lag[:, :], dram["lag"]).then_inc(sem["in_lag"], 16)
            for name in ["latent", "ret_qk", "ret_val", "ret_gate", "up_v", "up_k", "up_q", "mix_out2",
                         "up0", "down0", "up1", "down1", "up2", "down2"]:
                stage_loads(st[name])
            for k in range(DC):
                sp.wait_ge(sem["fin_done"], k + 1)
                sp.dma_start(out[:, k], y[:, k]).then_inc(sem["out_done"], 16)
            sp.wait_ge(sem["out_done"], 16 * DC)

        @block.tensor
        def _(pe):
            mm = nc.tensor.matmul

            def o_ps_read(name):
                if NORMS[name][0]:
                    pe.wait_ge(sem["ms_done"], rstds(name))

            def stat_sum(name):
                e, q0, n = NORMS[name]
                pe.wait_ge(sem["sum_done"], q0 + n)
                o_ps_read(name)
                mm(o_ps, ones[:, :], sq_sum[:, :], start=True, stop=True).then_inc(sem["stat_done"], 1)

            def stat_chunks(name):
                e, q0, n = NORMS[name]
                o_ps_read(name)
                for c in range(n):
                    pe.wait_ge(sem["sq_done"], q0 + c + 1)
                    mm(o_ps, ones[:, :], sq[(q0 + c) % 2][:, :], start=(c == 0), stop=(c == n - 1)).then_inc(sem["sum_done"], 1)

            PASSES = 3

            def tile(stage, slot, t, x_hi, x_lo, k0=0, rows=False, ready=None, passes=range(PASSES)):
                ps, kc = bank[2 * slot + t], stage.kc
                for r in range(2 if rows else 1):
                    for n in passes:
                        w, xv = ((w_hi, x_hi), (w_lo, x_hi), (w_hi, x_lo))[n]
                        for k in range(kc):
                            if ready and n == 0 and slot == 0 and t == 0 and r == 0 and k >= ready[2]:
                                pe.wait_ge(sem[ready[0]], ready[1] + k - ready[2] + 1)
                            first, final = n == 0 and k == 0, n == PASSES - 1 and k == kc - 1
                            if rows:
                                b = 2 * t + r
                                last = mm(ps[:, r * 256:(r + 1) * 256], xv[:, k0 + k, b * P:(b + 1) * P], w[slot][:, k, :],
                                          start=first, stop=final)
                            else:
                                last = mm(ps, w[slot][:, k, t * P:(t + 1) * P], xv[:, k0 + k, :], start=first, stop=final)
                if passes[-1] == PASSES - 1:
                    last.then_inc(sem["tile_done"], 1)

            def first_group(stage, x_hi, x_lo, k0, ready):
                for k in range(stage.kc):
                    if k >= ready[2]:
                        pe.wait_ge(sem[ready[0]], ready[1] + k - ready[2] + 1)
                    for t in range(2):
                        for n, (w, xv) in enumerate(((w_hi, x_hi), (w_lo, x_hi), (w_hi, x_lo))):
                            last = mm(bank[t], w[0][:, k, t * P:(t + 1) * P], xv[:, k0 + k, :],
                                      start=(n == 0 and k == 0), stop=(n == 2 and k == stage.kc - 1))
                        if k == stage.kc - 1:
                            last.then_inc(sem["tile_done"], 1)

            def weights(g):
                pe.wait_ge(sem["w_lo_done"], g + 1)
                if positive(g - 1):
                    pe.wait_ge(sem["group_free"], g - 1)

            def mod_column(a, slot):
                pe.wait_ge(sem["ada_sum"], a + 1)
                mm(psum[:, bass.ds(4 * S + ZW + ADA_FIRST + a, 1)], ada_acc[slot][:, :], ones[:, 0:1], start=True, stop=True
                   ).then_inc(sem["mod_cols"], 1)

            def gemm(stage, x_hi, x_lo, k0=0, rows=False, ready=None, ada=0, per=0, steps=None):
                def group(i, s, first=False):
                    for r in range(per):
                        mod_column(ada + (2 * i + s) * per + r, r if per > 1 else s)
                    weights(stage.g0 + 2 * i + s)
                    if first and ready and not rows:
                        first_group(stage, x_hi, x_lo, k0, ready)
                    else:
                        for t in range(2):
                            tile(stage, s, t, x_hi, x_lo, k0, rows, ready if first else None)

                begin, end = steps or (0, stage.n // 2)
                if ready or stage.g0 == 0:
                    group(begin, 0, True)
                    group(begin, 1)
                    begin += 1
                if begin < end:
                    with pe.Fori(begin, end) as i:
                        group(i, 0)
                        group(i, 1)

            def scores(zz, q_rows, k_rows, q_at, k_at, hi, lo, start_mask):
                for kb in range(QB):
                    a, w = BLOCK_AT[kb], BLOCK_W[kb]
                    for n, (kk, qq) in enumerate(((hi, hi), (hi, lo), (lo, hi))):
                        last = mm(zz[:, a:a + w], kk[k_rows, k_at, kb * P:(kb + 1) * P], qq[q_rows, q_at, kb * P:S],
                                  start=(n == 0 and kb < 3), stop=(n == 2), skip_group_check=True)
                    if start_mask:
                        last = mm(zz[:, a:a + P], ident_r, mask_kq_r, start=False, stop=True, skip_group_check=True)
                return last

            def values(o, vs_hi, vs_lo, v_at, p_hi, p_lo):
                for kb in range(QB):
                    a, w = BLOCK_AT[kb], BLOCK_W[kb]
                    for n, (vv, aa) in enumerate(((vs_hi, p_hi), (vs_hi, p_lo), (vs_lo, p_hi))):
                        last = mm(o[:, kb * P:S], vv[:, v_at, kb * P:(kb + 1) * P], aa[:, a:a + w],
                                  start=(n == 0 and kb == 0), stop=(n == 2 and kb == QB - 1), skip_group_check=True)
                return last

            pe.wait_ge(sem["in_mats"], 64)
            stat_sum("pre_mix")
            for b in range(4):
                pe.wait_ge(sem["ada0_sum"], b + 1)
                for k in range(4):
                    last = mm(mod_ps[:, 4 * b + k:4 * b + k + 1], ada_acc0[:, b, k, :], ones[:, 0:1], start=True, stop=True)
                last.then_inc(sem["mod0_cols"], 1)
            pe.wait_ge(sem["mod0_done"], 1)
            gemm(st["glu"], h_hi, h_lo, ready=("made_lo", MADE["pre_mix"], 0))
            gemm(st["qk"], h_hi, h_lo, ada=0, per=2)
            gemm(st["val"], h_hi, h_lo, rows=True, ada=8, per=2)

            def head(i, s):
                rows, n = slice(HD * s, HD * s + HD), 2 * i + s
                for r in range(2):
                    mod_column(12 + n * 2 + r, r)
                if s == 0:
                    pe.wait_ge(sem["qk_lo"], 2 * i + 2)
                scores(z, rows, rows, 0, 1, stage_hi, stage_lo, True).then_inc(sem["z_done"], 1)
                weights(st["gate"].g0 + n)
                tile(st["gate"], s, 0, h_hi, h_lo)
                tile(st["gate"], s, 1, h_hi, h_lo, passes=range(1))
                pe.wait_ge(sem["spl_done"], 2 * n + 2)
                for kb in range(QB):
                    a, w = BLOCK_AT[kb], BLOCK_W[kb]
                    for part in (t_hi, t_lo):
                        last = mm(z[:, a:a + w], tri_r, part[:, a:a + w], start=False, stop=True, skip_group_check=True)
                        for later in range(kb + 1, QB):
                            a2, w2 = BLOCK_AT[later], BLOCK_W[later]
                            last = mm(z[:, a + w - w2:a + w], ones_neg_r, part[:, a2:a2 + w2], start=False, stop=True,
                                      skip_group_check=True)
                last.then_inc(sem["cum_done"], 1)
                tile(st["gate"], s, 1, h_hi, h_lo, passes=range(1, PASSES))
                pe.wait_ge(sem["al_done"], 2 * n + 2)
                if s == 0:
                    pe.wait_ge(sem["v_lo"], i + 1)
                else:
                    pe.wait_ge(sem["o_evac"], n)
                values(o_ps, stage_hi, stage_lo, 2, t_hi, t_lo).then_inc(sem["o_done"], 1)

            with pe.Fori(0, PAIRS) as i:
                for s in range(2):
                    head(i, s)
            pe.wait_ge(sem["tap"], 4 * (TAPS + 1))
            pe.wait_ge(sem["o_evac"], HEADS)
            for k in range(4):
                last = mm(o_ps, ones[:, :], u[:, k, PAD:PAD + S] if k < 3 else conv3[:, :], start=(k == 0), stop=(k == 3))
            last.then_inc(sem["mean_ps"], 1)
            gemm(st["att_out"], h_hi, h_lo, k0=4, ready=("osp_lo", 0, 0), ada=28, per=1, steps=(0, 1))
            stat_sum("conv_ln")
            gemm(st["att_out"], h_hi, h_lo, k0=4, ada=28, per=1, steps=(1, 2))
            gemm(st["conv_out"], h_hi, h_lo, ready=("made_lo", MADE["conv"], 0))
            gemm(st["mix_out"], mid_hi, mid_lo, ready=("mid_lo_done", 0, 0))
            stat_sum("post_mix")
            stat_chunks("pre_ffn")
            for r, n in enumerate(FFN_PARTS):
                gemm(st[f"ffn_in{r}"], h_hi, h_lo, ready=("made_lo", MADE["pre_ffn"], 0) if r == 0 else None)
                gemm(st[f"ffn_out{r}"], mid_hi, mid_lo, ready=("mid_lo_done", 8 + PART_AT[r], 0))
            stat_sum("post_ffn")
            stat_chunks("attn2")
            gemm(st["latent"], h_hi, h_lo, ready=("made_lo", MADE["attn2"], 0))
            gemm(st["ret_qk"], h_hi, h_lo)
            stat_sum("c_q")
            stat_sum("c_kv")
            gemm(st["ret_val"], h_hi, h_lo, rows=True)
            gemm(st["ret_gate"], h_hi, h_lo)

            def ret_scores(i, s):
                rows = slice(HD * s, HD * s + HD)
                if s == 0:
                    pe.wait_ge(sem["qk_lo"], 2 * PAIRS + 2 * i + 2)
                scores(z2[s], rows, rows, 0, 1, stage_hi, stage_lo, False).then_inc(sem["rz_done"], 1)

            def ret_values(i, s):
                if s == 0:
                    pe.wait_ge(sem["v_lo"], PAIRS + i + 1)
                pe.wait_ge(sem["rp_lo"], 2 * i + s + 1)
                values(o2[s], stage_hi, stage_lo, 2, r_hi[s], r_lo[s]).then_inc(sem["ro_done"], 1)

            pe.wait_ge(sem["group_free"], st["up_v"].g0)
            pe.wait_ge(sem["ms_done"], 8)
            ret_scores(0, 0)
            ret_scores(0, 1)
            with pe.Fori(0, PAIRS - 1) as i:
                for s in range(2):
                    ret_values(i, s)
                    ret_scores(i + 1, s)
            ret_values(PAIRS - 1, 0)
            ret_values(PAIRS - 1, 1)
            pe.wait_ge(sem["ro_evac"], HEADS)
            gemm(st["up_v"], lat_hi, lat_lo, k0=2, rows=True, ready=("made_lo", MADE["lat"] + 2, 0))
            for k in range(PAIRS):
                if k:
                    pe.wait_ge(sem["ms_done"], 8 + k)
                mm(o_ps, block_mean[:, :], rqk[:, k, :], start=True, stop=True).then_inc(sem["gn_mean"], 1)
                pe.wait_ge(sem["gn_sq"], k + 1)
                mm(o_ps, block_mean[:, :], sq[k % 2][:, :], start=True, stop=True).then_inc(sem["gn_var"], 1)
            gemm(st["up_k"], lat_hi, lat_lo, k0=2)
            gemm(st["up_q"], lat_hi, lat_lo, ready=("made_lo", MADE["lat"], 0))

            pe.wait_ge(sem["group_free"], st["mix_out2"].g0)
            pe.wait_ge(sem["kst_lo"], 2)
            def mla_scores(i, s):
                pe.wait_ge(sem["mqk_lo"], 4 * i + 2 * s + 2)
                if positive(2 * i + s - 1):
                    pe.wait_ge(sem["mtl"], 2 * i + s - 1)
                for t in range(QB):
                    a, w = ROW_AT[t], ROW_W[t]
                    for n, (qq, kk) in enumerate(((m_hi, m_hi), (m_hi, m_lo), (m_lo, m_hi))):
                        mm(z2[s][:, a:a + w], qq[0:96, s, t * P:(t + 1) * P], kk[0:96, 2 + s, 0:w],
                           start=(n == 0), stop=(n == 2), skip_group_check=True)
                    last = mm(z2[s][:, a + w - P:a + w], ident_r, mask_qk_r, start=False, stop=True, skip_group_check=True)
                last.then_inc(sem["mz_done"], 1)

            def mla_transpose(i, s):
                pe.wait_ge(sem["pn_done"], 2 * i + s + 1)
                for kb in range(QB):
                    for t in range(kb, QB):
                        a = BLOCK_AT[kb] + (t - kb) * P
                        last = nc.tensor.transpose(z2[s][:, a:a + P], mp[s][:, ROW_AT[t] + kb * P:ROW_AT[t] + (kb + 1) * P],
                                                   ident[:, :])
                last.then_inc(sem["mt_done"], 1)

            def mla_values(i, s):
                if s == 0:
                    pe.wait_ge(sem["mv_lo"], i + 1)
                pe.wait_ge(sem["mtl"], 2 * i + s + 1)
                values(o2[s], m_hi, m_lo, 4, r_hi[s], mt_lo[s]).then_inc(sem["mo_done"], 1)

            def mla_period(i):
                mla_scores(i, 0)
                mla_transpose(i - 1, 1)
                mla_values(i - 1, 0)
                mla_scores(i, 1)
                mla_transpose(i, 0)
                mla_values(i - 1, 1)

            mla_scores(0, 0)
            mla_scores(0, 1)
            mla_transpose(0, 0)
            with pe.Fori(1, PAIRS) as i:
                mla_period(i)
            mla_transpose(PAIRS - 1, 1)
            mla_values(PAIRS - 1, 0)
            mla_values(PAIRS - 1, 1)
            pe.wait_ge(sem["mo_evac"], HEADS)
            pe.wait_ge(sem["made_lo"], MADE["gn"] + PAIRS)
            gemm(st["mix_out2"], h_hi, h_lo, ready=("mos_lo", 0, PAIRS))
            stat_sum("ffn2")
            for r, n in enumerate(FFN_PARTS):
                gemm(st[f"up{r}"], h_hi, h_lo, ready=("made_lo", MADE["ffn2"], 0) if r == 0 else None)
                gemm(st[f"down{r}"], mid_hi, mid_lo, ready=("mid_lo_done", 8 + FC + PART_AT[r], 0))
            stat_sum("final")

        @block.scalar
        def _(act):
            A = nc.scalar.activation
            hf = [0]
            norms = [0]

            def apart(n):
                A(spare[:, n:n + 1], small[:, 0:1], ACT.Copy)

            def split_hi(stage, k, slot, half):
                g = stage.g0 + k
                act.wait_ge(raw_full[slot], 16 * (stage.g0 // 2 + half + 1))
                if positive(g - 1):
                    act.wait_ge(sem["tile_done"], 2 * g - 2)
                A(w_hi[slot][:, 0:stage.kc, :], raw[slot][:, 0:stage.kc, :], ACT.Copy).then_inc(sem["w_hi_done"], 1)

            def run(stage, evac):
                def step(i, s, final=False):
                    def ahead():
                        if not (final and s):
                            split_hi(stage, 2 * i + s + 1, 1 - s, i + s)
                        elif stage.next:
                            split_hi(stage.next, 0, 0, 0)
                        return final
                    evac(i, s, 2 * i + s, ahead)
                n = stage.n // 2
                if n == 2:
                    step(0, 0)
                    step(0, 1)
                elif n > 2:
                    with act.Fori(0, n - 1) as i:
                        step(i, 0)
                        step(i, 1)
                step(n - 1, 0, True)
                step(n - 1, 1, True)

            def arrived(stage, k, t):
                act.wait_ge(sem["tile_done"], 2 * (stage.g0 + k) + t + 1)

            def free(stage, k, ins_of):
                if positive(stage.g0 + k):
                    act.wait_ge(sem["group_free"], stage.g0 + k)
                ins_of().then_inc(sem["group_free"], 1)

            def squares(name, of, wait, chunks=None):
                e, q0, n = NORMS[name]
                for c in chunks or range(n):
                    if q0 + c >= 2:
                        act.wait_ge(sem["sum_done"], q0 + c - 1)
                    wait(c)
                    A(sq[(q0 + c) % 2][:, :], of(c), ACT.Square).then_inc(sem["sq_done"], 1)

            def rstd(width, wait):
                nc.scalar.preload_act_table_set("natural_log_exp_and_others")
                wait()
                A(ln_ms[:, :], o_ps, ACT.Ln, scale=1.0 / width, bias=scol("eps")).then_inc(sem["ms_done"], 1)
                norms[0] += 1
                act.wait_ge(sem["ms_done"], norms[0])
                A(rs[:, :], ln_ms[:, :], ACT.Exp, scale=-0.5).then_inc(sem["rs_done"], 1)

            def norm_rstd(name, width):
                def wait():
                    if name in POOL_NORMS:
                        act.wait_ge(sem["stat_done"], POOL_NORMS.index(name) + 1)
                    else:
                        act.wait_ge(sem["sum_done"], NORMS[name][1] + NORMS[name][2])
                rstd(width, wait)

            def made(m, dst, shift=None, func=None):
                src = t_n[m % 2]
                act.wait_ge(sem["tn_done"], m + 1)
                if func is not None:
                    if m >= 2:
                        act.wait_ge(sem["made_lo"], m - 1)
                    A(h_f[m % 2][:, :], src[:, :], func, bias=shift).then_inc(sem["hf_done"], 1)
                    hf[0] += 1
                    act.wait_ge(sem["hf_done"], hf[0])
                    src, shift = h_f[m % 2], None
                if shift is None:
                    A(dst, src[:, :], ACT.Copy).then_inc(sem["made_hi"], 1)
                else:
                    A(dst, src[:, :], ACT.Identity, bias=shift).then_inc(sem["made_hi"], 1)

            act.wait_ge(sem["in_vec"], 16)
            A(c_act[:, :], col("c", 0, DC), ACT.Silu).then_inc(sem["c_act"], 1)
            act.wait_ge(sem["in_x"], 16)
            squares("pre_mix", lambda c: x[:, c, :], lambda c: None)
            act.wait_ge(sem["in_mats"], 64)
            A(rounded[:, :, :], const_raw[:, :, :], ACT.Copy).then_inc(sem["rounded"], 1)
            act.wait_ge(sem["in_const"], 16)
            norm_rstd("pre_mix", D)
            act.wait_ge(sem["mod0_done"], 1)
            for c in range(DC):
                if c == 2:
                    split_hi(st["glu"], 0, 0, 0)
                made(MADE["pre_mix"] + c, h_hi[:, c, :], mod[:, c:c + 1])

            def glu(i, s, k, ahead):
                ahead()
                arrived(st["glu"], k, 1)
                if positive(k - 1):
                    act.wait_ge(sem["group_free"], k - 1)
                A(glu_sig[s][:, :], bank[2 * s + 1], ACT.Sigmoid).then_inc(sem["sig_done"], 1)

            def qk(i, s, k, ahead):
                ahead()
                arrived(st["qk"], k, 0)
                A(qkT[:, 2 * k, :], bank[2 * s], ACT.Copy)
                arrived(st["qk"], k, 1)
                free(st["qk"], k, lambda: A(qkT[:, 2 * k + 1, :], bank[2 * s + 1], ACT.Copy))

            def rows_of(stage, dst):
                def evac(i, s, k, ahead):
                    ahead()
                    cols = slice(256 * k, 256 * k + 256)
                    arrived(stage, k, 0)
                    A(dst[:, 0:2, cols], bank[2 * s].rearrange("p (b n) -> p b n", b=2), ACT.Copy)
                    arrived(stage, k, 1)
                    free(stage, k, lambda: A(dst[:, 2:4, cols], bank[2 * s + 1].rearrange("p (b n) -> p b n", b=2), ACT.Copy))
                return evac

            run(st["glu"], glu)
            run(st["qk"], qk)
            run(st["val"], rows_of(st["val"], v_rows))

            def stage_qk(i, q, k):
                A(stage_hi[:, 0, :], chunk(q, i), ACT.Copy, scale=HD ** -0.5).then_inc(sem["qk_hi"], 1)
                A(stage_hi[:, 1, :], chunk(k, PAIRS + i), ACT.Copy).then_inc(sem["qk_hi"], 1)

            def stage_v(i, v):
                A(pair_v(stage_hi[:, 2, :]), v[:, :, bass.ds(P * i, P)], ACT.Copy).then_inc(sem["v_hi"], 1)

            def head(i, s, n, ahead):
                rows, g = slice(HD * s, HD * s + HD), st["gate"].g0 + n
                if s == 0:
                    stage_v(i, v_rows)
                for j, (a, b) in enumerate(HALVES):
                    act.wait_ge(sem["zm_done"], 2 * n + j + 1)
                    A(zbuf[:, a:b], zbuf[:, a:b], ACT.Exp).then_inc(sem["e_done"], 1)
                for j, (a, b) in enumerate(HALVES):
                    act.wait_ge(sem["e_done"], 2 * n + j + 1)
                    A(zbuf[:, a:b], zbuf[:, a:b], ACT.Ln, bias=1.0).then_inc(sem["l_done"], 1)
                for j, (a, b) in enumerate(HALVES):
                    act.wait_ge(sem["sp_done"], 2 * n + j + 1)
                    A(t_hi[:, a:b], zbuf[:, a:b], ACT.Copy).then_inc(sem["sph_done"], 1)
                arrived(st["gate"], n, 0)
                A(chunk(gates, 2 * n), bank[2 * s], ACT.Copy)
                if not ahead() and s:
                    stage_qk(i + 1, qkT, qkT)
                for j, (a, b) in enumerate(HALVES):
                    act.wait_ge(sem["cum_done"], n + 1)
                    A(zbuf[:, a:b], z[:, a:b], ACT.Exp).then_inc(sem["a_done"], 1)
                for j, (a, b) in enumerate(HALVES):
                    act.wait_ge(sem["a_done"], 2 * n + j + 1)
                    A(t_hi[:, a:b], zbuf[:, a:b], ACT.Copy).then_inc(sem["ah_done"], 1)
                arrived(st["gate"], n, 1)
                free(st["gate"], n, lambda: A(chunk(gates, 2 * n + 1), bank[2 * s + 1], ACT.Copy))
                act.wait_ge(sem["o_done"], n + 1)
                apart(0)
                A(chunk(qkT, i, rows), o_ps[rows, :], ACT.Copy).then_inc(sem["o_evac"], 1)

            nc.scalar.preload_act_table_set("natural_log_exp_and_others")
            act.wait_ge(sem["group_free"], st["gate"].g0)
            stage_qk(0, qkT, qkT)
            run(st["gate"], head)
            act.wait_ge(sem["o_evac"], HEADS)
            for c in range(4):
                A(h_hi[:, 4 + c, :], qkT[:, c, :], ACT.Copy).then_inc(sem["osp_hi"], 1)
            act.wait_ge(sem["mean_ps"], 1)
            A(mean[:, :], o_ps, ACT.Copy, scale=1.0 / (4 * P)).then_inc(sem["mean_done"], 1)

            def att_out(i, s, k, ahead):
                ahead()
                if k == 0:
                    act.wait_ge(sem["group_free"], st["att_out"].g0)
                    A(gates[:, DC:, :], gates[:, DC:, :], ACT.Sigmoid).then_inc(sem["gate_sig"], 1)
                elif k == 1:
                    squares("conv_ln", lambda c: u[:, c, PAD:PAD + S] if c < 3 else conv3[:, :],
                            lambda c: act.wait_ge(sem["xc_done"], c + 1))
                elif k == 2:
                    norm_rstd("conv_ln", 4 * P)
                else:
                    for c in range(4):
                        made(MADE["conv"] + c, h_hi[:, c, :], col("conv_ln_b", c), ACT.Silu)
                    A(gates[:, 0:DC, :], gates[:, 0:DC, :], ACT.Sigmoid).then_inc(sem["gate_sig"], 1)

            run(st["att_out"], att_out)

            def merged(i, s, k, ahead):
                ahead()
                for t in range(2):
                    n = 2 * k + t
                    act.wait_ge(sem["mid_f"], n + 1)
                    A(mid_hi[:, n, :], gates[:, n, :], ACT.Copy).then_inc(sem["mid_hi_done"], 1)

            def to_y(stage, norm=None):
                def evac(i, s, k, ahead):
                    ahead()
                    for t in range(2):
                        n = 2 * k + t
                        arrived(stage, k, t)
                        if norm:
                            squares(norm, lambda c: bank[2 * s + t], lambda c: None, [n])
                        copy = lambda: A(y[:, n, :], bank[2 * s + t], ACT.Copy)
                        if t == 0:
                            copy()
                        else:
                            free(stage, k, copy)
                return evac

            def squares_after(stage, norm, of):
                def evac(i, s, k, ahead):
                    ahead()
                    act.wait_ge(sem["group_free"], stage.g0 + k + 1)
                    squares(norm, of, lambda c: None, [2 * k, 2 * k + 1])
                return evac

            run(st["conv_out"], merged)
            run(st["mix_out"], to_y(st["mix_out"], "post_mix"))
            norm_rstd("post_mix", D)
            squares("pre_ffn", lambda c: x[:, c, :], lambda c: act.wait_ge(sem["x_done"], c + 1))
            norm_rstd("pre_ffn", D)
            act.wait_ge(sem["mod_done"], 1)
            for c in range(DC):
                made(MADE["pre_ffn"] + c, h_hi[:, c, :], mod[:, 3 * DC + c:3 * DC + c + 1])

            def gated(stage):
                def evac(i, s, k, ahead):
                    ahead()
                    arrived(stage, k, 0)
                    act.wait_ge(sem["group_free"], stage.g0 + k - 1)
                    A(act_a[s][:, :], bank[2 * s], ACT.Silu).then_inc(sem["mid_silu"], 1)
                    act.wait_ge(sem["group_free"], stage.g0 + k + 1)
                    A(chunk(mid_hi, k), act_p[s][:, :], ACT.Copy
                      ).then_inc(sem["mid_hi_done"], 1)
                return evac

            for r in range(3):
                run(st[f"ffn_in{r}"], gated(st[f"ffn_in{r}"]))
                if r == 1:
                    for k, table in enumerate((sin_ret, cos_ret, sin_mla, cos_mla)):
                        act.wait_ge(sem["ang_arg"], k + 1)
                        A(table[:, :], table[:, :], ACT.Sin).then_inc(sem["trig"], 1)
                run(st[f"ffn_out{r}"], (to_y(st["ffn_out0"]), lambda i, s, k, ahead: ahead(),
                                        squares_after(st["ffn_out2"], "post_ffn", lambda c: y[:, c, :]))[r])
            norm_rstd("post_ffn", D)
            squares("attn2", lambda c: x[:, c, :], lambda c: act.wait_ge(sem["x_done"], 8 + c + 1))
            norm_rstd("attn2", D)
            for c in range(DC):
                made(MADE["attn2"] + c, h_hi[:, c, :])

            def latent(i, s, k, ahead):
                ahead()
                arrived(st["latent"], k, 0)
                A(lat[:, 2 * k, :], bank[2 * s], ACT.Copy).then_inc(sem["lat_done"], 1)
                if k == 0:
                    arrived(st["latent"], k, 1)
                    free(st["latent"], k, lambda: A(lat[:, 1, :], bank[2 * s + 1], ACT.Copy))

            def rotary(i, s, k, ahead):
                ahead()
                for t in range(2):
                    arrived(st["ret_qk"], k, t)
                    if k:
                        act.wait_ge(sem["rp_done"], 2 * (k - 1) + t + 1)
                    for b in range(4):
                        last = A(swapped[t][32 * b:32 * b + 32, :], bank[2 * s + t][32 * (b ^ 1):32 * (b ^ 1) + 32, :], ACT.Copy)
                    last.then_inc(sem["sw_done"], 1)

            def ret_gate(i, s, k, ahead):
                ahead()
                arrived(st["ret_gate"], k, 0)
                A(rgate[:, 2 * k, :], bank[2 * s], ACT.Silu)
                arrived(st["ret_gate"], k, 1)
                free(st["ret_gate"], k, lambda: A(rgate[:, 2 * k + 1, :], bank[2 * s + 1], ACT.Silu))

            run(st["latent"], latent)
            act.wait_ge(sem["lat_done"], 2)
            act.wait_ge(sem["group_free"], st["latent"].g0 + 1)
            squares("c_q", lambda c: lat[:, c, :], lambda c: None)
            squares("c_kv", lambda c: lat[:, 2, :], lambda c: None)
            run(st["ret_qk"], rotary)
            norm_rstd("c_q", 2 * P)
            for c in range(2):
                made(MADE["lat"] + c, lat_hi[:, c, :])
            norm_rstd("c_kv", P)
            made(MADE["lat"] + 2, lat_hi[:, 2, :])
            run(st["ret_val"], rows_of(st["ret_val"], rv_rows))
            run(st["ret_gate"], ret_gate)

            nc.scalar.preload_act_table_set("natural_log_exp_and_others")
            act.wait_ge(sem["rp_done"], 2 * PAIRS)
            act.wait_ge(sem["group_free"], st["up_v"].g0)
            act.wait_ge(sem["in_lag"], 16)
            def decays(i):
                for s in range(2):
                    A(decay[s][:, :], lag[:, :], ACT.Exp, scale=scol("log_gamma", 2 * i + s)).then_inc(sem["dec_done"], 1)

            def ret_high(i, s):
                act.wait_ge(sem["rp_f"], 2 * i + s + 1)
                A(r_hi[s][:, :], rp[s][:, :], ACT.Copy).then_inc(sem["rp_hi"], 1)

            def ret_pair(i, final=False):
                ret_high(i, 0)
                if not final:
                    act.wait_ge(sem["rz_done"], 2 * i + 2)
                    apart(0)
                    stage_qk(i + 1, rqk, rqk)
                ret_high(i, 1)
                if not final:
                    decays(i + 1)
                act.wait_ge(sem["ro_done"], 2 * i + 2)
                apart(1)
                for s in range(2):
                    rows = slice(HD * s, HD * s + HD)
                    A(chunk(rqk, i, rows), o2[s][rows, :], ACT.Copy).then_inc(sem["ro_evac"], 1)
                if not final:
                    stage_v(i + 1, rv_rows)

            stage_qk(0, rqk, rqk)
            stage_v(0, rv_rows)
            decays(0)
            with act.Fori(0, PAIRS - 1) as i:
                ret_pair(i)
            ret_pair(PAIRS - 1, True)
            run(st["up_v"], rows_of(st["up_v"], mv_rows))
            for k in range(PAIRS):
                m = MADE["gn"] + k
                act.wait_ge(sem["gn_xc"], k + 1)
                A(sq[k % 2][:, :], rqk[:, k, :], ACT.Square).then_inc(sem["gn_sq"], 1)
                if k:
                    act.wait_ge(sem["tn_done"], m)
                rstd(1.0, lambda: act.wait_ge(sem["gn_var"], k + 1))
                act.wait_ge(sem["gn_y"], k + 1)
                A(h_hi[:, k, :], h_f[m % 2][:, :], ACT.Copy).then_inc(sem["made_hi"], 1)

            def keys(i, s, k, ahead):
                ahead()
                for t in range(2):
                    arrived(st["up_k"], k, t)
                    A(mk[0:HD, 2 * (2 * k + t), :], bank[2 * s + t][0:HD, :], ACT.Copy)
                    last = lambda: A(mk[0:HD, 2 * (2 * k + t) + 1, :], bank[2 * s + t][HD:P, :], ACT.Copy)
                    if t == 0:
                        last()
                    else:
                        free(st["up_k"], k, last)

            def queries(i, s, k, ahead):
                ahead()
                for t in range(2):
                    arrived(st["up_q"], k, t)
                    A(mq[0:HD, 2 * k + t, :], bank[2 * s + t][0:HD, :], ACT.Copy).then_inc(sem["mq_done"], 1)

            run(st["up_k"], keys)
            run(st["up_q"], queries)
            act.wait_ge(sem["kpe_done"], 1)
            act.wait_ge(sem["group_free"], st["mix_out2"].g0)
            for s in range(2):
                A(m_hi[64:96, 2 + s, :], kpe[64:96, :], ACT.Copy).then_inc(sem["kst_hi"], 1)
            act.wait_ge(sem["qrope_done"], HEADS)
            nc.scalar.preload_act_table_set("natural_log_exp_and_others")
            def mla_qk(i, s):
                A(m_hi[0:96, s, :], chunk(mq, 2 * i + s, slice(0, 96)), ACT.Copy).then_inc(sem["mqk_hi"], 1)
                A(m_hi[0:HD, 2 + s, :], chunk(mk, 2 * i + s, slice(0, HD)), ACT.Copy).then_inc(sem["mqk_hi"], 1)

            def mla_v(i):
                A(pair_v(m_hi[:, 4, :]), mv_rows[:, :, bass.ds(P * i, P)], ACT.Copy).then_inc(sem["mv_hi"], 1)

            def mla_exp(i, s):
                act.wait_ge(sem["nmx_done"], 2 * i + s + 1)
                for t in range(QB):
                    a, w = ROW_AT[t], ROW_W[t]
                    last = A(mp[s][:, a:a + w], z2[s][:, a:a + w], ACT.Exp, scale=MLA_SCALE, bias=row_stat[:, s, 4 + t:5 + t],
                             accum_out=row_stat[:, s, 8 + t:9 + t])
                last.then_inc(sem["mp_done"], 1)

            def mla_high(i, s):
                act.wait_ge(sem["mt_done"], 2 * i + s + 1)
                A(r_hi[s][:, :], z2[s][:, 0:ZW], ACT.Copy).then_inc(sem["mth"], 1)

            def mla_out(i, s):
                rows = slice(HD * s, HD * s + HD)
                act.wait_ge(sem["mo_done"], 2 * i + s + 1)
                apart(s)
                A(chunk(mq, 2 * i, rows), o2[s][rows, :], ACT.Copy).then_inc(sem["mo_evac"], 1)

            def mla_period(i, first=False, final=False):
                if not first:
                    mla_high(i - 1, 1)
                mla_exp(i, 0)
                if not final:
                    mla_qk(i + 1, 0)
                if not first:
                    mla_out(i - 1, 0)
                mla_high(i, 0)
                mla_exp(i, 1)
                if not final:
                    mla_qk(i + 1, 1)
                if not first:
                    mla_out(i - 1, 1)
                mla_v(i)

            mla_qk(0, 0)
            mla_qk(0, 1)
            mla_period(0, first=True)
            with act.Fori(1, PAIRS - 1) as i:
                mla_period(i)
            mla_period(PAIRS - 1, final=True)
            mla_high(PAIRS - 1, 1)
            mla_out(PAIRS - 1, 0)
            mla_out(PAIRS - 1, 1)
            act.wait_ge(sem["mo_evac"], HEADS)
            for c in range(4):
                A(h_hi[:, 4 + c, :], mq[:, 2 * c, :], ACT.Copy).then_inc(sem["mos_hi"], 1)
            run(st["mix_out2"], squares_after(st["mix_out2"], "ffn2", lambda c: x[:, c, :]))
            norm_rstd("ffn2", D)
            for c in range(DC):
                made(MADE["ffn2"] + c, h_hi[:, c, :])

            def conv_gated(stage, part):
                def evac(i, s, k, ahead):
                    c0 = PART_AT[part] + k
                    chan = c0
                    ahead()
                    act.wait_ge(sem["mid_f"], DC + c0 - 1)
                    for t, buf in ((0, act_a[s]), (1, act_b[s])):
                        arrived(stage, k, t)
                        A(buf[:, :], bank[2 * s + t], ACT.Identity, scale=col("conv_w_2", 2 * 2 * FC + t * FC + chan),
                          bias=col("conv_b_2", t * FC + chan)).then_inc(sem["ident_done"], 1)
                    act.wait_ge(sem["silu_arg"], c0 + 1)
                    A(act_a[s][:, :], act_a[s][:, :], ACT.Silu).then_inc(sem["mid_silu"], 1)
                    act.wait_ge(sem["mid_f"], DC + c0 + 1)
                    A(chunk(mid_hi, k), act_p[s][:, :], ACT.Copy
                      ).then_inc(sem["mid_hi_done"], 1)
                return evac

            for r in range(3):
                run(st[f"up{r}"], conv_gated(st[f"up{r}"], r))
                run(st[f"down{r}"], squares_after(st["down2"], "final", lambda c: x[:, c, :]) if r == 2
                    else (lambda i, s, k, ahead: ahead()))
            norm_rstd("final", D)

        @block.vector
        def _(dve):
            tt, ts, stt = nc.vector.tensor_tensor, nc.vector.tensor_scalar, nc.vector.scalar_tensor_tensor
            taps = [0]

            def less(out_lo, full, high):
                return tt(out_lo, full, high.bitcast(F32), ALU.subtract)

            def split_lo(stage, k, slot):
                dve.wait_ge(sem["w_hi_done"], stage.g0 + k + 1)
                less(w_lo[slot][:, 0:stage.kc, :], raw[slot][:, 0:stage.kc, :], w_hi[slot][:, 0:stage.kc, :]
                     ).then_inc(sem["w_lo_done"], 1)

            def run(stage, evac):
                def step(i, s, final=False):
                    def ahead():
                        if not (final and s):
                            split_lo(stage, 2 * i + s + 1, 1 - s)
                        elif stage.next:
                            split_lo(stage.next, 0, 0)
                        return final
                    evac(i, s, 2 * i + s, ahead)
                n = stage.n // 2
                if n == 2:
                    step(0, 0)
                    step(0, 1)
                elif n > 2:
                    with dve.Fori(0, n - 1) as i:
                        step(i, 0)
                        step(i, 1)
                step(n - 1, 0, True)
                step(n - 1, 1, True)

            def arrived(stage, k, t):
                dve.wait_ge(sem["tile_done"], 2 * (stage.g0 + k) + t + 1)

            def free(stage, k, ins_of):
                if positive(stage.g0 + k):
                    dve.wait_ge(sem["group_free"], stage.g0 + k)
                ins_of().then_inc(sem["group_free"], 1)

            def freed(stage, k):
                dve.wait_ge(sem["group_free"], stage.g0 + k + 1)

            def normalised(m, src, g):
                stt(t_n[m % 2][:, :], src, g, rs[:, :], ALU.mult, ALU.mult).then_inc(sem["tn_done"], 1)

            def made(m0, n, src, g, dst_hi, dst_lo, shift=None, silu=False, between=None):
                for c in range(n + 1):
                    if c < n:
                        if c >= 2:
                            dve.wait_ge(sem["made_lo"], m0 + c - 1)
                        normalised(m0 + c, src(c), g(c))
                    if c:
                        m = m0 + c - 1
                        dve.wait_ge(sem["made_hi"], m + 1)
                        full = (h_f if silu else t_n)[m % 2]
                        if shift:
                            last = stt(dst_lo[:, c - 1, :], full[:, :], shift(c - 1), dst_hi[:, c - 1, :].bitcast(F32), ALU.add, ALU.subtract)
                        else:
                            last = less(dst_lo[:, c - 1, :], full[:, :], dst_hi[:, c - 1, :])
                        last.then_inc(sem["made_lo"], 1)
                    if c == 2 and between:
                        between()

            dve.wait_ge(sem["c_act"], 1)
            for b in range(4):
                dve.wait_ge(sem[f"ada_f{b}"], 16)
                for k in range(8):
                    part, acc = ada_first[:, 4 * b:4 * b + 4, k, :], ada_acc0[:, b]
                    if k == 0:
                        last = ts(acc, part, c_act[:, 0:1], None, ALU.mult)
                    else:
                        dve.wait_ge(sem["ada0_step"], 7 * b + k)
                        last = stt(acc, part, c_act[:, k:k + 1], acc, ALU.mult, ALU.add)
                    last.then_inc(sem["ada0_step" if k < 7 else "ada0_sum"], 1)
            dve.wait_ge(sem["mod0_cols"], 4)
            tt(mod[:, 0:ADA_FIRST], mod_ps[:, 0:ADA_FIRST], col("ada_b", 0, ADA_FIRST), ALU.add).then_inc(sem["mod0_done"], 1)
            nc.vector.memset(u[:, :, 0:PAD], 0.0).then_inc(sem["gain_step"], 1)
            dve.wait_ge(sem["mod0_done"], 1)
            stt(gain[:, 0, :], mod[:, DC:2 * DC], 1.0, col("pre_mix_g", 0, DC), ALU.add, ALU.mult).then_inc(sem["gain_done"], 1)
            dve.wait_ge(sem["gain_done"], 1)
            dve.wait_ge(sem["rs_done"], 1)
            made(MADE["pre_mix"], DC, lambda c: x[:, c, :], lambda c: gain[:, 0, c:c + 1], h_hi, h_lo, lambda c: mod[:, c:c + 1],
                 between=lambda: split_lo(st["glu"], 0, 0))

            def glu(i, s, k, ahead):
                ahead()
                dve.wait_ge(sem["sig_done"], k + 1)
                arrived(st["glu"], k, 0)
                free(st["glu"], k, lambda: tt(u[:, k, PAD:PAD + S], glu_sig[s][:, :], bank[2 * s], ALU.mult))

            def conv_start(c, acc):
                if taps[0]:
                    dve.wait_ge(sem["tap"], taps[0])
                ts(acc[:, :], u[:, c, 0:S], col("conv_w", c * TAPS), col("conv_b", c), ALU.mult, ALU.add).then_inc(sem["tap"], 1)
                taps[0] += 1

            def conv_tap(c, j, acc, dst, before):
                dve.wait_ge(sem["tap"], before)
                stt(dst, u[:, c, bass.ds(j, S)], col("conv_w", c * TAPS + j), acc[:, :], ALU.mult, ALU.add).then_inc(sem["tap"], 1)

            def conv_half(c, half):
                if half == 0:
                    conv_start(c, conv_tmp)
                for j in range(half * TAPS // 2, (half + 1) * TAPS // 2):
                    conv_tap(c, j, conv_tmp, u[:, c, PAD:PAD + S] if j == TAPS - 1 else conv_tmp[:, :], taps[0])
                    taps[0] += 1

            def conv_beside(c0):
                def evac(i, s, k, ahead):
                    ahead()
                    conv_half(c0 + i, s)
                return evac

            run(st["glu"], glu)
            dve.wait_ge(sem["gain_step"], 1)
            dve.wait_ge(sem["group_free"], st["qk"].g0)
            run(st["qk"], conv_beside(0))
            run(st["val"], conv_beside(2))

            def stage_qk(i, before, q, k):
                dve.wait_ge(sem["qk_hi"], 2 * before + 2 * i + 1)
                stt(stage_lo[:, 0, :], chunk(q, i), HD ** -0.5, stage_hi[:, 0, :].bitcast(F32), ALU.mult, ALU.subtract
                    ).then_inc(sem["qk_lo"], 1)
                dve.wait_ge(sem["qk_hi"], 2 * before + 2 * i + 2)
                less(stage_lo[:, 1, :], chunk(k, PAIRS + i), stage_hi[:, 1, :]).then_inc(sem["qk_lo"], 1)

            def stage_v(i, before, v):
                dve.wait_ge(sem["v_hi"], before + i + 1)
                less(pair_v(stage_lo[:, 2, :]), v[:, :, bass.ds(P * i, P)], pair_v(stage_hi[:, 2, :])).then_inc(sem["v_lo"], 1)

            conv_start(3, conv3)

            def head(i, s, n, ahead):
                def some_taps(r0):
                    for r in range(r0, r0 + 2):
                        conv_tap(3, 4 * n + r, conv3, conv3[:, :], taps[0] + 4 * n + r)
                if s == 0:
                    stage_v(i, 0, v_rows)
                dve.wait_ge(sem["z_done"], n + 1)
                for a, b in HALVES:
                    ts(zbuf[:, a:b], z[:, a:b], 40.0, None, ALU.min).then_inc(sem["zm_done"], 1)
                some_taps(0)
                for j, (a, b) in enumerate(HALVES):
                    dve.wait_ge(sem["l_done"], 2 * n + j + 1)
                    tt(zbuf[:, a:b], z[:, a:b], zbuf[:, a:b], ALU.max).then_inc(sem["sp_done"], 1)
                for j, (a, b) in enumerate(HALVES):
                    dve.wait_ge(sem["sph_done"], 2 * n + j + 1)
                    less(t_lo[:, a:b], zbuf[:, a:b], t_hi[:, a:b]).then_inc(sem["spl_done"], 1)
                some_taps(2)
                if not ahead() and s:
                    stage_qk(i + 1, 0, qkT, qkT)
                for j, (a, b) in enumerate(HALVES):
                    dve.wait_ge(sem["ah_done"], 2 * n + j + 1)
                    less(t_lo[:, a:b], zbuf[:, a:b], t_hi[:, a:b]).then_inc(sem["al_done"], 1)

            stage_qk(0, 0, qkT, qkT)
            run(st["gate"], head)
            for c in range(PAIRS):
                dve.wait_ge(sem["osp_hi"], c + 1)
                less(h_lo[:, 4 + c, :], qkT[:, c, :], h_hi[:, 4 + c, :]).then_inc(sem["osp_lo"], 1)

            def convolved(c):
                return u[:, c, PAD:PAD + S] if c < 3 else conv3[:, :]

            dve.wait_ge(sem["mean_done"], 1)
            for c in range(4):
                tt(convolved(c), convolved(c), mean[:, :], ALU.subtract).then_inc(sem["xc_done"], 1)

            def gate_att(i, s, k, ahead):
                ahead()
                if k == 3:
                    dve.wait_ge(sem["xc_done"], 4)
                    dve.wait_ge(sem["rs_done"], 2)
                    made(MADE["conv"], 4, convolved, lambda c: col("conv_ln_g", c), h_hi, h_lo, silu=True)
                dve.wait_ge(sem["gate_sig"], 1)
                arrived(st["att_out"], k, 0)
                tt(gates[:, DC + 2 * k, :], gates[:, DC + 2 * k, :], bank[2 * s], ALU.mult)
                arrived(st["att_out"], k, 1)
                free(st["att_out"], k, lambda: tt(gates[:, DC + 2 * k + 1, :], gates[:, DC + 2 * k + 1, :], bank[2 * s + 1], ALU.mult))

            run(st["att_out"], gate_att)
            dve.wait_ge(sem["mod_cols"], ADA_REST)
            tt(mod[:, 2 * DC:], mod_ps[:, 2 * DC:], col("ada_b", 2 * DC, 4 * DC), ALU.add).then_inc(sem["mod_done"], 1)
            dve.wait_ge(sem["mod_done"], 1)
            tt(gain[:, 1, :], mod[:, 2 * DC:3 * DC], col("post_mix_g", 0, DC), ALU.mult).then_inc(sem["gain_done"], 1)
            stt(gain[:, 2, :], mod[:, 4 * DC:5 * DC], 1.0, col("pre_ffn_g", 0, DC), ALU.add, ALU.mult).then_inc(sem["gain_done"], 1)
            tt(gain[:, 3, :], mod[:, 5 * DC:6 * DC], col("post_ffn_g", 0, DC), ALU.mult).then_inc(sem["gain_done"], 1)

            def merged(i, s, k, ahead):
                ahead()
                dve.wait_ge(sem["gate_sig"], 2)
                for t in range(2):
                    n = 2 * k + t
                    arrived(st["conv_out"], k, t)
                    gate = lambda: tt(gates[:, n, :], gates[:, n, :], bank[2 * s + t], ALU.mult)
                    if t == 0:
                        gate().then_inc(sem["merge_m"], 1)
                        dve.wait_ge(sem["merge_m"], k + 1)
                    else:
                        free(st["conv_out"], k, gate)
                        freed(st["conv_out"], k)
                    tt(gates[:, n, :], gates[:, n, :], gates[:, DC + n, :], ALU.add).then_inc(sem["mid_f"], 1)
                for t in range(2):
                    n = 2 * k + t
                    dve.wait_ge(sem["mid_hi_done"], n + 1)
                    less(mid_lo[:, n, :], gates[:, n, :], mid_hi[:, n, :]).then_inc(sem["mid_lo_done"], 1)

            def add_normed(base, done, g):
                for c in range(DC + 1):
                    if c < DC:
                        if c >= 2:
                            dve.wait_ge(sem["x_done"], base + c - 1)
                        stt(t_n[c % 2][:, :], y[:, c, :], gain[:, g, c:c + 1], rs[:, :], ALU.mult, ALU.mult).then_inc(sem["upd_step"], 1)
                    if c:
                        dve.wait_ge(sem["upd_step"], base + c)
                        tt(x[:, c - 1, :], x[:, c - 1, :], t_n[(c - 1) % 2][:, :], ALU.add).then_inc(sem["x_done"], 1)

            run(st["conv_out"], merged)
            run(st["mix_out"], lambda i, s, k, ahead: ahead())
            dve.wait_ge(sem["gain_done"], 4)
            dve.wait_ge(sem["rs_done"], 3)
            add_normed(0, 0, 1)
            dve.wait_ge(sem["x_done"], DC)
            dve.wait_ge(sem["rs_done"], 4)
            made(MADE["pre_ffn"], DC, lambda c: x[:, c, :], lambda c: gain[:, 2, c:c + 1], h_hi, h_lo,
                 lambda c: mod[:, 3 * DC + c:3 * DC + c + 1])

            def mid_low(m, k, s):
                dve.wait_ge(sem["mid_hi_done"], m + 1)
                less(chunk(mid_lo, k), act_p[s][:, :], chunk(mid_hi, k)).then_inc(sem["mid_lo_done"], 1)

            def gated(stage, part):
                def evac(i, s, k, ahead):
                    ahead()
                    dve.wait_ge(sem["mid_silu"], PART_AT[part] + k + 1)
                    arrived(stage, k, 1)
                    free(stage, k, lambda: tt(act_p[s][:, :], act_a[s][:, :], bank[2 * s + 1], ALU.mult))
                    mid_low(DC + PART_AT[part] + k, k, s)
                return evac

            def add_to(dst, stage):
                def evac(i, s, k, ahead):
                    ahead()
                    arrived(stage, k, 0)
                    tt(dst[:, 2 * k, :], dst[:, 2 * k, :], bank[2 * s], ALU.add)
                    arrived(stage, k, 1)
                    free(stage, k, lambda: tt(dst[:, 2 * k + 1, :], dst[:, 2 * k + 1, :], bank[2 * s + 1], ALU.add))
                return evac

            for r in range(3):
                run(st[f"ffn_in{r}"], gated(st[f"ffn_in{r}"], r))
                run(st[f"ffn_out{r}"], add_to(y, st[f"ffn_out{r}"]) if r else (lambda i, s, k, ahead: ahead()))
            dve.wait_ge(sem["rs_done"], 5)
            add_normed(DC, DC, 3)
            dve.wait_ge(sem["x_done"], 2 * DC)
            dve.wait_ge(sem["rs_done"], 6)
            made(MADE["attn2"], DC, lambda c: x[:, c, :], lambda c: col("attn_norm_w_2", c), h_hi, h_lo)

            def latent(i, s, k, ahead):
                ahead()
                if k:
                    arrived(st["latent"], 1, 1)
                    dve.wait_ge(sem["trig"], 4)
                    tt(rope_t[0][64:96, :], bank[2 * s + 1][64:96, :], cos_mla[64:96, :], ALU.mult).then_inc(sem["rope_m"], 1)
                    dve.wait_ge(sem["lat_done"], 2)
                    free(st["latent"], 1, lambda: tt(rope_t[1][64:96, :], bank[2 * s + 1][96:128, :], sin_mla[96:128, :], ALU.mult))
                    freed(st["latent"], 1)
                    dve.wait_ge(sem["rope_m"], 1)
                    tt(kpe[64:96, :], rope_t[0][64:96, :], rope_t[1][64:96, :], ALU.add).then_inc(sem["kpe_done"], 1)

            def rotary(i, s, k, ahead):
                ahead()
                for t in range(2):
                    n = 2 * k + t
                    if n >= 2:
                        dve.wait_ge(sem["rp_done"], n - 1)
                    elif n == 0:
                        dve.wait_ge(sem["kpe_done"], 1)
                    dve.wait_ge(sem["sw_done"], n + 1)
                    turn = lambda: tt(rope_t[t][:, :], bank[2 * s + t], cos_ret[:, :], ALU.mult)
                    if t == 0:
                        turn().then_inc(sem["rope_m"], 1)
                    else:
                        free(st["ret_qk"], k, turn)
                    tt(swapped[t][:, :], swapped[t][:, :], sin_ret[:, :], ALU.mult).then_inc(sem["rope_s"], 1)
                    if t == 0:
                        dve.wait_ge(sem["rope_m"], 1 + k + 1)
                    else:
                        freed(st["ret_qk"], k)
                    dve.wait_ge(sem["rope_s"], n + 1)
                    tt(rqk[:, n, :], rope_t[t][:, :], swapped[t][:, :], ALU.add).then_inc(sem["rp_done"], 1)

            only_ahead = lambda i, s, k, ahead: ahead()
            run(st["latent"], latent)
            run(st["ret_qk"], rotary)
            dve.wait_ge(sem["rs_done"], 7)
            made(MADE["lat"], 2, lambda c: lat[:, c, :], lambda c: col("mla_q_norm_w_2", c), lat_hi, lat_lo)
            dve.wait_ge(sem["rs_done"], 8)
            dve.wait_ge(sem["made_lo"], MADE["lat"] + 1)
            made(MADE["lat"] + 2, 1, lambda c: lat[:, 2, :], lambda c: col("mla_kv_norm_w_2"), lat_hi[:, 2:3], lat_lo[:, 2:3])
            run(st["ret_val"], only_ahead)
            run(st["ret_gate"], only_ahead)

            dve.wait_ge(sem["rp_done"], 2 * PAIRS)
            def ret_decay(i, s):
                n = 2 * i + s
                dve.wait_ge(sem["dec_done"], n + 1)
                dve.wait_ge(sem["rz_done"], n + 1)
                for kb in range(QB):
                    a, w = BLOCK_AT[kb], BLOCK_W[kb]
                    last = tt(rp[s][:, a:a + w], z2[s][:, a:a + w], decay[s][:, 0:w], ALU.mult)
                last.then_inc(sem["rp_f"], 1)

            def ret_low(i, s):
                dve.wait_ge(sem["rp_hi"], 2 * i + s + 1)
                less(r_lo[s][:, :], rp[s][:, :], r_hi[s][:, :]).then_inc(sem["rp_lo"], 1)

            def ret_pair(i, final=False):
                ret_decay(i, 0)
                ret_low(i, 0)
                stage_v(i, PAIRS, rv_rows)
                ret_decay(i, 1)
                if not final:
                    stage_qk(i + 1, PAIRS, rqk, rqk)
                ret_low(i, 1)

            stage_qk(0, PAIRS, rqk, rqk)
            with dve.Fori(0, PAIRS - 1) as i:
                ret_pair(i)
            ret_pair(PAIRS - 1, True)
            run(st["up_v"], only_ahead)
            dve.wait_ge(sem["ro_evac"], HEADS)
            for k in range(PAIRS):
                m = MADE["gn"] + k
                dve.wait_ge(sem["gn_mean"], k + 1)
                tt(rqk[:, k, :], rqk[:, k, :], o_ps, ALU.subtract).then_inc(sem["gn_xc"], 1)
                dve.wait_ge(sem["gn_xc"], k + 1)
                dve.wait_ge(sem["rs_done"], 8 + k + 1)
                normalised(m, rqk[:, k, :], col("ret_gn_w_2", k))
                dve.wait_ge(sem["tn_done"], m + 1)
                tt(h_f[m % 2][:, :], t_n[m % 2][:, :], rgate[:, k, :], ALU.mult).then_inc(sem["gn_y"], 1)
                dve.wait_ge(sem["made_hi"], m + 1)
                less(h_lo[:, k, :], h_f[m % 2][:, :], h_hi[:, k, :]).then_inc(sem["made_lo"], 1)

            def queries(i, s, k, ahead):
                ahead()
                for t in range(2):
                    h = 2 * k + t
                    dve.wait_ge(sem["mq_done"], h + 1)
                    if h:
                        dve.wait_ge(sem["qrope_done"], h)
                    tt(rope_t[0][64:96, :], bank[2 * s + t][64:96, :], cos_mla[64:96, :], ALU.mult).then_inc(sem["rope_m"], 1)
                    turn = lambda: tt(rope_t[1][64:96, :], bank[2 * s + t][96:128, :], sin_mla[96:128, :], ALU.mult)
                    if t == 0:
                        turn().then_inc(sem["rope_s"], 1)
                        dve.wait_ge(sem["rope_s"], 2 * PAIRS + k + 1)
                    else:
                        free(st["up_q"], k, turn)
                        freed(st["up_q"], k)
                    dve.wait_ge(sem["rope_m"], 1 + PAIRS + h + 1)
                    tt(mq[64:96, h, :], rope_t[0][64:96, :], rope_t[1][64:96, :], ALU.add).then_inc(sem["qrope_done"], 1)

            run(st["up_k"], only_ahead)
            run(st["up_q"], queries)
            for s in range(2):
                dve.wait_ge(sem["kst_hi"], s + 1)
                less(m_lo[64:96, 2 + s, :], kpe[64:96, :], m_hi[64:96, 2 + s, :]).then_inc(sem["kst_lo"], 1)
            dve.wait_ge(sem["qrope_done"], HEADS)
            def mla_qk(i, s):
                dve.wait_ge(sem["mqk_hi"], 4 * i + 2 * s + 1)
                less(m_lo[0:96, s, :], chunk(mq, 2 * i + s, slice(0, 96)), m_hi[0:96, s, :]).then_inc(sem["mqk_lo"], 1)
                dve.wait_ge(sem["mqk_hi"], 4 * i + 2 * s + 2)
                less(m_lo[0:HD, 2 + s, :], chunk(mk, 2 * i + s, slice(0, HD)), m_hi[0:HD, 2 + s, :]).then_inc(sem["mqk_lo"], 1)

            def mla_v(i):
                dve.wait_ge(sem["mv_hi"], i + 1)
                less(pair_v(m_lo[:, 4, :]), mv_rows[:, :, bass.ds(P * i, P)], pair_v(m_hi[:, 4, :])).then_inc(sem["mv_lo"], 1)

            def mla_max(i, s):
                n = 2 * i + s
                dve.wait_ge(sem["mz_done"], n + 1)
                for t in range(QB):
                    a, w = ROW_AT[t], ROW_W[t]
                    last = nc.vector.reduce_max(row_stat[:, s, t:t + 1], z2[s][:, a:a + w], AX.X)
                last.then_inc(sem["mx_done"], 1)
                dve.wait_ge(sem["mx_done"], n + 1)
                ts(row_stat[:, s, 4:8], row_stat[:, s, 0:4], -MLA_SCALE, None, ALU.mult).then_inc(sem["nmx_done"], 1)

            def mla_norm(i, s):
                n = 2 * i + s
                dve.wait_ge(sem["mp_done"], n + 1)
                nc.vector.reciprocal(row_stat[:, s, 12:16], row_stat[:, s, 8:12]).then_inc(sem["rcp_done"], 1)
                dve.wait_ge(sem["rcp_done"], n + 1)
                for t in range(QB):
                    a, w = ROW_AT[t], ROW_W[t]
                    last = ts(mp[s][:, a:a + w], mp[s][:, a:a + w], row_stat[:, s, 12 + t:13 + t], None, ALU.mult)
                last.then_inc(sem["pn_done"], 1)

            def mla_low(i, s):
                dve.wait_ge(sem["mth"], 2 * i + s + 1)
                less(mt_lo[s][:, :], z2[s][:, 0:ZW], r_hi[s][:, :]).then_inc(sem["mtl"], 1)

            def mla_period(i, first=False, final=False):
                mla_max(i, 0)
                if not first:
                    mla_low(i - 1, 1)
                mla_norm(i, 0)
                if not final:
                    mla_qk(i + 1, 0)
                mla_max(i, 1)
                mla_low(i, 0)
                mla_norm(i, 1)
                if not final:
                    mla_qk(i + 1, 1)
                mla_v(i)

            mla_qk(0, 0)
            mla_qk(0, 1)
            mla_period(0, first=True)
            with dve.Fori(1, PAIRS - 1) as i:
                mla_period(i)
            mla_period(PAIRS - 1, final=True)
            mla_low(PAIRS - 1, 1)
            for c in range(PAIRS):
                dve.wait_ge(sem["mos_hi"], c + 1)
                less(h_lo[:, 4 + c, :], mq[:, 2 * c, :], h_hi[:, 4 + c, :]).then_inc(sem["mos_lo"], 1)
            run(st["mix_out2"], add_to(x, st["mix_out2"]))
            freed(st["mix_out2"], 3)
            dve.wait_ge(sem["rs_done"], 13)
            made(MADE["ffn2"], DC, lambda c: x[:, c, :], lambda c: col("ffn_norm_w_2", c), h_hi, h_lo)

            def conv_gated(stage, part):
                def evac(i, s, k, ahead):
                    c0 = PART_AT[part] + k
                    ahead()
                    for t, buf in ((0, act_a[s]), (1, act_b[s])):
                        tap = lambda back: stt(buf[:, back:], bank[2 * s + t][:, 0:S - back],
                                               col("conv_w_2", ((2 - back) * 2 + t) * FC + c0), buf[:, back:], ALU.mult, ALU.add)
                        dve.wait_ge(sem["ident_done"], 2 * c0 + t + 1)
                        tap(1).then_inc(sem["conv2"], 1)
                        dve.wait_ge(sem["conv2"], 2 * c0 + t + 1)
                        if t == 0:
                            tap(2).then_inc(sem["silu_arg"], 1)
                        else:
                            free(stage, k, lambda: tap(2))
                    freed(stage, k)
                    dve.wait_ge(sem["mid_silu"], FC + c0 + 1)
                    tt(act_p[s][:, :], act_a[s][:, :], act_b[s][:, :], ALU.mult).then_inc(sem["mid_f"], 1)
                    mid_low(DC + FC + c0, k, s)
                return evac

            for r in range(3):
                run(st[f"up{r}"], conv_gated(st[f"up{r}"], r))
                run(st[f"down{r}"], add_to(x, st[f"down{r}"]))
            freed(st["down2"], 3)
            dve.wait_ge(sem["rs_done"], 14)
            for k in range(DC):
                stt(y[:, k, :], x[:, k, :], col("final_norm_w_2", k), rs[:, :], ALU.mult, ALU.mult).then_inc(sem["fin_done"], 1)

        @block.gpsimd
        def _(pool):
            tt, ts = nc.gpsimd.tensor_tensor, nc.gpsimd.tensor_scalar

            def sums(name):
                e, q0, n = NORMS[name]
                for q in range(q0, q0 + n):
                    pool.wait_ge(sem["sq_done"], q + 1)
                    if q == q0:
                        if e:
                            pool.wait_ge(sem["stat_done"], POOL_NORMS.index(name))
                        last = nc.gpsimd.tensor_copy(sq_sum[:, :], sq[q % 2][:, :])
                    else:
                        pool.wait_ge(sem["sum_done"], q)
                        last = tt(sq_sum[:, :], sq_sum[:, :], sq[q % 2][:, :], ALU.add)
                    last.then_inc(sem["sum_done"], 1)

            def ada_tile(a, slot, half):
                r = ada_raw[slot]
                pool.wait_ge(ada_full[slot], 16 * (half + 1))
                tt(r[:, :, :], r[:, :, :], c_act[:, :].unsqueeze(2).to_broadcast([P, 8, P]), ALU.mult).then_inc(sem["ada_step"], 1)
                for k, n in enumerate((4, 2, 1)):
                    pool.wait_ge(sem["ada_step"], 3 * a + k + 1)
                    if n > 1:
                        tt(r[:, 0:n], r[:, 0:n], r[:, n:2 * n], ALU.add).then_inc(sem["ada_step"], 1)
                if positive(a - 1):
                    pool.wait_ge(sem["mod_cols"], a - 1)
                tt(ada_acc[slot][:, :], r[:, 0, :], r[:, 1, :], ALU.add).then_inc(sem["ada_sum"], 1)

            sums("pre_mix")
            pool.wait_ge(sem["c_act"], 1)
            ada_tile(0, 0, 0)
            ada_tile(1, 1, 0)
            with pool.Fori(1, ADA_REST // 2) as i:
                ada_tile(2 * i, 0, i)
                ada_tile(2 * i + 1, 1, i)
            for name in ["conv_ln", "post_mix"]:
                sums(name)

            steps = [0]

            def step(ins):
                ins.then_inc(sem["ang_step"], 1)
                steps[0] += 1
                pool.wait_ge(sem["ang_step"], steps[0])

            pool.wait_ge(sem["in_pos"], 16)
            step(nc.gpsimd.tensor_copy(pos_f[:, :], pos_i[:, :]))
            for kind, sin_t, cos_t in (("ret", sin_ret, cos_ret), ("mla", sin_mla, cos_mla)):
                step(ts(angle[:, :], pos_f[:, :], scol("freq_" + kind), None, ALU.mult))
                step(ts(turns[:, :], angle[:, :], 1 / (2 * np.pi), MAGIC, ALU.mult, ALU.add))
                step(ts(turns[:, :], turns[:, :], MAGIC, None, ALU.subtract))
                for part in TWO_PI:
                    step(ts(sin_t[:, :], turns[:, :], part, None, ALU.mult))
                    step(tt(angle[:, :], angle[:, :], sin_t[:, :], ALU.subtract))
                step(ts(angle[:, :], angle[:, :], PI, -PI, ALU.min, ALU.max))
                ts(sin_t[:, :], angle[:, :], scol("sign_" + kind), None, ALU.mult).then_inc(sem["ang_arg"], 1)
                step(ts(turns[:, :], angle[:, :], 0.0, None, ALU.max))
                step(ts(angle[:, :], angle[:, :], 0.0, None, ALU.min))
                step(tt(turns[:, :], turns[:, :], angle[:, :], ALU.subtract))
                ts(cos_t[:, :], turns[:, :], -1.0, float(np.float32(np.pi / 2)), ALU.mult, ALU.add).then_inc(sem["ang_arg"], 1)

            for name in ["post_ffn", "c_q", "c_kv", "ffn2", "final"]:
                sums(name)


def packed(vectors):
    return np.ascontiguousarray(np.concatenate([v.reshape(-1, P).T for v in vectors], axis=1))


def shape_constants():
    p, f = np.arange(P)[:, None], np.arange(P)[None, :]
    mats = {"ident": p == f, "tri": -1.0 * (p >= f), "ones_neg": -np.ones((P, P)), "mask_kq": NEG * (p >= f),
            "mask_qk": NEG * (f > p), "ones": np.ones((P, P)), "block_mean": (p // HD == f // HD) / HD}
    j = np.arange(P)
    small = np.zeros((P, N_SMALL), np.float32)
    small[:, SMALL["eps"]] = EPS
    small[:, SMALL["freq_ret"]] = 10000.0 ** (-2.0 * (j % 32) / 64)
    small[:, SMALL["sign_ret"]] = np.where(j % 64 < 32, -1, 1)
    small[:, SMALL["freq_mla"]] = 10000.0 ** (-2.0 * (j % 16) / 32)
    small[:, SMALL["sign_mla"]] = np.where(j % 32 < 16, -1, 1)
    small[:, SMALL["log_gamma"]:SMALL["log_gamma"] + HEADS] = np.log1p(-2.0 ** (-5.0 - np.arange(HEADS)))
    lag = np.where(np.arange(S)[None, :] >= p, np.arange(S)[None, :] - p, 1e9)
    return np.stack([mats[n] for n in MATS], axis=1).astype(np.float32), small, lag.astype(np.float32)


def grouped(w, groups):
    rows, cols = w.shape
    return np.ascontiguousarray(w.reshape(rows // P, P, groups, 256).transpose(2, 1, 0, 3).reshape(groups, P, -1))


def stage_weights(a):
    def halves(w, width, first, n):
        return np.concatenate([w[:, half * width + P * c:half * width + P * c + P] for c in range(first, first + n) for half in range(2)], axis=1)

    w_in, w_in2 = a["w_in"][0], a["w_in_2"][0]
    w_uq = a["w_uq_2"][0].reshape(-1, HEADS, 96)
    w_ukv = a["w_ukv_2"][0].reshape(-1, HEADS, P)
    rope = w_in2[:, 2432:2464]
    out = {"glu": halves(w_in[:, 0:1024], 512, 0, 4), "qk": w_in[:, 1024:2048], "val": w_in[:, 2048:2560], "gate": w_in[:, 2560:],
           "att_out": a["w_att_out"][0], "conv_out": a["w_conv_out"][0], "mix_out": a["w_o"][0],
           "latent": np.concatenate([w_in2[:, 2048:2432], rope, rope, rope, rope[:, 16:], rope[:, :16]], axis=1),
           "ret_qk": w_in2[:, 0:1024], "ret_val": w_in2[:, 1024:1536], "ret_gate": w_in2[:, 1536:2048],
           "up_v": w_ukv[:, :, 64:].reshape(P, -1), "up_k": w_ukv[:, :, :64].reshape(P, -1),
           "up_q": np.concatenate([w_uq, w_uq[:, :, 80:96], w_uq[:, :, 64:80]], axis=2).reshape(256, -1), "mix_out2": a["w_out_2"][0]}
    for r, n in enumerate(FFN_PARTS):
        rows = slice(PART_AT[r] * P, (PART_AT[r] + n) * P)
        out[f"ffn_in{r}"] = halves(a["w_ffn_in"][0], FF, PART_AT[r], n)
        out[f"ffn_out{r}"] = a["w_ffn_out"][0][rows]
        out[f"up{r}"] = halves(a["w_up_2"][0], FF, PART_AT[r], n)
        out[f"down{r}"] = a["w_down_2"][0][rows]
    return {name: grouped(out[name], groups) for name, groups, _ in STAGES}


def kernel(**inputs):
    import concourse.bacc as bacc
    from concourse.bass_utils import run_bass_kernel_spmd

    a = {name: np.asarray(v) for name, v in inputs.items()}
    mats, small, lag = shape_constants()
    zero_tap = np.zeros((1, 4 * P), np.float32)
    vectors = dict(a, conv_w=np.concatenate([zero_tap, a["conv_w"][0]]).reshape(TAPS, 4, P).transpose(1, 0, 2))
    arrays = {"x": np.ascontiguousarray(a["x"][0].T.reshape(DC, P, S).transpose(1, 0, 2)),
              "ada": np.ascontiguousarray(a["ada_w"][0].reshape(DC, P, 6 * DC, P).transpose(2, 1, 0, 3)),
              "vec": packed([vectors[name] for name, _ in VECTORS]), "small": small, "mats": mats, "lag": lag,
              "positions": a["positions_2"].astype(np.int32, copy=False)}
    for name, w in stage_weights(a).items():
        arrays["w_" + name] = w
    nc = bacc.Bacc("TRN2", target_bir_lowering=False, num_devices=1)
    dram = {name: nc.dram_tensor(name, v.shape, mybir.dt.from_np(v.dtype), kind="ExternalInput").ap() for name, v in arrays.items()}
    out = nc.dram_tensor("out", (P, DC, S), F32, kind="ExternalOutput").ap()
    build(nc, dram, out)
    r = run_bass_kernel_spmd(nc, [arrays], core_ids=[0])
    got = np.asarray(r.results[0]["out"])
    return np.ascontiguousarray(got.transpose(1, 0, 2).reshape(1, D, S).transpose(0, 2, 1))
```

```python
from contextlib import ExitStack

import numpy as np
import concourse.bass as bass
from concourse import mybir

F32 = mybir.dt.float32
F32R = mybir.dt.float32r
I32 = mybir.dt.int32
ACT = mybir.ActivationFunctionType
ALU = mybir.AluOpType
AX = mybir.AxisListType

P = 128
S = 512
D = 1024
DC = D // P
FF = 2816
FC = FF // P
HEADS = 8
PAIRS = HEADS // 2
HD = 64
QB = S // P
EPS = 1e-6
MLA_SCALE = (64 + 32) ** -0.5
NEG = -1e30
TAPS = 32
PAD = TAPS - 1

STAGES = [
    ("glu", 4, 8), ("qk", 4, 8), ("val", 2, 8), ("gate", 8, 8),
    ("att_out", 4, 4), ("conv_out", 4, 4), ("mix_out", 4, 8),
    ("ffn_in0", 8, 8), ("ffn_out0", 4, 8), ("ffn_in1", 8, 8), ("ffn_out1", 4, 8), ("ffn_in2", 6, 8), ("ffn_out2", 4, 6),
    ("ret_qk", 4, 8), ("ret_val", 2, 8), ("latent", 2, 8), ("ret_gate", 2, 8),
    ("up_v", 2, 1), ("up_q", 4, 2), ("up_k", 2, 1), ("mix_out2", 4, 8),
    ("up0", 8, 8), ("down0", 4, 8), ("up1", 8, 8), ("down1", 4, 8), ("up2", 6, 8), ("down2", 4, 6),
]
FFN_PARTS = [8, 8, 6]
PART_AT = [0, 8, 16]
ADA_FIRST = 16
ADA_REST = 6 * DC - ADA_FIRST
SCALE_SUMS = [1, 2, 3, 4, 5, 6, 7]
SHIFT_SUMS = [1, 2, 3, 4, 5, 6]

VECTORS = [("c", DC), ("ada_b", 6 * DC), ("pre_mix_g", DC), ("post_mix_g", DC), ("pre_ffn_g", DC), ("post_ffn_g", DC),
           ("conv_w", 4 * TAPS), ("conv_b", 4), ("conv_ln_g", 4), ("conv_ln_b", 4),
           ("attn_norm_w_2", DC), ("ret_gn_w_2", PAIRS), ("mla_q_norm_w_2", 2), ("mla_kv_norm_w_2", 1),
           ("ffn_norm_w_2", DC), ("conv_w_2", 3 * 2 * FC), ("conv_b_2", 2 * FC), ("final_norm_w_2", DC)]
VEC, N_VEC = {}, 0
for _name, _n in VECTORS:
    VEC[_name] = N_VEC
    N_VEC += _n

MATS = ["ident", "tri", "ones_neg", "mask_kq", "mask_qk", "ones", "block_mean"]
SMALL = {"eps": 0, "freq_ret": 1, "sign_ret": 2, "freq_mla": 3, "sign_mla": 4, "log_gamma": 5}
N_SMALL = 16

BLOCK_AT = [0, 512, 1024, 896]
BLOCK_W = [S - kb * P for kb in range(QB)]
ZW = 1280
ROW_AT = [896, 1024, 512, 0]
ROW_W = [(t + 1) * P for t in range(QB)]
HALVES = [(0, 512), (512, ZW)]

NORMS = {}
_q = 0
for _e, (_name, _n) in enumerate([("pre_mix", 8), ("conv_ln", 4), ("post_mix", 8), ("pre_ffn", 8), ("post_ffn", 8),
                                  ("attn2", 8), ("c_kv", 1), ("c_q", 2), ("ffn2", 8), ("final", 8)]):
    NORMS[_name] = (_e, _q, _n)
    _q += _n
ADDED_NORMS = ["pre_mix", "conv_ln", "post_mix", "post_ffn", "attn2", "ffn2", "final"]
MADE = {"pre_mix": 0, "conv": 8, "pre_ffn": 12, "attn2": 20, "lat": 28, "gn": 31, "ffn2": 35}

MAGIC = 1.5 * 2.0 ** 23
TWO_PI = [6.28125, float(np.float32(0.0019350051879882812)), 2 * np.pi - 6.28125 - float(np.float32(0.0019350051879882812))]
PI = float(np.nextafter(np.float32(np.pi), np.float32(0)))


class Stage:

    def __init__(self, name, groups, chunks, first):
        self.name, self.n, self.kc, self.g0, self.next = name, groups, chunks, first, None


def plan():
    out, g = {}, 0
    for name, n, kc in STAGES:
        out[name] = Stage(name, n, kc, g)
        g += n
    order = list(out.values())
    for a, b in zip(order, order[1:]):
        a.next = b
    return out


def normed(m):
    return m + 1 - (DC if m >= MADE["lat"] else 0)


def positive(v):
    return not isinstance(v, int) or v > 0


def build(nc, dram, out):
    st = plan()
    off = [16512]

    def fixed(name, shape, dt=F32):
        size = int(np.prod(shape[1:])) * 4
        t = nc.alloc_sbuf_tensor_at(name, shape, dt, offset=off[0])
        off[0] += (size + 31) // 32 * 32
        return t

    x = fixed("x", [P, DC, S])
    h_hi, h_lo = (fixed(f"h_{p}", [P, DC, S], F32R) for p in ("hi", "lo"))
    raw = [fixed(f"raw{s}", [P, 8, 256]) for s in range(2)]
    w_hi = [fixed(f"w_hi{s}", [P, 8, 256], F32R) for s in range(2)]
    w_lo = [fixed(f"w_lo{s}", [P, 8, 256], F32R) for s in range(2)]
    vec, small = fixed("vec", [P, N_VEC]), fixed("small", [P, N_SMALL])
    mod, gain, c_act = fixed("mod", [P, 6 * DC]), fixed("gain", [P, 4, DC]), fixed("c_act", [P, DC])
    spare = fixed("spare", [P, 2])
    row_stat = fixed("row_stat", [P, 2, 16])
    rounded = fixed("rounded", [P, 5, P], F32R)
    ident, ones, block_mean = fixed("ident", [P, P]), fixed("ones", [P, P]), fixed("block_mean", [P, P])
    ident_r, tri_r, ones_neg_r, mask_kq_r, mask_qk_r = (rounded[:, k, :] for k in range(5))
    BASE = off[0]
    ROOM = 229344 - BASE

    def at(name, kb, shape, dt=F32):
        size = int(np.prod(shape[1:])) * 4
        assert kb * 1024 + size <= ROOM, (name, kb, size, ROOM)
        return nc.alloc_sbuf_tensor_at(name, shape, dt, offset=BASE + int(kb * 1024))

    ada_first = at("ada_first", 0, [P, ADA_FIRST, 8, P])
    const_raw = at("const_raw", 86.5, [P, 5, P])
    qkT = at("qkT", 0, [P, 2 * PAIRS, S])
    v_rows = at("v_rows", 16, [P, QB, S])
    zbuf = at("zbuf", 24, [P, ZW])
    ada_acc = [at(f"ada_acc_{s}", 29 + s / 2, [P, P]) for s in range(2)]
    conv_tmp = at("conv_tmp", 30, [P, S])
    gates = at("gates", 32, [P, 2 * DC, S])
    u = at("u", 64, [P, 4, PAD + S])
    conv3 = at("conv3", 72.5, [P, S])
    stage_hi = at("stage_hi", 74.5, [P, 3, S], F32R)
    stage_lo = at("stage_lo", 80.5, [P, 3, S], F32R)
    t_hi, t_lo = at("t_hi", 86.5, [P, ZW], F32R), at("t_lo", 91.5, [P, ZW], F32R)
    ada_raw = [at(f"ada_raw{s}", 96.5 + 4 * s, [P, 8, P]) for s in range(2)]
    glu_sig = [at(f"glu_sig{s}", 92.5 + 2 * s, [P, S]) for s in range(2)]
    sq = [at(f"sq{s}", 74.5 + 2 * s, [P, S]) for s in range(2)]
    sq_sum = at("sq_sum", 78.5, [P, S])
    rs = at("rs", 80.5, [P, S])
    t_n = [at(f"t_n{s}", 82.5 + 2 * s, [P, S]) for s in range(2)]
    h_f = [at(f"h_f{s}", 86.5 + 2 * s, [P, S]) for s in range(2)]
    mean, ln_ms = at("mean", 90.5, [P, S]), at("ln_ms", 92.5, [P, S])
    mid_hi, mid_lo = at("mid_hi", 0, [P, DC, S], F32R), at("mid_lo", 16, [P, DC, S], F32R)
    y = at("y", 32, [P, DC, S])
    act_a = [at(f"act_a{s}", 48 + 2 * s, [P, S]) for s in range(2)]
    act_b = [at(f"act_b{s}", 52 + 2 * s, [P, S]) for s in range(2)]
    act_p = [at(f"act_p{s}", 56 + 2 * s, [P, S]) for s in range(2)]
    cos_ret, sin_ret, cos_mla, sin_mla = (at(n, 61 + 2 * k, [P, S]) for k, n in
                                          enumerate(["cos_ret", "sin_ret", "cos_mla", "sin_mla"]))
    pos_i = at("pos_i", 94.5, [P, S], I32)
    pos_f, angle, turns = (at(n, 96.5 + 2 * k, [P, S]) for k, n in enumerate(["pos_f", "angle", "turns"]))
    rqk = at("rqk", 0, [P, 2 * PAIRS, S])
    rv_rows = at("rv_rows", 16, [P, QB, S])
    rgate = at("rgate", 24, [P, PAIRS, S])
    lat = at("lat", 32, [P, 3, S])
    rs_attn = at("rs_attn", 38, [P, S])
    lat_hi, lat_lo = at("lat_hi", 40, [P, 3, S], F32R), at("lat_lo", 46, [P, 3, S], F32R)
    swapped = [at(f"swapped{s}", 52 + 2 * s, [P, S]) for s in range(2)]
    lag = at("lag", 57, [P, S])
    decay = [at(f"decay{s}", kb, [P, S]) for s, kb in enumerate((61, 63, 52, 54))]
    rope_t = [at(f"rope_t{s}", 96.5 + 2 * s, [P, S]) for s in range(2)]
    kpe = at("kpe", 102.5, [P, S])
    rp = at("rp", 69, [P, ZW])
    r_hi = [t_hi, at("r_hi1", 96.5, [P, ZW], F32R)]
    mk, mv_rows, mq = at("mk", 16, [P, HEADS, S]), at("mv_rows", 32, [P, QB, S]), at("mq", 0, [P, HEADS, S])
    m_hi, m_lo = at("m_hi", 40, [P, 5, S], F32R), at("m_lo", 50, [P, 5, S], F32R)
    mp = [at("mp0", 74.5, [P, ZW]), at("mp1", 79.5, [P, ZW])]
    mt_lo = [t_lo, at("mt_lo1", 60, [P, ZW], F32R)]

    names = """in_const in_mats in_round in_vec in_x0 in_x1 in_lag in_pos ada_f0 ada_f1 ada_f2 ada_f3 ada_f4 ada_f5 ada_f6 ada_f7 ada_a0 ada_a1 raw_full0 raw_full1
        rounded c_act ada0_prod ada0_tree shift0_sum ada0_step scale0_sum mod0_cols mod0_done gain_first pads gain_done
        w_hi_done w_lo_done tile_done group_free
        sq_done sum_done stat_done ms_done rs_done tn_done hf_done made_hi made_lo upd_step x_even x_odd
        ada_step ada_sum mod_cols mod_done
        sig_done tap
        qk_hi qk_lo v_hi v_lo z_done zm_done e_done l_done sp_done sph_done spl_done cum_done a_done ah_done al_done o_done o_evac
        gate_sig osp_hi osp_lo mean_ps mean_done xc_done
        merge_m mid_silu mid_f mid_hi_done mid_lo_done
        ident_done conv2 silu_arg
        ang_step ang_arg trig sw_done rope_m rope_s rp_done lat_done kpe_raw kpe_done rs_tables rs_diag rs_col gate_raw
        rz_done dec_done rp_f rp_hi rp_lo ro_done ro_evac
        gn_mean gn_xc gn_sq gn_var gn_y
        mq_done qrope_done mqk_hi mqk_lo mv_hi mv_lo kst_hi kst_lo mz_done mx_done nmx_done mp_done rcp_done pn_done mt_done mth mtl
        mo_done mo_evac mos_hi mos_lo fin_done out_done""".split()

    with ExitStack() as ctx:
        sem = {n: ctx.enter_context(nc.semaphore(n)) for n in names}
        psum = ctx.enter_context(nc.psum_tensor("psum", [P, 8 * S], F32))
        bank = [psum[:, b * S:(b + 1) * S] for b in range(8)]
        z2 = [psum[:, 4 * S:7 * S], psum[:, 0:3 * S]]
        o2 = [bank[7], bank[3]]
        z, o_ps = z2[0], o2[0]
        mod_ps = z[:, ZW:ZW + 6 * DC]
        rs_col = row_stat[:, 0, 0:QB]
        raw_full = [sem["raw_full0"], sem["raw_full1"]]
        ada_full = [sem["ada_a0"], sem["ada_a1"]]
        block = ctx.enter_context(nc.Block())

        def col(name, k=0, n=1):
            return vec[:, bass.ds(VEC[name] + k, n)]

        def scol(name, k=0):
            return small[:, bass.ds(SMALL[name] + k, 1)]

        def rstds(name):
            return NORMS[name][0] + (PAIRS if name in ("ffn2", "final") else 0)

        def chunk(t, k, rows=slice(0, P)):
            return t[rows, bass.ds(k, 1), :].rearrange("p a n -> p (a n)")

        def pair_v(t):
            return t.rearrange("p (b n) -> p b n", b=QB)

        @block.sync
        def _(sp):
            sp.dma_start(small[:, :], dram["small"]).then_inc(sem["in_const"], 16)
            sp.dma_start(vec[:, :], dram["vec"]).then_inc(sem["in_vec"], 16)
            def load(stage, k, slot):
                g = stage.g0 + k
                if positive(g - 1):
                    sp.wait_ge(sem["w_lo_done"], g - 1)
                sp.dma_start(raw[slot][:, 0:stage.kc, :].rearrange("p k n -> p (k n)"),
                             dram["w_" + stage.name][bass.ds(k, 1)].rearrange("g p n -> p (g n)")).then_inc(raw_full[slot], 16)

            def load_ada(a, slot):
                if positive(a - 1):
                    sp.wait_ge(sem["ada_sum"], a - 1)
                sp.dma_start(ada_raw[slot][:, :, :].rearrange("p k n -> p (k n)"),
                             dram["ada"][bass.ds(ADA_FIRST + a, 1)].rearrange("g p k n -> p (g k n)")).then_inc(ada_full[slot], 16)

            def stage_loads(stage, ada=None, per=0):
                def body(i):
                    for s in range(2):
                        load(stage, 2 * i + s, s)
                        for r in range(per):
                            load_ada(ada + (2 * i + s) * per + r, r if per > 1 else s)
                with sp.Fori(0, stage.n // 2) as i:
                    body(i)

            def load_first(*chunks):
                for c in chunks:
                    for half in range(2):
                        sp.dma_start(ada_first[:, 2 * c + half], dram["ada"][half * DC + c]).then_inc(sem[f"ada_f{c}"], 16)

            for t, k in ((ident, 0), (ones, 5), (block_mean, 6)):
                sp.dma_start(t[:, :], dram["mats"][:, k, :]).then_inc(sem["in_mats"], 16)
            load_first(0, 1, 2, 3)
            for half in range(2):
                part = slice(half * DC // 2, (half + 1) * DC // 2)
                sp.dma_start(x[:, part, :], dram["x"][:, part, :]).then_inc(sem[f"in_x{half}"], 16)
            load(st["glu"], 0, 0)
            load_first(4, 5)
            load(st["glu"], 1, 1)
            load_first(6, 7)
            sp.dma_start(const_raw[:, :, :], dram["mats"][:, 0:5, :]).then_inc(sem["in_round"], 16)
            for s in range(2):
                load_ada(s, s)
            for k in range(2, st["glu"].n):
                load(st["glu"], k, k % 2)
                load_ada(k, k % 2)
            stage_loads(st["qk"], 4, 2)
            stage_loads(st["val"], 12, 2)
            stage_loads(st["gate"], 16, 2)
            stage_loads(st["att_out"])
            stage_loads(st["conv_out"])
            stage_loads(st["mix_out"])
            stage_loads(st["ffn_in0"])
            sp.wait_ge(sem["made_lo"], MADE["attn2"])
            sp.dma_start(pos_i[:, :], dram["positions"].to_broadcast([P, S])).then_inc(sem["in_pos"], 16)
            for name in ["ffn_out0", "ffn_in1", "ffn_out1", "ffn_in2", "ffn_out2"]:
                stage_loads(st[name])
            sp.wait_ge(sem["mid_lo_done"], 8 + FC)
            sp.dma_start(lag[:, :], dram["lag"]).then_inc(sem["in_lag"], 16)
            for name in ["ret_qk", "ret_val", "latent", "ret_gate", "up_v", "up_q", "up_k", "mix_out2",
                         "up0", "down0", "up1", "down1", "up2", "down2"]:
                stage_loads(st[name])
            for k in range(DC):
                sp.wait_ge(sem["fin_done"], k + 1)
                sp.dma_start(out[:, k], y[:, k]).then_inc(sem["out_done"], 16)
            sp.wait_ge(sem["out_done"], 16 * DC)

        @block.tensor
        def _(pe):
            mm = nc.tensor.matmul

            def o_ps_read(name):
                if NORMS[name][0]:
                    pe.wait_ge(sem["ms_done"], rstds(name))

            def stat_sum(name):
                e, q0, n = NORMS[name]
                pe.wait_ge(sem["sum_done"], q0 + n)
                o_ps_read(name)
                mm(o_ps, ones[:, :], sq_sum[:, :], start=True, stop=True).then_inc(sem["stat_done"], 1)

            def stat_chunks(name):
                e, q0, n = NORMS[name]
                o_ps_read(name)
                for c in range(n):
                    pe.wait_ge(sem["sq_done"], q0 + c + 1)
                    mm(o_ps, ones[:, :], sq[(q0 + c) % 2][:, :], start=(c == 0), stop=(c == n - 1)).then_inc(sem["sum_done"], 1)

            PASSES = 3

            def tile(stage, slot, t, x_hi, x_lo, k0=0, rows=False, ready=None, passes=range(PASSES)):
                ps, kc = bank[2 * slot + t], stage.kc
                for r in range(2 if rows else 1):
                    for n in passes:
                        w, xv = ((w_hi, x_hi), (w_lo, x_hi), (w_hi, x_lo))[n]
                        for k in range(kc):
                            if ready and n == 0 and slot == 0 and t == 0 and r == 0 and k >= ready[2]:
                                pe.wait_ge(sem[ready[0]], ready[1] + k - ready[2] + 1)
                            first, final = n == 0 and k == 0, n == PASSES - 1 and k == kc - 1
                            if rows:
                                b = 2 * t + r
                                last = mm(ps[:, r * 256:(r + 1) * 256], xv[:, k0 + k, b * P:(b + 1) * P], w[slot][:, k, :],
                                          start=first, stop=final)
                            else:
                                last = mm(ps, w[slot][:, k, t * P:(t + 1) * P], xv[:, k0 + k, :], start=first, stop=final)
                if passes[-1] == PASSES - 1:
                    last.then_inc(sem["tile_done"], 1)

            def first_group(stage, x_hi, x_lo, k0, ready):
                for k in range(stage.kc):
                    if k >= ready[2]:
                        pe.wait_ge(sem[ready[0]], ready[1] + k - ready[2] + 1)
                    for t in range(2):
                        for n, (w, xv) in enumerate(((w_hi, x_hi), (w_lo, x_hi), (w_hi, x_lo))):
                            last = mm(bank[t], w[0][:, k, t * P:(t + 1) * P], xv[:, k0 + k, :],
                                      start=(n == 0 and k == 0), stop=(n == 2 and k == stage.kc - 1))
                        if k == stage.kc - 1:
                            last.then_inc(sem["tile_done"], 1)

            def weights(g):
                pe.wait_ge(sem["w_lo_done"], g + 1)
                if positive(g - 1):
                    pe.wait_ge(sem["group_free"], g - 1)

            def mod_column(a, slot):
                pe.wait_ge(sem["ada_sum"], a + 1)
                mm(psum[:, bass.ds(4 * S + ZW + ADA_FIRST + a, 1)], ada_acc[slot][:, :], ones[:, 0:1], start=True, stop=True
                   ).then_inc(sem["mod_cols"], 1)

            def gemm(stage, x_hi, x_lo, k0=0, rows=False, ready=None, ada=0, per=0, steps=None):
                def group(i, s, first=False):
                    for r in range(per):
                        mod_column(ada + (2 * i + s) * per + r, r if per > 1 else s)
                    weights(stage.g0 + 2 * i + s)
                    if first and ready and not rows:
                        first_group(stage, x_hi, x_lo, k0, ready)
                    else:
                        for t in range(2):
                            tile(stage, s, t, x_hi, x_lo, k0, rows, ready if first else None)

                begin, end = steps or (0, stage.n // 2)
                if ready:
                    group(begin, 0, True)
                    group(begin, 1)
                    begin += 1
                if begin < end:
                    with pe.Fori(begin, end) as i:
                        group(i, 0)
                        group(i, 1)

            def scores(zz, q_rows, k_rows, q_at, k_at, hi, lo, start_mask):
                for kb in range(QB):
                    a, w = BLOCK_AT[kb], BLOCK_W[kb]
                    for n, (kk, qq) in enumerate(((hi, hi), (hi, lo), (lo, hi))):
                        last = mm(zz[:, a:a + w], kk[k_rows, k_at, kb * P:(kb + 1) * P], qq[q_rows, q_at, kb * P:S],
                                  start=(n == 0 and kb < 3), stop=(n == 2), skip_group_check=True)
                    if start_mask:
                        last = mm(zz[:, a:a + P], ident_r, mask_kq_r, start=False, stop=True, skip_group_check=True)
                return last

            def values(o, vs_hi, vs_lo, v_at, p_hi, p_lo):
                for kb in range(QB):
                    a, w = BLOCK_AT[kb], BLOCK_W[kb]
                    for n, (vv, aa) in enumerate(((vs_hi, p_hi), (vs_hi, p_lo), (vs_lo, p_hi))):
                        last = mm(o[:, kb * P:S], vv[:, v_at, kb * P:(kb + 1) * P], aa[:, a:a + w],
                                  start=(n == 0 and kb == 0), stop=(n == 2 and kb == QB - 1), skip_group_check=True)
                return last

            pe.wait_ge(sem["in_mats"], 48)

            def first_columns(c):
                if c >= 4:
                    pe.wait_ge(sem["mod0_done"], c - 3)
                if c not in SCALE_SUMS or c not in SHIFT_SUMS:
                    pe.wait_ge(sem[f"ada_f{c}"], 32)
                    pe.wait_ge(sem["c_act"], 1)
                if c in SCALE_SUMS:
                    pe.wait_ge(sem["scale0_sum"], SCALE_SUMS.index(c) + 1)
                if c in SHIFT_SUMS:
                    pe.wait_ge(sem["shift0_sum"], SHIFT_SUMS.index(c) + 1)
                for at_col, tile_at, parts in ((DC + c, 2 * c + 1, 2 if c in SCALE_SUMS else DC), (c, 2 * c, 1 if c in SHIFT_SUMS else DC)):
                    for k in range(parts):
                        last = mm(mod_ps[:, at_col:at_col + 1], ada_first[:, tile_at, k, :], c_act[:, k:k + 1] if parts == DC else ones[:, 0:1],
                                  start=(k == 0), stop=(k == parts - 1))
                last.then_inc(sem["mod0_cols"], 1)

            def first_products(g, k):
                if k == 0:
                    weights(g)
                if g == 0:
                    pe.wait_ge(sem["made_lo"], MADE["pre_mix"] + k + 1)
                for t in range(2):
                    for n, (w, xv) in enumerate(((w_hi, h_hi), (w_lo, h_hi), (w_hi, h_lo))):
                        last = mm(bank[2 * g + t], w[g][:, k, t * P:(t + 1) * P], xv[:, k, :],
                                  start=(n == 0 and k == 0), stop=(n == 2 and k == DC - 1))
                    if k == DC - 1:
                        last.then_inc(sem["tile_done"], 1)

            for c in range(4):
                first_columns(c)
            stat_sum("pre_mix")
            for k in range(2):
                first_products(0, k)
            first_columns(4)
            first_products(0, 2)
            first_columns(5)
            for g, k in ((0, 3), (0, 4), (1, 0), (1, 1), (0, 5)):
                first_products(g, k)
            first_columns(6)
            first_products(1, 2)
            first_columns(7)
            for g, k in ((1, 3), (0, 6), (1, 4), (0, 7), (1, 5), (1, 6), (1, 7)):
                first_products(g, k)
            pe.wait_ge(sem["mod0_done"], DC - 3)
            for a in range(2):
                mod_column(a, a)
            gemm(st["glu"], h_hi, h_lo, ada=0, per=1, steps=(1, 2))
            gemm(st["qk"], h_hi, h_lo, ada=4, per=2)
            gemm(st["val"], h_hi, h_lo, rows=True, ada=12, per=2)

            def head(i, s):
                rows, n = slice(HD * s, HD * s + HD), 2 * i + s
                for r in range(2):
                    mod_column(16 + n * 2 + r, r)
                if s == 0:
                    pe.wait_ge(sem["qk_lo"], 2 * i + 2)
                scores(z, rows, rows, 0, 1, stage_hi, stage_lo, True).then_inc(sem["z_done"], 1)
                weights(st["gate"].g0 + n)
                tile(st["gate"], s, 0, h_hi, h_lo)
                tile(st["gate"], s, 1, h_hi, h_lo, passes=range(1))
                pe.wait_ge(sem["spl_done"], 2 * n + 2)
                for kb in range(QB):
                    a, w = BLOCK_AT[kb], BLOCK_W[kb]
                    for part in (t_hi, t_lo):
                        last = mm(z[:, a:a + w], tri_r, part[:, a:a + w], start=False, stop=True, skip_group_check=True)
                        for later in range(kb + 1, QB):
                            a2, w2 = BLOCK_AT[later], BLOCK_W[later]
                            last = mm(z[:, a + w - w2:a + w], ones_neg_r, part[:, a2:a2 + w2], start=False, stop=True,
                                      skip_group_check=True)
                last.then_inc(sem["cum_done"], 1)
                tile(st["gate"], s, 1, h_hi, h_lo, passes=range(1, PASSES))
                pe.wait_ge(sem["al_done"], 2 * n + 2)
                if s == 0:
                    pe.wait_ge(sem["v_lo"], i + 1)
                else:
                    pe.wait_ge(sem["o_evac"], n)
                values(o_ps, stage_hi, stage_lo, 2, t_hi, t_lo).then_inc(sem["o_done"], 1)

            with pe.Fori(0, PAIRS) as i:
                for s in range(2):
                    head(i, s)
            pe.wait_ge(sem["tap"], 2 * TAPS + 2 * (TAPS + 1))
            pe.wait_ge(sem["o_evac"], HEADS)
            for k in range(4):
                last = mm(o_ps, ones[:, :], (u[:, k, PAD:PAD + S], conv_tmp[:, :], conv3[:, :])[max(0, k - 1)], start=(k == 0), stop=(k == 3))
            last.then_inc(sem["mean_ps"], 1)
            gemm(st["att_out"], h_hi, h_lo, k0=4, ready=("osp_lo", 0, 0), steps=(0, 1))
            stat_sum("conv_ln")
            gemm(st["att_out"], h_hi, h_lo, k0=4, steps=(1, 2))
            gemm(st["conv_out"], h_hi, h_lo, ready=("made_lo", MADE["conv"], 0))
            gemm(st["mix_out"], mid_hi, mid_lo, ready=("mid_lo_done", 0, 0))
            stat_sum("post_mix")
            stat_chunks("pre_ffn")
            for r, n in enumerate(FFN_PARTS):
                gemm(st[f"ffn_in{r}"], h_hi, h_lo, ready=("made_lo", MADE["pre_ffn"], 0) if r == 0 else None)
                gemm(st[f"ffn_out{r}"], mid_hi, mid_lo, ready=("mid_lo_done", 8 + PART_AT[r], 0))
            stat_sum("post_ffn")
            weights(st["ret_qk"].g0)
            first_group(st["ret_qk"], h_hi, h_lo, 0, ("made_lo", MADE["attn2"], 0))
            weights(st["ret_qk"].g0 + 1)
            tile(st["ret_qk"], 1, 0, h_hi, h_lo, passes=range(1))
            stat_sum("attn2")
            tile(st["ret_qk"], 1, 0, h_hi, h_lo, passes=range(1, PASSES))
            tile(st["ret_qk"], 1, 1, h_hi, h_lo)
            gemm(st["ret_qk"], h_hi, h_lo, steps=(1, 2))
            gemm(st["ret_val"], h_hi, h_lo, rows=True)

            for i, (stage, k) in enumerate(((st["latent"], 0), (st["latent"], 1), (st["ret_gate"], 0), (st["ret_gate"], 1))):
                for s in range(2):
                    rows, n = slice(HD * s, HD * s + HD), 2 * i + s
                    if s == 0:
                        pe.wait_ge(sem["qk_lo"], 2 * PAIRS + 2 * i + 2)
                    if n == 0:
                        pe.wait_ge(sem["ms_done"], 6)
                    scores(z, rows, rows, 0, 1, stage_hi, stage_lo, False).then_inc(sem["rz_done"], 1)
                    if s == 0:
                        weights(stage.g0 + k)
                    tile(stage, k, s, h_hi, h_lo)
                    if s == 0:
                        pe.wait_ge(sem["v_lo"], PAIRS + i + 1)
                    if n:
                        pe.wait_ge(sem["ro_evac"], n)
                    pe.wait_ge(sem["rp_lo"], n + 1)
                    values(o_ps, stage_hi, stage_lo, 2, t_hi, t_lo).then_inc(sem["ro_done"], 1)
            pe.wait_ge(sem["ro_evac"], HEADS)
            stat_chunks("c_kv")
            stat_chunks("c_q")
            gemm(st["up_v"], lat_hi, lat_lo, k0=2, rows=True, ready=("made_lo", MADE["lat"], 0))
            for k in range(PAIRS):
                c = PAIRS - 1 - k
                if k:
                    pe.wait_ge(sem["ms_done"], 8 + k)
                mm(o_ps, block_mean[:, :], rqk[:, c, :], start=True, stop=True).then_inc(sem["gn_mean"], 1)
                weights(st["up_q"].g0 + k)
                if k == 0:
                    for c in range(2):
                        pe.wait_ge(sem["made_lo"], MADE["lat"] + 1 + c + 1)
                tile(st["up_q"], k % 2, 0, lat_hi, lat_lo)
                pe.wait_ge(sem["gn_sq"], k + 1)
                mm(o_ps, block_mean[:, :], sq[k % 2][:, :], start=True, stop=True).then_inc(sem["gn_var"], 1)
                tile(st["up_q"], k % 2, 1, lat_hi, lat_lo)
            gemm(st["up_k"], lat_hi, lat_lo, k0=2)

            pe.wait_ge(sem["group_free"], st["mix_out2"].g0)
            def mla_scores(i, s):
                pe.wait_ge(sem["mqk_lo"], 4 * i + 2 * s + 2)
                if positive(2 * i + s - 1):
                    pe.wait_ge(sem["mtl"], 2 * i + s - 1)
                for t in range(QB):
                    a, w = ROW_AT[t], ROW_W[t]
                    for n, (qq, kk) in enumerate(((m_hi, m_hi), (m_hi, m_lo), (m_lo, m_hi))):
                        mm(z2[s][:, a:a + w], qq[0:96, s, t * P:(t + 1) * P], kk[0:96, 2 + s, 0:w],
                           start=(n == 0), stop=(n == 2), skip_group_check=True)
                    last = mm(z2[s][:, a + w - P:a + w], ident_r, mask_qk_r, start=False, stop=True, skip_group_check=True)
                last.then_inc(sem["mz_done"], 1)

            def mla_transpose(i, s):
                pe.wait_ge(sem["pn_done"], 2 * i + s + 1)
                for kb in range(QB):
                    for t in range(kb, QB):
                        a = BLOCK_AT[kb] + (t - kb) * P
                        last = nc.tensor.transpose(z2[s][:, a:a + P], mp[s][:, ROW_AT[t] + kb * P:ROW_AT[t] + (kb + 1) * P],
                                                   ident[:, :])
                last.then_inc(sem["mt_done"], 1)

            def mla_values(i, s):
                if s == 0:
                    pe.wait_ge(sem["mv_lo"], i + 1)
                pe.wait_ge(sem["mtl"], 2 * i + s + 1)
                values(o2[s], m_hi, m_lo, 4, r_hi[s], mt_lo[s]).then_inc(sem["mo_done"], 1)

            def mla_period(i):
                mla_scores(i, 0)
                mla_transpose(i - 1, 1)
                mla_values(i - 1, 0)
                mla_scores(i, 1)
                mla_transpose(i, 0)
                mla_values(i - 1, 1)

            for s in range(2):
                pe.wait_ge(sem["kst_lo"], s + 1)
                mla_scores(0, s)
            mla_transpose(0, 0)
            with pe.Fori(1, PAIRS) as i:
                mla_period(i)
            mla_transpose(PAIRS - 1, 1)
            mla_values(PAIRS - 1, 0)
            mla_values(PAIRS - 1, 1)
            pe.wait_ge(sem["mo_evac"], HEADS)
            pe.wait_ge(sem["made_lo"], MADE["gn"] + PAIRS)
            gemm(st["mix_out2"], h_hi, h_lo, ready=("mos_lo", 0, PAIRS))
            stat_sum("ffn2")
            for r, n in enumerate(FFN_PARTS):
                gemm(st[f"up{r}"], h_hi, h_lo, ready=("made_lo", MADE["ffn2"], 0) if r == 0 else None)
                gemm(st[f"down{r}"], mid_hi, mid_lo, ready=("mid_lo_done", 8 + FC + PART_AT[r], 0))
            stat_sum("final")

        @block.scalar
        def _(act):
            A = nc.scalar.activation
            hf = [0]
            norms = [0]

            def apart(n):
                A(spare[:, n:n + 1], small[:, 0:1], ACT.Copy)

            def split_hi(stage, k, slot, half):
                g = stage.g0 + k
                act.wait_ge(raw_full[slot], 16 * (stage.g0 // 2 + half + 1))
                if positive(g - 1):
                    act.wait_ge(sem["tile_done"], 2 * g - 2)
                A(w_hi[slot][:, 0:stage.kc, :], raw[slot][:, 0:stage.kc, :], ACT.Copy).then_inc(sem["w_hi_done"], 1)

            def run(stage, evac):
                def step(i, s, final=False):
                    def ahead():
                        if not (final and s):
                            split_hi(stage, 2 * i + s + 1, 1 - s, i + s)
                        elif stage.next:
                            split_hi(stage.next, 0, 0, 0)
                        return final
                    evac(i, s, 2 * i + s, ahead)
                n = stage.n // 2
                if n == 2:
                    step(0, 0)
                    step(0, 1)
                elif n > 2:
                    with act.Fori(0, n - 1) as i:
                        step(i, 0)
                        step(i, 1)
                step(n - 1, 0, True)
                step(n - 1, 1, True)

            def arrived(stage, k, t):
                act.wait_ge(sem["tile_done"], 2 * (stage.g0 + k) + t + 1)

            def free(stage, k, ins_of):
                if positive(stage.g0 + k):
                    act.wait_ge(sem["group_free"], stage.g0 + k)
                ins_of().then_inc(sem["group_free"], 1)

            def squares(name, of, wait, chunks=None):
                e, q0, n = NORMS[name]
                for c in chunks or range(n):
                    if q0 + c >= 2:
                        act.wait_ge(sem["sum_done"], q0 + c - 1)
                    wait(c)
                    A(sq[(q0 + c) % 2][:, :], of(c), ACT.Square).then_inc(sem["sq_done"], 1)

            def rstd(width, wait, load=True, dst=rs):
                if load:
                    nc.scalar.preload_act_table_set("natural_log_exp_and_others")
                wait()
                A(ln_ms[:, :], o_ps, ACT.Ln, scale=1.0 / width, bias=scol("eps")).then_inc(sem["ms_done"], 1)
                norms[0] += 1
                act.wait_ge(sem["ms_done"], norms[0])
                A(dst[:, :], ln_ms[:, :], ACT.Exp, scale=-0.5).then_inc(sem["rs_done"], 1)

            def norm_rstd(name, width, load=True, dst=rs):
                def wait():
                    if name in ADDED_NORMS:
                        act.wait_ge(sem["stat_done"], ADDED_NORMS.index(name) + 1)
                    else:
                        act.wait_ge(sem["sum_done"], NORMS[name][1] + NORMS[name][2])
                rstd(width, wait, load, dst)

            def made(m, dst, shift=None, func=None):
                src = t_n[m % 2]
                act.wait_ge(sem["tn_done"], normed(m))
                if func is not None:
                    if m >= 2:
                        act.wait_ge(sem["made_lo"], m - 1)
                    A(h_f[m % 2][:, :], src[:, :], func, bias=shift).then_inc(sem["hf_done"], 1)
                    hf[0] += 1
                    act.wait_ge(sem["hf_done"], hf[0])
                    src, shift = h_f[m % 2], None
                if shift is None:
                    A(dst, src[:, :], ACT.Copy).then_inc(sem["made_hi"], 1)
                else:
                    A(dst, src[:, :], ACT.Identity, bias=shift).then_inc(sem["made_hi"], 1)

            act.wait_ge(sem["in_vec"], 16)
            A(c_act[:, :], col("c", 0, DC), ACT.Silu).then_inc(sem["c_act"], 1)
            act.wait_ge(sem["c_act"], 1)

            def first_products(c):
                act.wait_ge(sem[f"ada_f{c}"], 32)
                for k in range(DC):
                    part = ada_first[:, 2 * c, k, :]
                    last = A(part, part, ACT.Copy, scale=c_act[:, k:k + 1])
                last.then_inc(sem["ada0_prod"], 1)

            nc.scalar.preload_act_table_set("natural_log_exp_and_others")
            for c in SHIFT_SUMS[:3]:
                first_products(c)
            for half in range(2):
                act.wait_ge(sem[f"in_x{half}"], 16)
                squares("pre_mix", lambda c: x[:, c, :], lambda c: None, range(half * DC // 2, (half + 1) * DC // 2))
            split_hi(st["glu"], 0, 0, 0)
            act.wait_ge(sem["in_const"], 16)
            norm_rstd("pre_mix", D, load=False)
            for c in range(DC):
                if c in (2, 3):
                    first_products(c + 2)
                if c == 5:
                    split_hi(st["glu"], 1, 1, 0)
                if c == 6:
                    first_products(6)
                act.wait_ge(sem["mod0_done"], max(1, c - 2))
                made(MADE["pre_mix"] + c, h_hi[:, c, :], mod[:, c:c + 1])
            act.wait_ge(sem["in_round"], 16)
            A(rounded[:, :, :], const_raw[:, :, :], ACT.Copy).then_inc(sem["rounded"], 1)

            def glu(i, s, k, ahead):
                if k == 0:
                    split_hi(st["glu"], 2, 0, 1)
                elif k > 1:
                    ahead()
                arrived(st["glu"], k, 1)
                if positive(k - 1):
                    act.wait_ge(sem["group_free"], k - 1)
                A(glu_sig[s][:, :], bank[2 * s + 1], ACT.Sigmoid).then_inc(sem["sig_done"], 1)

            def qk(i, s, k, ahead):
                ahead()
                arrived(st["qk"], k, 0)
                A(qkT[:, 2 * k, :], bank[2 * s], ACT.Copy)
                arrived(st["qk"], k, 1)
                free(st["qk"], k, lambda: A(qkT[:, 2 * k + 1, :], bank[2 * s + 1], ACT.Copy))

            def rows_of(stage, dst):
                def evac(i, s, k, ahead):
                    ahead()
                    cols = slice(256 * k, 256 * k + 256)
                    arrived(stage, k, 0)
                    A(dst[:, 0:2, cols], bank[2 * s].rearrange("p (b n) -> p b n", b=2), ACT.Copy)
                    arrived(stage, k, 1)
                    free(stage, k, lambda: A(dst[:, 2:4, cols], bank[2 * s + 1].rearrange("p (b n) -> p b n", b=2), ACT.Copy))
                return evac

            run(st["glu"], glu)
            run(st["qk"], qk)
            run(st["val"], rows_of(st["val"], v_rows))

            def stage_qk(i, q, k):
                A(stage_hi[:, 0, :], chunk(q, i), ACT.Copy, scale=HD ** -0.5).then_inc(sem["qk_hi"], 1)
                A(stage_hi[:, 1, :], chunk(k, PAIRS + i), ACT.Copy).then_inc(sem["qk_hi"], 1)

            def stage_v(i, v):
                A(pair_v(stage_hi[:, 2, :]), v[:, :, bass.ds(P * i, P)], ACT.Copy).then_inc(sem["v_hi"], 1)

            def head(i, s, n, ahead):
                rows, g = slice(HD * s, HD * s + HD), st["gate"].g0 + n
                if s == 0:
                    stage_v(i, v_rows)
                for j, (a, b) in enumerate(HALVES):
                    act.wait_ge(sem["zm_done"], 2 * n + j + 1)
                    A(zbuf[:, a:b], zbuf[:, a:b], ACT.Exp).then_inc(sem["e_done"], 1)
                for j, (a, b) in enumerate(HALVES):
                    act.wait_ge(sem["e_done"], 2 * n + j + 1)
                    A(zbuf[:, a:b], zbuf[:, a:b], ACT.Ln, bias=1.0).then_inc(sem["l_done"], 1)
                for j, (a, b) in enumerate(HALVES):
                    act.wait_ge(sem["sp_done"], 2 * n + j + 1)
                    A(t_hi[:, a:b], zbuf[:, a:b], ACT.Copy).then_inc(sem["sph_done"], 1)
                arrived(st["gate"], n, 0)
                A(chunk(gates, 2 * n), bank[2 * s], ACT.Copy)
                if not ahead() and s:
                    stage_qk(i + 1, qkT, qkT)
                for j, (a, b) in enumerate(HALVES):
                    act.wait_ge(sem["cum_done"], n + 1)
                    A(zbuf[:, a:b], z[:, a:b], ACT.Exp).then_inc(sem["a_done"], 1)
                for j, (a, b) in enumerate(HALVES):
                    act.wait_ge(sem["a_done"], 2 * n + j + 1)
                    A(t_hi[:, a:b], zbuf[:, a:b], ACT.Copy).then_inc(sem["ah_done"], 1)
                arrived(st["gate"], n, 1)
                free(st["gate"], n, lambda: A(chunk(gates, 2 * n + 1), bank[2 * s + 1], ACT.Copy))
                act.wait_ge(sem["o_done"], n + 1)
                apart(0)
                A(chunk(qkT, i, rows), o_ps[rows, :], ACT.Copy).then_inc(sem["o_evac"], 1)

            nc.scalar.preload_act_table_set("natural_log_exp_and_others")
            act.wait_ge(sem["group_free"], st["gate"].g0)
            stage_qk(0, qkT, qkT)
            run(st["gate"], head)
            act.wait_ge(sem["o_evac"], HEADS)
            for c in range(4):
                A(h_hi[:, 4 + c, :], qkT[:, c, :], ACT.Copy).then_inc(sem["osp_hi"], 1)
            act.wait_ge(sem["mean_ps"], 1)
            A(mean[:, :], o_ps, ACT.Copy, scale=1.0 / (4 * P)).then_inc(sem["mean_done"], 1)

            def att_out(i, s, k, ahead):
                if k < 3:
                    ahead()
                if k == 0:
                    act.wait_ge(sem["group_free"], st["att_out"].g0)
                    A(gates[:, DC:, :], gates[:, DC:, :], ACT.Sigmoid).then_inc(sem["gate_sig"], 1)
                elif k == 1:
                    squares("conv_ln", lambda c: (u[:, c, PAD:PAD + S], conv_tmp[:, :], conv3[:, :])[max(0, c - 1)],
                            lambda c: act.wait_ge(sem["xc_done"], c + 1))
                elif k == 2:
                    norm_rstd("conv_ln", 4 * P)
                else:
                    for c in range(4):
                        made(MADE["conv"] + c, h_hi[:, c, :], col("conv_ln_b", c), ACT.Silu)
                    ahead()
                    A(gates[:, 0:DC, :], gates[:, 0:DC, :], ACT.Sigmoid).then_inc(sem["gate_sig"], 1)

            run(st["att_out"], att_out)

            def merged(i, s, k, ahead):
                ahead()
                for t in range(2):
                    n = 2 * k + t
                    act.wait_ge(sem["mid_f"], n + 1)
                    A(mid_hi[:, n, :], gates[:, n, :], ACT.Copy).then_inc(sem["mid_hi_done"], 1)

            def to_y(stage, norm=None):
                def evac(i, s, k, ahead):
                    ahead()
                    for t in range(2):
                        n = 2 * k + t
                        arrived(stage, k, t)
                        if norm:
                            squares(norm, lambda c: bank[2 * s + t], lambda c: None, [n])
                        copy = lambda: A(y[:, n, :], bank[2 * s + t], ACT.Copy)
                        if t == 0:
                            copy()
                        else:
                            free(stage, k, copy)
                return evac

            def squares_after(stage, norm, of):
                def evac(i, s, k, ahead):
                    ahead()
                    act.wait_ge(sem["group_free"], stage.g0 + k + 1)
                    squares(norm, of, lambda c: None, [2 * k, 2 * k + 1])
                return evac

            run(st["conv_out"], merged)
            run(st["mix_out"], to_y(st["mix_out"], "post_mix"))
            norm_rstd("post_mix", D)
            def x_chunk(pairs):
                return lambda c: act.wait_ge(sem["x_odd" if c % 2 else "x_even"], pairs + c // 2 + 1)

            squares("pre_ffn", lambda c: x[:, c, :], x_chunk(0))
            norm_rstd("pre_ffn", D, load=False)
            act.wait_ge(sem["mod_done"], 1)
            for c in range(DC):
                made(MADE["pre_ffn"] + c, h_hi[:, c, :], mod[:, 3 * DC + c:3 * DC + c + 1])

            def gated(stage):
                def evac(i, s, k, ahead):
                    ahead()
                    arrived(stage, k, 0)
                    act.wait_ge(sem["group_free"], stage.g0 + k - 1)
                    A(act_a[s][:, :], bank[2 * s], ACT.Silu).then_inc(sem["mid_silu"], 1)
                    act.wait_ge(sem["group_free"], stage.g0 + k + 1)
                    A(chunk(mid_hi, k), act_p[s][:, :], ACT.Copy
                      ).then_inc(sem["mid_hi_done"], 1)
                return evac

            for r in range(3):
                run(st[f"ffn_in{r}"], gated(st[f"ffn_in{r}"]))
                if r == 1:
                    for k, table in enumerate((sin_ret, cos_ret, sin_mla, cos_mla)):
                        act.wait_ge(sem["ang_arg"], k + 1)
                        A(table[:, :], table[:, :], ACT.Sin).then_inc(sem["trig"], 1)
                run(st[f"ffn_out{r}"], (to_y(st["ffn_out0"]), lambda i, s, k, ahead: ahead(),
                                        squares_after(st["ffn_out2"], "post_ffn", lambda c: y[:, c, :]))[r])
            norm_rstd("post_ffn", D)
            for c in range(DC):
                squares("attn2", lambda c: x[:, c, :], x_chunk(DC // 2), [c])
                A(h_hi[:, c, :], x[:, c, :], ACT.Copy, scale=col("attn_norm_w_2", c)).then_inc(sem["made_hi"], 1)

            def rotary(i, s, k, ahead):
                ahead()
                if k == 0:
                    norm_rstd("attn2", D, load=False, dst=rs_attn)
                for t in range(2):
                    arrived(st["ret_qk"], k, t)
                    if k:
                        act.wait_ge(sem["rp_done"], 2 * (k - 1) + t + 1)
                    for b in range(4):
                        last = A(swapped[t][32 * b:32 * b + 32, :], bank[2 * s + t][32 * (b ^ 1):32 * (b ^ 1) + 32, :], ACT.Copy)
                    last.then_inc(sem["sw_done"], 1)

            run(st["ret_qk"], rotary)
            def values_by_rs(i, s, k, ahead):
                ahead()
                if k == 0:
                    act.wait_ge(sem["rs_col"], 1)
                for b in range(QB):
                    if b % 2 == 0:
                        arrived(st["ret_val"], k, b // 2)
                    copy = lambda: A(rv_rows[:, b, 256 * k:256 * k + 256], bank[2 * s + b // 2][:, b % 2 * 256:b % 2 * 256 + 256],
                                     ACT.Copy, scale=rs_col[:, b:b + 1])
                    if b < QB - 1:
                        copy()
                    else:
                        free(st["ret_val"], k, copy)

            run(st["ret_val"], values_by_rs)

            def decays(n):
                A(decay[n % 4][:, :], lag[:, :], ACT.Exp, scale=scol("log_gamma", n)).then_inc(sem["dec_done"], 1)

            def ret_pair(stage, i0, beside):
                def evac(_, slot, k, ahead):
                    i = i0 + k
                    for s in range(2):
                        rows, n = slice(HD * s, HD * s + HD), 2 * i + s
                        act.wait_ge(sem["rp_f"], n + 1)
                        A(t_hi[:, :], rp[:, :], ACT.Copy).then_inc(sem["rp_hi"], 1)
                        if s == 0:
                            ahead()
                        elif i < PAIRS - 1:
                            stage_qk(i + 1, rqk, rqk)
                        if n < 4:
                            decays(n + 4)
                        if beside:
                            beside(k, s)
                        act.wait_ge(sem["ro_done"], n + 1)
                        A(rqk[rows, i, :], o_ps[rows, :], ACT.Copy).then_inc(sem["ro_evac"], 1)
                    if i < PAIRS - 1:
                        stage_v(i + 1, rv_rows)
                return evac

            def ret_gate(k, t):
                if t:
                    act.wait_ge(sem["group_free"], st["ret_gate"].g0 + k + 1)
                else:
                    act.wait_ge(sem["gate_raw"], k + 1)
                A(rgate[:, 2 * k + t, :], rgate[:, 2 * k + t, :], ACT.Silu)

            nc.scalar.preload_act_table_set("natural_log_exp_and_others")
            act.wait_ge(sem["rp_done"], 2 * PAIRS)
            act.wait_ge(sem["group_free"], st["latent"].g0)
            act.wait_ge(sem["in_lag"], 16)
            stage_qk(0, rqk, rqk)
            stage_v(0, rv_rows)
            for n in range(4):
                decays(n)
            run(st["latent"], ret_pair(st["latent"], 0, None))
            run(st["ret_gate"], ret_pair(st["ret_gate"], 2, ret_gate))
            act.wait_ge(sem["lat_done"], 2)
            squares("c_kv", lambda c: lat[:, 2, :], lambda c: None)
            squares("c_q", lambda c: lat[:, c, :], lambda c: None)
            norm_rstd("c_kv", P)
            made(MADE["lat"], lat_hi[:, 2, :])
            norm_rstd("c_q", 2 * P, load=False)
            for c in range(2):
                made(MADE["lat"] + 1 + c, lat_hi[:, c, :])
            run(st["up_v"], rows_of(st["up_v"], mv_rows))
            def keys(i, s, k, ahead):
                ahead()
                for t in range(2):
                    arrived(st["up_k"], k, t)
                    A(mk[0:HD, 2 * (2 * k + t), :], bank[2 * s + t][0:HD, :], ACT.Copy)
                    odd = lambda: A(mk[0:HD, 2 * (2 * k + t) + 1, :], bank[2 * s + t][HD:P, :], ACT.Copy)
                    if t == 0:
                        odd()
                    else:
                        free(st["up_k"], k, odd)

            def queries(i, s, k, ahead):
                m, c = MADE["gn"] + k, PAIRS - 1 - k
                ahead()
                act.wait_ge(sem["gn_xc"], k + 1)
                A(sq[k % 2][:, :], rqk[:, c, :], ACT.Square).then_inc(sem["gn_sq"], 1)
                if k:
                    act.wait_ge(sem["tn_done"], normed(m - 1))
                rstd(1.0, lambda: act.wait_ge(sem["gn_var"], k + 1), load=(k == 0))
                act.wait_ge(sem["gn_y"], k + 1)
                A(h_hi[:, c, :], h_f[m % 2][:, :], ACT.Copy).then_inc(sem["made_hi"], 1)
                for t in range(2):
                    arrived(st["up_q"], k, t)
                    A(mq[0:HD, 2 * c + t, :], bank[2 * s + t][0:HD, :], ACT.Copy).then_inc(sem["mq_done"], 1)

            run(st["up_q"], queries)
            run(st["up_k"], keys)
            act.wait_ge(sem["kpe_done"], 1)
            act.wait_ge(sem["group_free"], st["mix_out2"].g0)
            act.wait_ge(sem["qrope_done"], HEADS)
            def mla_qk(i, s):
                A(m_hi[0:96, s, :], chunk(mq, 2 * i + s, slice(0, 96)), ACT.Copy).then_inc(sem["mqk_hi"], 1)
                A(m_hi[0:HD, 2 + s, :], chunk(mk, 2 * i + s, slice(0, HD)), ACT.Copy).then_inc(sem["mqk_hi"], 1)

            def mla_v(i):
                A(pair_v(m_hi[:, 4, :]), mv_rows[:, :, bass.ds(P * i, P)], ACT.Copy).then_inc(sem["mv_hi"], 1)

            def mla_exp(i, s):
                act.wait_ge(sem["nmx_done"], 2 * i + s + 1)
                for t in range(QB):
                    a, w = ROW_AT[t], ROW_W[t]
                    last = A(mp[s][:, a:a + w], z2[s][:, a:a + w], ACT.Exp, scale=MLA_SCALE, bias=row_stat[:, s, 4 + t:5 + t],
                             accum_out=row_stat[:, s, 8 + t:9 + t])
                last.then_inc(sem["mp_done"], 1)

            def mla_high(i, s):
                act.wait_ge(sem["mt_done"], 2 * i + s + 1)
                A(r_hi[s][:, :], z2[s][:, 0:ZW], ACT.Copy).then_inc(sem["mth"], 1)

            def mla_out(i, s):
                rows = slice(HD * s, HD * s + HD)
                act.wait_ge(sem["mo_done"], 2 * i + s + 1)
                apart(s)
                A(chunk(mq, 2 * i, rows), o2[s][rows, :], ACT.Copy).then_inc(sem["mo_evac"], 1)

            def mla_period(i, first=False, final=False):
                if not first:
                    mla_high(i - 1, 1)
                mla_exp(i, 0)
                if not final:
                    mla_qk(i + 1, 0)
                if not first:
                    mla_out(i - 1, 0)
                mla_high(i, 0)
                mla_exp(i, 1)
                if not final:
                    mla_qk(i + 1, 1)
                if not first:
                    mla_out(i - 1, 1)
                mla_v(i)

            for s in range(2):
                A(m_hi[64:96, 2 + s, :], kpe[64:96, :], ACT.Copy).then_inc(sem["kst_hi"], 1)
                mla_qk(0, s)
            mla_period(0, first=True)
            with act.Fori(1, PAIRS - 1) as i:
                mla_period(i)
            mla_period(PAIRS - 1, final=True)
            mla_high(PAIRS - 1, 1)
            mla_out(PAIRS - 1, 0)
            mla_out(PAIRS - 1, 1)
            act.wait_ge(sem["mo_evac"], HEADS)
            for c in range(4):
                A(h_hi[:, 4 + c, :], mq[:, 2 * c, :], ACT.Copy).then_inc(sem["mos_hi"], 1)
            run(st["mix_out2"], squares_after(st["mix_out2"], "ffn2", lambda c: x[:, c, :]))
            norm_rstd("ffn2", D)
            for c in range(DC):
                made(MADE["ffn2"] + c, h_hi[:, c, :])

            def conv_gated(stage, part):
                def evac(i, s, k, ahead):
                    c0 = PART_AT[part] + k
                    chan = c0
                    ahead()
                    act.wait_ge(sem["mid_f"], DC + c0 - 1)
                    for t, buf in ((0, act_a[s]), (1, act_b[s])):
                        arrived(stage, k, t)
                        A(buf[:, :], bank[2 * s + t], ACT.Identity, scale=col("conv_w_2", 2 * 2 * FC + t * FC + chan),
                          bias=col("conv_b_2", t * FC + chan)).then_inc(sem["ident_done"], 1)
                    act.wait_ge(sem["silu_arg"], c0 + 1)
                    A(act_a[s][:, :], act_a[s][:, :], ACT.Silu).then_inc(sem["mid_silu"], 1)
                    act.wait_ge(sem["mid_f"], DC + c0 + 1)
                    A(chunk(mid_hi, k), act_p[s][:, :], ACT.Copy
                      ).then_inc(sem["mid_hi_done"], 1)
                return evac

            for r in range(3):
                run(st[f"up{r}"], conv_gated(st[f"up{r}"], r))
                run(st[f"down{r}"], squares_after(st["down2"], "final", lambda c: x[:, c, :]) if r == 2
                    else (lambda i, s, k, ahead: ahead()))
            norm_rstd("final", D)

        @block.vector
        def _(dve):
            tt, ts, stt = nc.vector.tensor_tensor, nc.vector.tensor_scalar, nc.vector.scalar_tensor_tensor
            taps = [0]

            def less(out_lo, full, high):
                return tt(out_lo, full, high.bitcast(F32), ALU.subtract)

            def split_lo(stage, k, slot):
                dve.wait_ge(sem["w_hi_done"], stage.g0 + k + 1)
                less(w_lo[slot][:, 0:stage.kc, :], raw[slot][:, 0:stage.kc, :], w_hi[slot][:, 0:stage.kc, :]
                     ).then_inc(sem["w_lo_done"], 1)

            def run(stage, evac):
                def step(i, s, final=False):
                    def ahead():
                        if not (final and s):
                            split_lo(stage, 2 * i + s + 1, 1 - s)
                        elif stage.next:
                            split_lo(stage.next, 0, 0)
                        return final
                    evac(i, s, 2 * i + s, ahead)
                n = stage.n // 2
                if n == 2:
                    step(0, 0)
                    step(0, 1)
                elif n > 2:
                    with dve.Fori(0, n - 1) as i:
                        step(i, 0)
                        step(i, 1)
                step(n - 1, 0, True)
                step(n - 1, 1, True)

            def arrived(stage, k, t):
                dve.wait_ge(sem["tile_done"], 2 * (stage.g0 + k) + t + 1)

            def free(stage, k, ins_of):
                if positive(stage.g0 + k):
                    dve.wait_ge(sem["group_free"], stage.g0 + k)
                ins_of().then_inc(sem["group_free"], 1)

            def freed(stage, k):
                dve.wait_ge(sem["group_free"], stage.g0 + k + 1)

            def normalised(m, src, g):
                stt(t_n[m % 2][:, :], src, g, rs[:, :], ALU.mult, ALU.mult).then_inc(sem["tn_done"], 1)

            def made(m0, n, src, g, dst_hi, dst_lo, shift=None, silu=False):
                for c in range(n + 1):
                    if c < n:
                        if c >= 2:
                            dve.wait_ge(sem["made_lo"], m0 + c - 1)
                        normalised(m0 + c, src(c), g(c))
                    if c:
                        m = m0 + c - 1
                        dve.wait_ge(sem["made_hi"], m + 1)
                        full = (h_f if silu else t_n)[m % 2]
                        if shift:
                            last = stt(dst_lo[:, c - 1, :], full[:, :], shift(c - 1), dst_hi[:, c - 1, :].bitcast(F32), ALU.add, ALU.subtract)
                        else:
                            last = less(dst_lo[:, c - 1, :], full[:, :], dst_hi[:, c - 1, :])
                        last.then_inc(sem["made_lo"], 1)

            nc.vector.memset(u[:, :, 0:PAD], 0.0).then_inc(sem["pads"], 1)
            dve.wait_ge(sem["in_vec"], 16)
            dve.wait_ge(sem["c_act"], 1)

            def scale_sums(c):
                dve.wait_ge(sem[f"ada_f{c}"], 32)
                for k in range(DC):
                    part, acc = ada_first[:, 2 * c + 1, k, :], ada_first[:, 2 * c + 1, k % 2, :]
                    if k < 2:
                        last = ts(acc, part, c_act[:, k:k + 1], None, ALU.mult)
                    else:
                        dve.wait_ge(sem["ada0_step"], 7 * SCALE_SUMS.index(c) + k - 1)
                        last = stt(acc, part, c_act[:, k:k + 1], acc, ALU.mult, ALU.add)
                    last.then_inc(sem["ada0_step" if k < DC - 1 else "scale0_sum"], 1)

            def modulate(c, n=1):
                both = lambda t: t.rearrange("p (h c) -> p h c", h=2)[:, :, c:c + n]
                dve.wait_ge(sem["mod0_cols"], c + n)
                tt(both(mod[:, 0:2 * DC]), both(mod_ps[:, 0:2 * DC]), both(col("ada_b", 0, 2 * DC)), ALU.add).then_inc(sem["mod0_done"], 1)
                dve.wait_ge(sem["mod0_done"], max(1, c - 2))
                stt(gain[:, 0, c:c + n], mod[:, DC + c:DC + c + n], 1.0, col("pre_mix_g", c, n), ALU.add, ALU.mult).then_inc(sem["gain_first"], 1)
                dve.wait_ge(sem["gain_first"], max(1, c - 2))

            def norm(c):
                if c >= 2:
                    dve.wait_ge(sem["made_lo"], c - 1)
                normalised(c, x[:, c, :], gain[:, 0, c:c + 1])

            def low(c):
                dve.wait_ge(sem["made_hi"], c + 1)
                stt(h_lo[:, c, :], t_n[c % 2][:, :], mod[:, c:c + 1], h_hi[:, c, :].bitcast(F32), ALU.add, ALU.subtract
                    ).then_inc(sem["made_lo"], 1)

            for c in range(1, 4):
                scale_sums(c)
            for c in range(1, DC):
                dve.wait_ge(sem["sq_done"], c + 1)
                if c > 1:
                    dve.wait_ge(sem["sum_done"], c)
                tt(sq_sum[:, :], sq[0][:, :] if c == 1 else sq_sum[:, :], sq[c % 2][:, :], ALU.add
                   ).then_inc(sem["sum_done"], 2 if c == 1 else 1)
            modulate(0, 4)
            split_lo(st["glu"], 0, 0)
            dve.wait_ge(sem["rs_done"], 1)
            norm(0)
            norm(1)
            low(0)
            norm(2)
            low(1)
            scale_sums(4)
            norm(3)
            low(2)
            scale_sums(5)
            low(3)
            modulate(4)
            norm(4)
            modulate(5)
            low(4)
            norm(5)
            split_lo(st["glu"], 1, 1)
            low(5)
            scale_sums(6)
            scale_sums(7)
            modulate(6)
            norm(6)
            low(6)
            modulate(7)
            norm(7)
            low(7)

            def glu(i, s, k, ahead):
                if k == 0:
                    split_lo(st["glu"], 2, 0)
                elif k > 1:
                    ahead()
                dve.wait_ge(sem["sig_done"], k + 1)
                arrived(st["glu"], k, 0)
                free(st["glu"], k, lambda: tt(u[:, k, PAD:PAD + S], glu_sig[s][:, :], bank[2 * s], ALU.mult))

            sums = [conv_tmp, conv3]

            def conv_start(pair):
                for a in range(2):
                    c = 2 * pair + a
                    if taps[0] > a:
                        dve.wait_ge(sem["tap"], taps[0] - 1 + a)
                    ts(sums[a][:, :], u[:, c, 0:S], col("conv_w", c * TAPS), col("conv_b", c), ALU.mult, ALU.add).then_inc(sem["tap"], 1)
                taps[0] += 2

            def conv_tap(pair, j, before, last=False):
                for a in range(2):
                    c = 2 * pair + a
                    dve.wait_ge(sem["tap"], before - 1 + a)
                    stt(u[:, c, PAD:PAD + S] if last else sums[a][:, :], u[:, c, bass.ds(j, S)], col("conv_w", c * TAPS + j),
                        sums[a][:, :], ALU.mult, ALU.add).then_inc(sem["tap"], 1)

            def conv_beside(first):
                def evac(i, s, k, ahead):
                    ahead()
                    step = first + k
                    if step == 0:
                        conv_start(0)
                    for j in range(1 + 6 * step, min(1 + 6 * step + 6, TAPS)):
                        conv_tap(0, j, taps[0], j == TAPS - 1)
                        taps[0] += 2
                return evac

            run(st["glu"], glu)
            dve.wait_ge(sem["pads"], 1)
            dve.wait_ge(sem["group_free"], st["qk"].g0)
            run(st["qk"], conv_beside(0))
            run(st["val"], conv_beside(4))

            def stage_qk(i, before, q, k):
                dve.wait_ge(sem["qk_hi"], 2 * before + 2 * i + 1)
                stt(stage_lo[:, 0, :], chunk(q, i), HD ** -0.5, stage_hi[:, 0, :].bitcast(F32), ALU.mult, ALU.subtract
                    ).then_inc(sem["qk_lo"], 1)
                dve.wait_ge(sem["qk_hi"], 2 * before + 2 * i + 2)
                less(stage_lo[:, 1, :], chunk(k, PAIRS + i), stage_hi[:, 1, :]).then_inc(sem["qk_lo"], 1)

            def stage_v(i, before, v):
                dve.wait_ge(sem["v_hi"], before + i + 1)
                less(pair_v(stage_lo[:, 2, :]), v[:, :, bass.ds(P * i, P)], pair_v(stage_hi[:, 2, :])).then_inc(sem["v_lo"], 1)

            def head(i, s, n, ahead):
                def some_taps(*rs):
                    for r in rs:
                        conv_tap(1, 4 * n + r, taps[0] + 8 * n + 2 * r)
                if s == 0:
                    stage_v(i, 0, v_rows)
                dve.wait_ge(sem["z_done"], n + 1)
                for a, b in HALVES:
                    ts(zbuf[:, a:b], z[:, a:b], 40.0, None, ALU.min).then_inc(sem["zm_done"], 1)
                some_taps(0)
                for j, (a, b) in enumerate(HALVES):
                    dve.wait_ge(sem["l_done"], 2 * n + j + 1)
                    tt(zbuf[:, a:b], z[:, a:b], zbuf[:, a:b], ALU.max).then_inc(sem["sp_done"], 1)
                for j, (a, b) in enumerate(HALVES):
                    dve.wait_ge(sem["sph_done"], 2 * n + j + 1)
                    less(t_lo[:, a:b], zbuf[:, a:b], t_hi[:, a:b]).then_inc(sem["spl_done"], 1)
                some_taps(1)
                if not ahead() and s:
                    stage_qk(i + 1, 0, qkT, qkT)
                for j, (a, b) in enumerate(HALVES):
                    dve.wait_ge(sem["ah_done"], 2 * n + j + 1)
                    less(t_lo[:, a:b], zbuf[:, a:b], t_hi[:, a:b]).then_inc(sem["al_done"], 1)
                some_taps(2, 3)

            stage_qk(0, 0, qkT, qkT)
            conv_start(1)
            run(st["gate"], head)
            for c in range(PAIRS):
                dve.wait_ge(sem["osp_hi"], c + 1)
                less(h_lo[:, 4 + c, :], qkT[:, c, :], h_hi[:, 4 + c, :]).then_inc(sem["osp_lo"], 1)

            def convolved(c):
                return u[:, c, PAD:PAD + S] if c < 2 else sums[c - 2][:, :]

            dve.wait_ge(sem["mean_done"], 1)
            for c in range(4):
                tt(convolved(c), convolved(c), mean[:, :], ALU.subtract).then_inc(sem["xc_done"], 1)

            def gate_att(i, s, k, ahead):
                if k < 3:
                    ahead()
                else:
                    dve.wait_ge(sem["xc_done"], 4)
                    dve.wait_ge(sem["rs_done"], 2)
                    made(MADE["conv"], 4, convolved, lambda c: col("conv_ln_g", c), h_hi, h_lo, silu=True)
                    ahead()
                dve.wait_ge(sem["gate_sig"], 1)
                arrived(st["att_out"], k, 0)
                tt(gates[:, DC + 2 * k, :], gates[:, DC + 2 * k, :], bank[2 * s], ALU.mult)
                arrived(st["att_out"], k, 1)
                free(st["att_out"], k, lambda: tt(gates[:, DC + 2 * k + 1, :], gates[:, DC + 2 * k + 1, :], bank[2 * s + 1], ALU.mult))

            run(st["att_out"], gate_att)
            dve.wait_ge(sem["mod_cols"], ADA_REST)
            tt(mod[:, 2 * DC:], mod_ps[:, 2 * DC:], col("ada_b", 2 * DC, 4 * DC), ALU.add).then_inc(sem["mod_done"], 1)
            dve.wait_ge(sem["mod_done"], 1)
            tt(gain[:, 1, :], mod[:, 2 * DC:3 * DC], col("post_mix_g", 0, DC), ALU.mult).then_inc(sem["gain_done"], 1)
            stt(gain[:, 2, :], mod[:, 4 * DC:5 * DC], 1.0, col("pre_ffn_g", 0, DC), ALU.add, ALU.mult).then_inc(sem["gain_done"], 1)
            tt(gain[:, 3, :], mod[:, 5 * DC:6 * DC], col("post_ffn_g", 0, DC), ALU.mult).then_inc(sem["gain_done"], 1)

            def merged(i, s, k, ahead):
                ahead()
                dve.wait_ge(sem["gate_sig"], 2)
                for t in range(2):
                    n = 2 * k + t
                    arrived(st["conv_out"], k, t)
                    gate = lambda: tt(gates[:, n, :], gates[:, n, :], bank[2 * s + t], ALU.mult)
                    if t == 0:
                        gate().then_inc(sem["merge_m"], 1)
                        dve.wait_ge(sem["merge_m"], k + 1)
                    else:
                        free(st["conv_out"], k, gate)
                        freed(st["conv_out"], k)
                    tt(gates[:, n, :], gates[:, n, :], gates[:, DC + n, :], ALU.add).then_inc(sem["mid_f"], 1)
                for t in range(2):
                    n = 2 * k + t
                    dve.wait_ge(sem["mid_hi_done"], n + 1)
                    less(mid_lo[:, n, :], gates[:, n, :], mid_hi[:, n, :]).then_inc(sem["mid_lo_done"], 1)

            def add_normed(first, g, low=None):
                for c in range(DC + 1):
                    if c < DC:
                        if c >= 2:
                            dve.wait_ge(sem["x_odd" if c % 2 else "x_even"], first // 2 + c // 2)
                        stt(t_n[c % 2][:, :], y[:, c, :], gain[:, g, c:c + 1], rs[:, :], ALU.mult, ALU.mult).then_inc(sem["upd_step"], 1)
                    if c % 2:
                        dve.wait_ge(sem["upd_step"], first + c)
                        tt(x[:, c - 1, :], x[:, c - 1, :], t_n[0][:, :], ALU.add).then_inc(sem["x_even"], 1)
                        if low and c > 1:
                            low(c - 3)
                            low(c - 2)
                dve.wait_ge(sem["x_even"], first // 2 + DC // 2)
                dve.wait_ge(sem["x_odd"], first // 2 + DC // 2)

            run(st["conv_out"], merged)
            run(st["mix_out"], lambda i, s, k, ahead: ahead())
            dve.wait_ge(sem["gain_done"], 3)
            dve.wait_ge(sem["rs_done"], 3)
            add_normed(0, 1)
            dve.wait_ge(sem["rs_done"], 4)
            made(MADE["pre_ffn"], DC, lambda c: x[:, c, :], lambda c: gain[:, 2, c:c + 1], h_hi, h_lo,
                 lambda c: mod[:, 3 * DC + c:3 * DC + c + 1])

            def mid_low(m, k, s):
                dve.wait_ge(sem["mid_hi_done"], m + 1)
                less(chunk(mid_lo, k), act_p[s][:, :], chunk(mid_hi, k)).then_inc(sem["mid_lo_done"], 1)

            def gated(stage, part):
                def evac(i, s, k, ahead):
                    ahead()
                    dve.wait_ge(sem["mid_silu"], PART_AT[part] + k + 1)
                    arrived(stage, k, 1)
                    free(stage, k, lambda: tt(act_p[s][:, :], act_a[s][:, :], bank[2 * s + 1], ALU.mult))
                    mid_low(DC + PART_AT[part] + k, k, s)
                return evac

            def add_to(dst, stage):
                def evac(i, s, k, ahead):
                    ahead()
                    arrived(stage, k, 0)
                    tt(dst[:, 2 * k, :], dst[:, 2 * k, :], bank[2 * s], ALU.add)
                    arrived(stage, k, 1)
                    free(stage, k, lambda: tt(dst[:, 2 * k + 1, :], dst[:, 2 * k + 1, :], bank[2 * s + 1], ALU.add))
                return evac

            for r in range(3):
                run(st[f"ffn_in{r}"], gated(st[f"ffn_in{r}"], r))
                run(st[f"ffn_out{r}"], add_to(y, st[f"ffn_out{r}"]) if r else (lambda i, s, k, ahead: ahead()))
            dve.wait_ge(sem["rs_done"], 5)
            def gained_low(c):
                dve.wait_ge(sem["made_hi"], MADE["attn2"] + c + 1)
                stt(h_lo[:, c, :], x[:, c, :], col("attn_norm_w_2", c), h_hi[:, c, :].bitcast(F32), ALU.mult, ALU.subtract
                    ).then_inc(sem["made_lo"], 1)

            add_normed(DC, 3, gained_low)
            for c in range(DC - 2, DC):
                gained_low(c)

            def rotary(i, s, k, ahead):
                ahead()
                if k == 0:
                    dve.wait_ge(sem["trig"], 4)
                    dve.wait_ge(sem["rs_done"], 6)
                    for table in (cos_ret, sin_ret):
                        tt(table[:, :], table[:, :], rs_attn[:, :], ALU.mult).then_inc(sem["rs_tables"], 1)
                    dve.wait_ge(sem["rs_tables"], 2)
                elif k == 1:
                    tt(pair_v(t_n[0][:, :]), pair_v(rs_attn[:, :]), ident[:, :].unsqueeze(1).to_broadcast([P, QB, P]), ALU.mult
                       ).then_inc(sem["rs_diag"], 1)
                for t in range(2):
                    n = 2 * k + t
                    if n >= 2:
                        dve.wait_ge(sem["rp_done"], n - 1)
                    dve.wait_ge(sem["sw_done"], n + 1)
                    turn = lambda: tt(rope_t[t][:, :], bank[2 * s + t], cos_ret[:, :], ALU.mult)
                    if t == 0:
                        turn().then_inc(sem["rope_m"], 1)
                    else:
                        free(st["ret_qk"], k, turn)
                    tt(swapped[t][:, :], swapped[t][:, :], sin_ret[:, :], ALU.mult).then_inc(sem["rope_s"], 1)
                    if t == 0:
                        dve.wait_ge(sem["rope_m"], k + 1)
                    else:
                        freed(st["ret_qk"], k)
                    dve.wait_ge(sem["rope_s"], n + 1)
                    tt(rqk[:, n, :], rope_t[t][:, :], swapped[t][:, :], ALU.add).then_inc(sem["rp_done"], 1)

            only_ahead = lambda i, s, k, ahead: ahead()
            run(st["ret_qk"], rotary)
            dve.wait_ge(sem["rs_diag"], 1)
            nc.vector.reduce_sum(rs_col, pair_v(t_n[0][:, :]), AX.X).then_inc(sem["rs_col"], 1)
            run(st["ret_val"], only_ahead)

            def key_rope():
                ps = bank[2 * 1 + 1]
                arrived(st["latent"], 1, 1)
                tt(rope_t[0][64:96, :], ps[64:96, :], cos_mla[64:96, :], ALU.mult).then_inc(sem["rope_m"], 1)
                free(st["latent"], 1, lambda: tt(rope_t[1][64:96, :], ps[96:128, :], sin_mla[96:128, :], ALU.mult))
                freed(st["latent"], 1)
                dve.wait_ge(sem["rope_m"], PAIRS + 1)
                tt(kpe[64:96, :], rope_t[0][64:96, :], rope_t[1][64:96, :], ALU.add).then_inc(sem["kpe_raw"], 1)
                dve.wait_ge(sem["kpe_raw"], 1)
                tt(kpe[64:96, :], kpe[64:96, :], rs_attn[64:96, :], ALU.mult).then_inc(sem["kpe_done"], 1)

            def beside(n):
                stage, k, t = st["latent" if n < 4 else "ret_gate"], n // 2 % 2, n % 2
                if n == 3:
                    return key_rope()
                arrived(stage, k, t)
                dst = lat[:, n, :] if n < 4 else rgate[:, n - 4, :]
                out_of = lambda: tt(dst, bank[n % 4], rs_attn[:, :], ALU.mult)
                if t:
                    free(stage, k, out_of)
                else:
                    out_of().then_inc(sem["lat_done" if n < 4 else "gate_raw"], 1)

            def ret_pair(i0):
                def evac(_, slot, k, ahead):
                    i = i0 + k
                    for s in range(2):
                        n = 2 * i + s
                        dve.wait_ge(sem["dec_done"], n + 1)
                        dve.wait_ge(sem["rz_done"], n + 1)
                        if n:
                            dve.wait_ge(sem["rp_lo"], n)
                        for kb in range(QB):
                            a, w = BLOCK_AT[kb], BLOCK_W[kb]
                            last = tt(rp[:, a:a + w], z[:, a:a + w], decay[n % 4][:, 0:w], ALU.mult)
                        last.then_inc(sem["rp_f"], 1)
                        if s == 0:
                            stage_v(i, PAIRS, rv_rows)
                        dve.wait_ge(sem["rp_hi"], n + 1)
                        less(t_lo[:, :], rp[:, :], t_hi[:, :]).then_inc(sem["rp_lo"], 1)
                        if s == 0:
                            ahead()
                        elif i < PAIRS - 1:
                            stage_qk(i + 1, PAIRS, rqk, rqk)
                        beside(n)
                return evac

            dve.wait_ge(sem["rp_done"], 2 * PAIRS)
            stage_qk(0, PAIRS, rqk, rqk)
            run(st["latent"], ret_pair(0))
            run(st["ret_gate"], ret_pair(2))
            dve.wait_ge(sem["rs_done"], 7)
            made(MADE["lat"], 1, lambda c: lat[:, 2, :], lambda c: col("mla_kv_norm_w_2"), lat_hi[:, 2:3], lat_lo[:, 2:3])
            dve.wait_ge(sem["rs_done"], 8)
            dve.wait_ge(sem["made_lo"], MADE["lat"] + 1)
            made(MADE["lat"] + 1, 2, lambda c: lat[:, c, :], lambda c: col("mla_q_norm_w_2", c), lat_hi, lat_lo)
            run(st["up_v"], only_ahead)
            dve.wait_ge(sem["ro_evac"], HEADS)

            def rotate(k):
                c, s = PAIRS - 1 - k, k % 2
                for t in range(2):
                    h = 2 * k + t
                    dve.wait_ge(sem["mq_done"], h + 1)
                    if h:
                        dve.wait_ge(sem["qrope_done"], h)
                    tt(rope_t[0][64:96, :], bank[2 * s + t][64:96, :], cos_mla[64:96, :], ALU.mult).then_inc(sem["rope_m"], 1)
                    turn = lambda: tt(rope_t[1][64:96, :], bank[2 * s + t][96:128, :], sin_mla[96:128, :], ALU.mult)
                    if t == 0:
                        turn().then_inc(sem["rope_s"], 1)
                        dve.wait_ge(sem["rope_s"], 2 * PAIRS + k + 1)
                    else:
                        free(st["up_q"], k, turn)
                        freed(st["up_q"], k)
                    dve.wait_ge(sem["rope_m"], 1 + PAIRS + h + 1)
                    tt(mq[64:96, 2 * c + t, :], rope_t[0][64:96, :], rope_t[1][64:96, :], ALU.add).then_inc(sem["qrope_done"], 1)

            def queries(i, s, k, ahead):
                m, c = MADE["gn"] + k, PAIRS - 1 - k
                dve.wait_ge(sem["gn_mean"], k + 1)
                tt(rqk[:, c, :], rqk[:, c, :], o_ps, ALU.subtract).then_inc(sem["gn_xc"], 1)
                ahead()
                if k:
                    rotate(k - 1)
                dve.wait_ge(sem["gn_xc"], k + 1)
                dve.wait_ge(sem["rs_done"], 8 + k + 1)
                normalised(m, rqk[:, c, :], col("ret_gn_w_2", c))
                dve.wait_ge(sem["tn_done"], normed(m))
                tt(h_f[m % 2][:, :], t_n[m % 2][:, :], rgate[:, c, :], ALU.mult).then_inc(sem["gn_y"], 1)
                dve.wait_ge(sem["made_hi"], m + 1)
                less(h_lo[:, c, :], h_f[m % 2][:, :], h_hi[:, c, :]).then_inc(sem["made_lo"], 1)
                if k == PAIRS - 1:
                    rotate(k)

            run(st["up_q"], queries)
            run(st["up_k"], only_ahead)
            dve.wait_ge(sem["qrope_done"], HEADS)
            def mla_qk(i, s):
                dve.wait_ge(sem["mqk_hi"], 4 * i + 2 * s + 1)
                less(m_lo[0:96, s, :], chunk(mq, 2 * i + s, slice(0, 96)), m_hi[0:96, s, :]).then_inc(sem["mqk_lo"], 1)
                dve.wait_ge(sem["mqk_hi"], 4 * i + 2 * s + 2)
                less(m_lo[0:HD, 2 + s, :], chunk(mk, 2 * i + s, slice(0, HD)), m_hi[0:HD, 2 + s, :]).then_inc(sem["mqk_lo"], 1)

            def mla_v(i):
                dve.wait_ge(sem["mv_hi"], i + 1)
                less(pair_v(m_lo[:, 4, :]), mv_rows[:, :, bass.ds(P * i, P)], pair_v(m_hi[:, 4, :])).then_inc(sem["mv_lo"], 1)

            def mla_max(i, s):
                n = 2 * i + s
                dve.wait_ge(sem["mz_done"], n + 1)
                for t in range(QB):
                    a, w = ROW_AT[t], ROW_W[t]
                    last = nc.vector.reduce_max(row_stat[:, s, t:t + 1], z2[s][:, a:a + w], AX.X)
                last.then_inc(sem["mx_done"], 1)
                dve.wait_ge(sem["mx_done"], n + 1)
                ts(row_stat[:, s, 4:8], row_stat[:, s, 0:4], -MLA_SCALE, None, ALU.mult).then_inc(sem["nmx_done"], 1)

            def mla_norm(i, s):
                n = 2 * i + s
                dve.wait_ge(sem["mp_done"], n + 1)
                nc.vector.reciprocal(row_stat[:, s, 12:16], row_stat[:, s, 8:12]).then_inc(sem["rcp_done"], 1)
                dve.wait_ge(sem["rcp_done"], n + 1)
                for t in range(QB):
                    a, w = ROW_AT[t], ROW_W[t]
                    last = ts(mp[s][:, a:a + w], mp[s][:, a:a + w], row_stat[:, s, 12 + t:13 + t], None, ALU.mult)
                last.then_inc(sem["pn_done"], 1)

            def mla_low(i, s):
                dve.wait_ge(sem["mth"], 2 * i + s + 1)
                less(mt_lo[s][:, :], z2[s][:, 0:ZW], r_hi[s][:, :]).then_inc(sem["mtl"], 1)

            def mla_period(i, first=False, final=False):
                mla_max(i, 0)
                if not first:
                    mla_low(i - 1, 1)
                mla_norm(i, 0)
                if not final:
                    mla_qk(i + 1, 0)
                mla_max(i, 1)
                mla_low(i, 0)
                mla_norm(i, 1)
                if not final:
                    mla_qk(i + 1, 1)
                mla_v(i)

            for s in range(2):
                dve.wait_ge(sem["kst_hi"], s + 1)
                less(m_lo[64:96, 2 + s, :], kpe[64:96, :], m_hi[64:96, 2 + s, :]).then_inc(sem["kst_lo"], 1)
                mla_qk(0, s)
            mla_period(0, first=True)
            with dve.Fori(1, PAIRS - 1) as i:
                mla_period(i)
            mla_period(PAIRS - 1, final=True)
            mla_low(PAIRS - 1, 1)
            for c in range(PAIRS):
                dve.wait_ge(sem["mos_hi"], c + 1)
                less(h_lo[:, 4 + c, :], mq[:, 2 * c, :], h_hi[:, 4 + c, :]).then_inc(sem["mos_lo"], 1)
            run(st["mix_out2"], add_to(x, st["mix_out2"]))
            freed(st["mix_out2"], 3)
            dve.wait_ge(sem["rs_done"], 13)
            made(MADE["ffn2"], DC, lambda c: x[:, c, :], lambda c: col("ffn_norm_w_2", c), h_hi, h_lo)

            def conv_gated(stage, part):
                def evac(i, s, k, ahead):
                    c0 = PART_AT[part] + k
                    ahead()
                    for t, buf in ((0, act_a[s]), (1, act_b[s])):
                        tap = lambda back: stt(buf[:, back:], bank[2 * s + t][:, 0:S - back],
                                               col("conv_w_2", ((2 - back) * 2 + t) * FC + c0), buf[:, back:], ALU.mult, ALU.add)
                        dve.wait_ge(sem["ident_done"], 2 * c0 + t + 1)
                        tap(1).then_inc(sem["conv2"], 1)
                        dve.wait_ge(sem["conv2"], 2 * c0 + t + 1)
                        if t == 0:
                            tap(2).then_inc(sem["silu_arg"], 1)
                        else:
                            free(stage, k, lambda: tap(2))
                    freed(stage, k)
                    dve.wait_ge(sem["mid_silu"], FC + c0 + 1)
                    tt(act_p[s][:, :], act_a[s][:, :], act_b[s][:, :], ALU.mult).then_inc(sem["mid_f"], 1)
                    mid_low(DC + FC + c0, k, s)
                return evac

            for r in range(3):
                run(st[f"up{r}"], conv_gated(st[f"up{r}"], r))
                run(st[f"down{r}"], add_to(x, st[f"down{r}"]))
            freed(st["down2"], 3)
            dve.wait_ge(sem["rs_done"], 14)
            for k in range(DC):
                stt(y[:, k, :], x[:, k, :], col("final_norm_w_2", k), rs[:, :], ALU.mult, ALU.mult).then_inc(sem["fin_done"], 1)

        @block.gpsimd
        def _(pool):
            tt, ts = nc.gpsimd.tensor_tensor, nc.gpsimd.tensor_scalar

            def sums(name, ahead=None):
                e, q0, n = NORMS[name]
                for q in range(q0, q0 + n):
                    if ahead:
                        ahead(q - q0)
                    pool.wait_ge(sem["sq_done"], q + 1)
                    if q == q0:
                        if e:
                            pool.wait_ge(sem["stat_done"], ADDED_NORMS.index(name))
                        last = nc.gpsimd.tensor_copy(sq_sum[:, :], sq[q % 2][:, :])
                    else:
                        pool.wait_ge(sem["sum_done"], q)
                        last = tt(sq_sum[:, :], sq_sum[:, :], sq[q % 2][:, :], ALU.add)
                    last.then_inc(sem["sum_done"], 1)

            def ada_tile(a, slot, half):
                r = ada_raw[slot]
                pool.wait_ge(ada_full[slot], 16 * (half + 1))
                tt(r[:, :, :], r[:, :, :], c_act[:, :].unsqueeze(2).to_broadcast([P, 8, P]), ALU.mult).then_inc(sem["ada_step"], 1)
                for k, n in enumerate((4, 2, 1)):
                    pool.wait_ge(sem["ada_step"], 3 * a + k + 1)
                    if n > 1:
                        tt(r[:, 0:n], r[:, 0:n], r[:, n:2 * n], ALU.add).then_inc(sem["ada_step"], 1)
                if positive(a - 1):
                    pool.wait_ge(sem["mod_cols"], a - 1)
                tt(ada_acc[slot][:, :], r[:, 0, :], r[:, 1, :], ALU.add).then_inc(sem["ada_sum"], 1)

            for a, c in enumerate(SHIFT_SUMS):
                r = ada_first[:, 2 * c]
                pool.wait_ge(sem["ada0_prod"], a + 1)
                for j, n in enumerate((4, 2, 1)):
                    if j:
                        pool.wait_ge(sem["ada0_tree"], 2 * a + j)
                    tt(r[:, 0:n], r[:, 0:n], r[:, n:2 * n], ALU.add).then_inc(sem["ada0_tree" if n > 1 else "shift0_sum"], 1)
            pool.wait_ge(sem["mod0_cols"], 4)
            ada_tile(0, 0, 0)
            ada_tile(1, 1, 0)
            with pool.Fori(1, ADA_REST // 2) as i:
                ada_tile(2 * i, 0, i)
                ada_tile(2 * i + 1, 1, i)
            for name in ["conv_ln", "post_mix"]:
                sums(name)

            def add_odd(first, c):
                pool.wait_ge(sem["upd_step"], first + c + 1)
                tt(x[:, c, :], x[:, c, :], t_n[1][:, :], ALU.add).then_inc(sem["x_odd"], 1)

            for c in range(1, DC, 2):
                add_odd(0, c)
            steps = [0]

            def step(ins):
                ins.then_inc(sem["ang_step"], 1)
                steps[0] += 1
                pool.wait_ge(sem["ang_step"], steps[0])

            pool.wait_ge(sem["in_pos"], 16)
            step(nc.gpsimd.tensor_copy(pos_f[:, :], pos_i[:, :]))
            for kind, sin_t, cos_t in (("ret", sin_ret, cos_ret), ("mla", sin_mla, cos_mla)):
                step(ts(angle[:, :], pos_f[:, :], scol("freq_" + kind), None, ALU.mult))
                step(ts(turns[:, :], angle[:, :], 1 / (2 * np.pi), MAGIC, ALU.mult, ALU.add))
                step(ts(turns[:, :], turns[:, :], MAGIC, None, ALU.subtract))
                for part in TWO_PI:
                    step(ts(sin_t[:, :], turns[:, :], part, None, ALU.mult))
                    step(tt(angle[:, :], angle[:, :], sin_t[:, :], ALU.subtract))
                step(ts(angle[:, :], angle[:, :], PI, -PI, ALU.min, ALU.max))
                ts(sin_t[:, :], angle[:, :], scol("sign_" + kind), None, ALU.mult).then_inc(sem["ang_arg"], 1)
                step(ts(turns[:, :], angle[:, :], 0.0, None, ALU.max))
                step(ts(angle[:, :], angle[:, :], 0.0, None, ALU.min))
                step(tt(turns[:, :], turns[:, :], angle[:, :], ALU.subtract))
                ts(cos_t[:, :], turns[:, :], -1.0, float(np.float32(np.pi / 2)), ALU.mult, ALU.add).then_inc(sem["ang_arg"], 1)

            sums("post_ffn")
            sums("attn2", lambda c: add_odd(DC, 1 if c == 0 else c + 2) if c == 0 or c % 2 and c < DC - 2 else None)
            for name in ["ffn2", "final"]:
                sums(name)


def packed(vectors):
    return np.ascontiguousarray(np.concatenate([v.reshape(-1, P).T for v in vectors], axis=1))


def shape_constants():
    p, f = np.arange(P)[:, None], np.arange(P)[None, :]
    mats = {"ident": p == f, "tri": -1.0 * (p >= f), "ones_neg": -np.ones((P, P)), "mask_kq": NEG * (p >= f),
            "mask_qk": NEG * (f > p), "ones": np.ones((P, P)), "block_mean": (p // HD == f // HD) / HD}
    j = np.arange(P)
    small = np.zeros((P, N_SMALL), np.float32)
    small[:, SMALL["eps"]] = EPS
    small[:, SMALL["freq_ret"]] = 10000.0 ** (-2.0 * (j % 32) / 64)
    small[:, SMALL["sign_ret"]] = np.where(j % 64 < 32, -1, 1)
    small[:, SMALL["freq_mla"]] = 10000.0 ** (-2.0 * (j % 16) / 32)
    small[:, SMALL["sign_mla"]] = np.where(j % 32 < 16, -1, 1)
    small[:, SMALL["log_gamma"]:SMALL["log_gamma"] + HEADS] = np.log1p(-2.0 ** (-5.0 - np.arange(HEADS)))
    lag = np.where(np.arange(S)[None, :] >= p, np.arange(S)[None, :] - p, 1e9)
    return np.stack([mats[n] for n in MATS], axis=1).astype(np.float32), small, lag.astype(np.float32)


def grouped(w, groups):
    rows, cols = w.shape
    return np.ascontiguousarray(w.reshape(rows // P, P, groups, 256).transpose(2, 1, 0, 3).reshape(groups, P, -1))


def stage_weights(a):
    def halves(w, width, first, n):
        return np.concatenate([w[:, half * width + P * c:half * width + P * c + P] for c in range(first, first + n) for half in range(2)], axis=1)

    w_in, w_in2 = a["w_in"][0], a["w_in_2"][0]
    w_uq = a["w_uq_2"][0].reshape(-1, HEADS, 96)
    w_ukv = a["w_ukv_2"][0].reshape(-1, HEADS, P)
    rope = w_in2[:, 2432:2464]
    out = {"glu": halves(w_in[:, 0:1024], 512, 0, 4), "qk": w_in[:, 1024:2048], "val": w_in[:, 2048:2560], "gate": w_in[:, 2560:],
           "att_out": a["w_att_out"][0], "conv_out": a["w_conv_out"][0], "mix_out": a["w_o"][0],
           "latent": np.concatenate([w_in2[:, 2048:2432], rope, rope, rope, rope[:, 16:], rope[:, :16]], axis=1),
           "ret_qk": w_in2[:, 0:1024], "ret_val": w_in2[:, 1024:1536], "ret_gate": w_in2[:, 1536:2048],
           "up_v": w_ukv[:, :, 64:].reshape(P, -1), "up_k": w_ukv[:, :, :64].reshape(P, -1),
           "up_q": np.concatenate([w_uq, w_uq[:, :, 80:96], w_uq[:, :, 64:80]], axis=2).reshape(256, PAIRS, -1)[:, ::-1].reshape(256, -1), "mix_out2": a["w_out_2"][0]}
    for r, n in enumerate(FFN_PARTS):
        rows = slice(PART_AT[r] * P, (PART_AT[r] + n) * P)
        out[f"ffn_in{r}"] = halves(a["w_ffn_in"][0], FF, PART_AT[r], n)
        out[f"ffn_out{r}"] = a["w_ffn_out"][0][rows]
        out[f"up{r}"] = halves(a["w_up_2"][0], FF, PART_AT[r], n)
        out[f"down{r}"] = a["w_down_2"][0][rows]
    return {name: grouped(out[name], groups) for name, groups, _ in STAGES}


def kernel(**inputs):
    import concourse.bacc as bacc
    from concourse.bass_utils import run_bass_kernel_spmd

    a = {name: np.asarray(v) for name, v in inputs.items()}
    mats, small, lag = shape_constants()
    zero_tap = np.zeros((1, 4 * P), np.float32)
    vectors = dict(a, conv_w=np.concatenate([zero_tap, a["conv_w"][0]]).reshape(TAPS, 4, P).transpose(1, 0, 2))
    arrays = {"x": np.ascontiguousarray(a["x"][0].T.reshape(DC, P, S).transpose(1, 0, 2)),
              "ada": np.ascontiguousarray(a["ada_w"][0].reshape(DC, P, 6 * DC, P).transpose(2, 1, 0, 3)),
              "vec": packed([vectors[name] for name, _ in VECTORS]), "small": small, "mats": mats, "lag": lag,
              "positions": a["positions_2"].astype(np.int32, copy=False)}
    for name, w in stage_weights(a).items():
        arrays["w_" + name] = w
    nc = bacc.Bacc("TRN2", target_bir_lowering=False, num_devices=1)
    dram = {name: nc.dram_tensor(name, v.shape, mybir.dt.from_np(v.dtype), kind="ExternalInput").ap() for name, v in arrays.items()}
    out = nc.dram_tensor("out", (P, DC, S), F32, kind="ExternalOutput").ap()
    build(nc, dram, out)
    r = run_bass_kernel_spmd(nc, [arrays], core_ids=[0])
    got = np.asarray(r.results[0]["out"])
    return np.ascontiguousarray(got.transpose(1, 0, 2).reshape(1, D, S).transpose(0, 2, 1))
```
